# Optimizing a Trainium2 kernel written in Bass

```python
import jax, jax.numpy as jnp
from jax import lax
import numpy as np
import math

D_MODEL = 1024
BATCH = 1
SEQ = 512
DEPTH = 1

GLA_HEADS = 4
GLA_DK = 128
GLA_DV = 256
GLA_KW = GLA_HEADS * GLA_DK
GLA_VW = GLA_HEADS * GLA_DV
GATE_RANK = 16
GATE_NORMALIZER = 16.0
GLA_CHUNK = 64
CONV_WIDTH = 1024
CONV_GROUPS = 8
CONV_K = 3
PLE_DIM = 256
EPS = 1e-6

SPLITS = [GLA_KW, GLA_KW, GLA_VW, GLA_VW, GATE_RANK,
          CONV_WIDTH, CONV_WIDTH, CONV_WIDTH, CONV_WIDTH,
          D_MODEL, D_MODEL]
IN_COLS = sum(SPLITS)


def rms_norm(x, g):
    xf = x.astype(jnp.float32)
    y = xf * lax.rsqrt(jnp.mean(xf * xf, axis=-1, keepdims=True) + EPS)
    return (y * g.astype(jnp.float32)).astype(x.dtype)

def gla_chunked(q, k, v, gk):
    bsz, s, h, dk = q.shape
    dv = v.shape[-1]
    n = s // GLA_CHUNK

    def to_chunks(t):
        return t.astype(jnp.float32).reshape(bsz, n, GLA_CHUNK, h, t.shape[-1]).transpose(1, 0, 3, 2, 4)

    q, k, v, gk = to_chunks(q) * (dk ** -0.5), to_chunks(k), to_chunks(v), to_chunks(gk)
    b = jnp.cumsum(gk, axis=3)
    b_last = b[:, :, :, -1:, :]
    q_in = q * jnp.exp(b)
    k_in = k * jnp.exp(-b)
    k_dec = k * jnp.exp(b_last - b)
    causal = jnp.tril(jnp.ones((GLA_CHUNK, GLA_CHUNK), dtype=bool))
    a = jnp.where(causal, jnp.einsum('nbhid,nbhjd->nbhij', q_in, k_in), 0.0)
    o_intra = jnp.einsum('nbhij,nbhjv->nbhiv', a, v)
    decay = jnp.exp(b_last[:, :, :, 0, :])

    def step(state, xs):
        q_n, k_n, v_n, d_n = xs
        o_n = jnp.einsum('bhcd,bhdv->bhcv', q_n, state)
        state = d_n[..., None] * state + jnp.einsum('bhcd,bhcv->bhdv', k_n, v_n)
        return state, o_n

    state0 = jnp.zeros((bsz, h, dk, dv), jnp.float32)
    _, o_inter = lax.scan(step, state0, (q_in, k_dec, v, decay))
    o = o_intra + o_inter
    return o.transpose(1, 0, 3, 2, 4).reshape(bsz, s, h, dv)

def causal_dwconv(u, w):
    s = u.shape[1]
    u_pad = jnp.pad(u, ((0, 0), (CONV_K - 1, 0), (0, 0)))
    y = w[0] * u_pad[:, 0:s, :]
    for j in range(1, CONV_K):
        y = y + w[j] * u_pad[:, j:j + s, :]
    return y

def first_inputs(seed: int = 0) -> dict:
    key = jax.random.key(seed)
    ks = jax.random.split(key, 20)
    nrm = lambda k, shape, scale: jax.random.normal(k, shape, jnp.float32) * scale
    gain = lambda k, shape: 1.0 + 0.05 * jax.random.normal(k, shape, jnp.float32)
    return {
        "x": nrm(ks[0], (BATCH, SEQ, D_MODEL), 1.0),
        "p": nrm(ks[1], (DEPTH, BATCH, SEQ, PLE_DIM), 1.0),
        "norm_mix_g": gain(ks[2], (DEPTH, D_MODEL)),
        "w_in": nrm(ks[3], (DEPTH, D_MODEL, IN_COLS), D_MODEL ** -0.5),
        "b_merge": nrm(ks[4], (DEPTH, 2 * D_MODEL), 0.02),
        "w_gk2": nrm(ks[5], (DEPTH, GATE_RANK, GLA_KW), GATE_RANK ** -0.5),
        "b_gk": nrm(ks[6], (DEPTH, GLA_KW), 0.02),
        "gla_norm_g": gain(ks[7], (DEPTH, GLA_DV)),
        "conv_w": nrm(ks[8], (DEPTH, CONV_K, CONV_WIDTH), CONV_K ** -0.5),
        "w_branch_a": nrm(ks[9], (DEPTH, GLA_VW, D_MODEL), GLA_VW ** -0.5),
        "w_branch_c": nrm(ks[10], (DEPTH, CONV_WIDTH, D_MODEL), CONV_WIDTH ** -0.5),
        "w_out": nrm(ks[11], (DEPTH, D_MODEL, D_MODEL), D_MODEL ** -0.5),
        "norm_ple_g": gain(ks[12], (DEPTH, D_MODEL)),
        "w_ple_gate": nrm(ks[13], (DEPTH, D_MODEL, D_MODEL), D_MODEL ** -0.5),
        "w_ple_proj": nrm(ks[14], (DEPTH, PLE_DIM, D_MODEL), PLE_DIM ** -0.5),
        "norm_final_g": gain(ks[15], (D_MODEL,)),
    }

def first_block(x, p, norm_mix_g, w_in, b_merge, w_gk2, b_gk, gla_norm_g, conv_w,
              w_branch_a, w_branch_c, w_out, norm_ple_g, w_ple_gate, w_ple_proj,
              norm_final_g):
    bsz, s, _ = x.shape
    idx = np.cumsum(SPLITS)[:-1].tolist()
    for i in range(DEPTH):
        h = rms_norm(x, norm_mix_g[i])
        proj = jnp.einsum('bsd,dc->bsc', h, w_in[i])
        (q, k, v, z_a, gk_low, cb, cc, xc, z_c, g_a, g_c) = jnp.split(proj, idx, axis=-1)

        gk = jax.nn.log_sigmoid((jnp.einsum('bsr,rk->bsk', gk_low, w_gk2[i]) + b_gk[i]).astype(jnp.float32)) / GATE_NORMALIZER
        o = gla_chunked(q.reshape(bsz, s, GLA_HEADS, GLA_DK),
                        k.reshape(bsz, s, GLA_HEADS, GLA_DK),
                        v.reshape(bsz, s, GLA_HEADS, GLA_DV),
                        gk.reshape(bsz, s, GLA_HEADS, GLA_DK))
        o = rms_norm(o, gla_norm_g[i]).reshape(bsz, s, GLA_VW).astype(x.dtype)
        y_a = jnp.einsum('bsv,vd->bsd', o * jax.nn.silu(z_a), w_branch_a[i])

        u = causal_dwconv(cc * xc, conv_w[i])
        y_c = jnp.einsum('bsc,cd->bsd', (cb * u) * jax.nn.silu(z_c), w_branch_c[i])

        b_ga, b_gc = b_merge[i][:D_MODEL], b_merge[i][D_MODEL:]
        merged = jax.nn.sigmoid(g_a + b_ga) * y_a + jax.nn.sigmoid(g_c + b_gc) * y_c
        x = x + jnp.einsum('bsd,de->bse', merged, w_out[i])

        ple_gate = jax.nn.sigmoid(jnp.einsum('bsd,de->bse', rms_norm(x, norm_ple_g[i]), w_ple_gate[i]))
        x = x + ple_gate * jnp.einsum('bsq,qd->bsd', p[i], w_ple_proj[i])
    return rms_norm(x, norm_final_g)


MLSTM_HEADS = 4
MLSTM_DH = 128
MLSTM_W = MLSTM_HEADS * MLSTM_DH
MLSTM_CHUNK = 128
CONV_W = 5
N_MGATES = 4 * MLSTM_HEADS

DIFF_HEADS = 4
DIFF_DH = 64
DIFF_DV = 2 * DIFF_DH
DIFF_QK_W = DIFF_HEADS * 2 * DIFF_DH
DIFF_W = DIFF_HEADS * DIFF_DV
Q_BLOCK = 128

OFF_MQ = 0
OFF_MK = OFF_MQ + MLSTM_W
OFF_MV = OFF_MK + MLSTM_W
OFF_MO = OFF_MV + MLSTM_W
OFF_MG = OFF_MO + MLSTM_W
OFF_DQ = OFF_MG + N_MGATES
OFF_DK = OFF_DQ + DIFF_QK_W
OFF_DV = OFF_DK + DIFF_QK_W
OFF_GATE = OFF_DV + DIFF_W
N_BRANCH = 2
IN_COLS_2 = OFF_GATE + N_BRANCH * D_MODEL

N_EXPERTS = 16
EC_CAPACITY = 2
D_FF_EXPERT = 2 * D_MODEL


def rms_norm_2(x, g):
    xf = x.astype(jnp.float32)
    xf = xf * lax.rsqrt(jnp.mean(xf * xf, axis=-1, keepdims=True) + EPS)
    return (xf * g.astype(jnp.float32)).astype(x.dtype)

def centred_dwconv(x, w, b):
    c = x.shape[-1]
    pad = CONV_W // 2
    y = lax.conv_general_dilated(x, w[:, None, :].astype(x.dtype), window_strides=(1,),
                                 padding=[(pad, pad)], dimension_numbers=('NWC', 'WIO', 'NWC'),
                                 feature_group_count=c)
    return y + b.astype(x.dtype)

def mlstm_chunkwise(q, k, v, i_pre, f_pre):
    B, H, S, dk = q.shape
    dv = v.shape[-1]
    L = MLSTM_CHUNK
    NC = S // L
    q = q.astype(jnp.float32).reshape(B, H, NC, L, dk)
    k = (k.astype(jnp.float32) * dk ** -0.5).reshape(B, H, NC, L, dk)
    v = v.astype(jnp.float32).reshape(B, H, NC, L, dv)
    log_f = jax.nn.log_sigmoid(f_pre).reshape(B, H, NC, L)
    log_i = i_pre.reshape(B, H, NC, L)
    b = jnp.cumsum(log_f, axis=-1)
    g = b[..., -1]
    a = g[..., None] - b + log_i
    a_max = a.max(-1)
    w = jnp.exp(a - a_max[..., None])
    C_loc = jnp.einsum('bhclv,bhclk->bhcvk', v * w[..., None], k)
    n_loc = jnp.einsum('bhcl,bhclk->bhck', w, k)

    def step(carry, inp):
        C, n, m = carry
        C_l, n_l, am, gc = inp
        m_new = jnp.maximum(gc + m, am)
        sp = jnp.exp(gc + m - m_new)
        sl = jnp.exp(am - m_new)
        C_new = sp[..., None, None] * C + sl[..., None, None] * C_l
        n_new = sp[..., None] * n + sl[..., None] * n_l
        return (C_new, n_new, m_new), (C, n, m)

    xs = (jnp.moveaxis(C_loc, 2, 0), jnp.moveaxis(n_loc, 2, 0),
          jnp.moveaxis(a_max, 2, 0), jnp.moveaxis(g, 2, 0))
    init = (jnp.zeros((B, H, dv, dk), jnp.float32), jnp.zeros((B, H, dk), jnp.float32),
            jnp.zeros((B, H), jnp.float32))
    _, (C_in, n_in, m_in) = lax.scan(step, init, xs)
    C_in = jnp.moveaxis(C_in, 0, 2)
    n_in = jnp.moveaxis(n_in, 0, 2)
    m_in = jnp.moveaxis(m_in, 0, 2)

    lower = jnp.tril(jnp.ones((L, L), dtype=bool))
    D = b[..., :, None] - b[..., None, :] + log_i[..., None, :]
    D = jnp.where(lower, D, -jnp.inf)
    inter = b + m_in[..., None]
    m_t = jnp.maximum(inter, D.max(-1))
    P = jnp.exp(D - m_t[..., None])
    W = jnp.einsum('bhctd,bhcsd->bhcts', q, k) * P
    s_in = jnp.exp(inter - m_t)
    num = (jnp.einsum('bhcts,bhcsv->bhctv', W, v)
           + s_in[..., None] * jnp.einsum('bhcvk,bhctk->bhctv', C_in, q))
    den = W.sum(-1) + s_in * jnp.einsum('bhck,bhctk->bhct', n_in, q)
    h = num / jnp.maximum(jnp.abs(den), jnp.exp(-m_t))[..., None]
    return h.reshape(B, H, S, dv)

def mlstm_branch(z, conv_w, conv_b, b_mgate, norm_g):
    B, S, _ = z.shape
    qk = jax.nn.silu(centred_dwconv(z[..., OFF_MQ:OFF_MV], conv_w, conv_b))
    to_heads = lambda t: t.reshape(B, S, MLSTM_HEADS, MLSTM_DH).transpose(0, 2, 1, 3)
    q = to_heads(qk[..., :MLSTM_W])
    k = to_heads(qk[..., MLSTM_W:])
    v = to_heads(z[..., OFF_MV:OFF_MO])
    o = z[..., OFF_MO:OFF_MG]
    gates = z[..., OFF_MG:OFF_MG + N_MGATES].astype(jnp.float32) + b_mgate.astype(jnp.float32)
    gates = gates.reshape(B, S, 2, 2, MLSTM_HEADS).transpose(2, 3, 0, 4, 1)
    h_fwd = mlstm_chunkwise(q, k, v, gates[0, 0], gates[0, 1])
    flip = lambda t: jnp.flip(t, axis=2)
    h_bwd = flip(mlstm_chunkwise(flip(q), flip(k), flip(v),
                                 jnp.flip(gates[1, 0], -1), jnp.flip(gates[1, 1], -1)))
    h = h_fwd + h_bwd
    mu = h.mean(-1, keepdims=True)
    var = jnp.mean((h - mu) ** 2, axis=-1, keepdims=True)
    h = ((h - mu) * lax.rsqrt(var + EPS)).transpose(0, 2, 1, 3).reshape(B, S, MLSTM_W)
    h = h * norm_g.astype(jnp.float32) * jax.nn.sigmoid(o.astype(jnp.float32))
    return h.astype(z.dtype)

def diff_attention_branch(z, lam, norm_g, lam_init):
    B, S, _ = z.shape
    H = DIFF_HEADS
    q = z[..., OFF_DQ:OFF_DK].reshape(B, S, H, 2, DIFF_DH).transpose(0, 2, 3, 1, 4)
    k = z[..., OFF_DK:OFF_DV].reshape(B, S, H, 2, DIFF_DH).transpose(0, 2, 3, 1, 4)
    v = z[..., OFF_DV:OFF_GATE].reshape(B, S, H, DIFF_DV).transpose(0, 2, 1, 3)
    lamf = lam.astype(jnp.float32)
    lam_full = (jnp.exp(jnp.sum(lamf[0] * lamf[1])) - jnp.exp(jnp.sum(lamf[2] * lamf[3]))
                + lam_init)
    slopes = jnp.exp2(-8.0 * jnp.arange(1, H + 1, dtype=jnp.float32) / H)
    scale = DIFF_DH ** -0.5
    NB = S // Q_BLOCK
    qb = q.reshape(B, H, 2, NB, Q_BLOCK, DIFF_DH).transpose(3, 0, 1, 2, 4, 5)
    pos = jnp.arange(S, dtype=jnp.int32)

    def block(args):
        q_blk, start = args
        s = jnp.einsum('bhiqd,bhikd->bhiqk', q_blk, k).astype(jnp.float32) * scale
        tq = start + jnp.arange(Q_BLOCK, dtype=jnp.int32)
        dist = jnp.abs(tq[:, None] - pos[None, :]).astype(jnp.float32)
        s = s - (slopes[:, None, None] * dist)[None, :, None]
        p = jax.nn.softmax(s, axis=-1)
        a = p[:, :, 0] - lam_full * p[:, :, 1]
        return jnp.einsum('bhqk,bhkv->bhqv', a.astype(v.dtype), v)

    starts = jnp.arange(NB, dtype=jnp.int32) * Q_BLOCK
    o = lax.map(block, (qb, starts))
    o = o.transpose(1, 2, 0, 3, 4).reshape(B, H, S, DIFF_DV).astype(jnp.float32)
    o = o * lax.rsqrt(jnp.mean(o * o, axis=-1, keepdims=True) + EPS)
    o = o * norm_g.astype(jnp.float32) * (1.0 - lam_init)
    return o.transpose(0, 2, 1, 3).reshape(B, S, DIFF_W).astype(z.dtype)

def expert_choice_ffn(h, w_router, w_gate, w_up, w_down):
    B, S, _ = h.shape
    cap = EC_CAPACITY * S // N_EXPERTS
    aff = jax.nn.softmax(jnp.einsum('bsd,de->bse', h, w_router).astype(jnp.float32), axis=-1)
    g, idx = lax.top_k(aff.transpose(0, 2, 1), cap)
    bidx = jnp.arange(B)[:, None, None]
    xe = h[bidx, idx]
    hid = (jax.nn.silu(jnp.einsum('becd,edf->becf', xe, w_gate))
           * jnp.einsum('becd,edf->becf', xe, w_up))
    ye = jnp.einsum('becf,efd->becd', hid, w_down) * g[..., None].astype(h.dtype)
    return jnp.zeros_like(h).at[bidx, idx].add(ye)

def second_inputs(seed: int = 0) -> dict:
    key = jax.random.key(seed)
    ks = jax.random.split(key, 20)
    nrm = lambda k, shape, s: jax.random.normal(k, shape, jnp.float32) * s
    i_bias = nrm(ks[3], (DEPTH, 2, MLSTM_HEADS), 0.1)
    f_bias = jnp.linspace(3.0, 6.0, MLSTM_HEADS, dtype=jnp.float32) + nrm(ks[4], (DEPTH, 2, MLSTM_HEADS), 0.1)
    b_mgate = jnp.stack([i_bias, f_bias], axis=2).reshape(DEPTH, N_MGATES)
    return {
        "x": nrm(ks[0], (BATCH, SEQ, D_MODEL), 1.0),
        "norm_mix_g": 1.0 + nrm(ks[1], (DEPTH, D_MODEL), 0.01),
        "w_in": nrm(ks[2], (DEPTH, D_MODEL, IN_COLS_2), D_MODEL ** -0.5),
        "b_mgate": b_mgate,
        "conv_w": nrm(ks[5], (DEPTH, CONV_W, 2 * MLSTM_W), CONV_W ** -0.5),
        "conv_b": nrm(ks[6], (DEPTH, 2 * MLSTM_W), 0.01),
        "mlstm_norm_g": 1.0 + nrm(ks[7], (DEPTH, MLSTM_W), 0.01),
        "diff_lam": nrm(ks[8], (DEPTH, 4, DIFF_DH), 0.1),
        "diff_norm_g": 1.0 + nrm(ks[9], (DEPTH, DIFF_DV), 0.01),
        "w_up_a": nrm(ks[10], (DEPTH, MLSTM_W, D_MODEL), MLSTM_W ** -0.5),
        "w_up_b": nrm(ks[11], (DEPTH, DIFF_W, D_MODEL), DIFF_W ** -0.5),
        "w_out": nrm(ks[12], (DEPTH, D_MODEL, D_MODEL), D_MODEL ** -0.5),
        "norm_ffn_g": 1.0 + nrm(ks[13], (DEPTH, D_MODEL), 0.01),
        "w_router": nrm(ks[14], (DEPTH, D_MODEL, N_EXPERTS), D_MODEL ** -0.5),
        "w_gate_e": nrm(ks[15], (DEPTH, N_EXPERTS, D_MODEL, D_FF_EXPERT), D_MODEL ** -0.5),
        "w_up_e": nrm(ks[16], (DEPTH, N_EXPERTS, D_MODEL, D_FF_EXPERT), D_MODEL ** -0.5),
        "w_down_e": nrm(ks[17], (DEPTH, N_EXPERTS, D_FF_EXPERT, D_MODEL), D_FF_EXPERT ** -0.5),
        "norm_f_g": 1.0 + nrm(ks[18], (D_MODEL,), 0.01),
    }

def second_block(x, norm_mix_g, w_in, b_mgate, conv_w, conv_b, mlstm_norm_g, diff_lam, diff_norm_g,
              w_up_a, w_up_b, w_out, norm_ffn_g, w_router, w_gate_e, w_up_e, w_down_e, norm_f_g):
    for l in range(DEPTH):
        lam_init = 0.8 - 0.6 * math.exp(-0.3 * l)
        h = rms_norm_2(x, norm_mix_g[l])
        z = jnp.einsum('bsd,dc->bsc', h, w_in[l])
        y_a = jnp.einsum('bsw,wd->bsd', mlstm_branch(z, conv_w[l], conv_b[l], b_mgate[l], mlstm_norm_g[l]), w_up_a[l])
        y_b = jnp.einsum('bsw,wd->bsd', diff_attention_branch(z, diff_lam[l], diff_norm_g[l], lam_init), w_up_b[l])
        g_a = jax.nn.sigmoid(z[..., OFF_GATE:OFF_GATE + D_MODEL])
        g_b = jax.nn.sigmoid(z[..., OFF_GATE + D_MODEL:])
        x = x + jnp.einsum('bsd,de->bse', g_a * y_a + g_b * y_b, w_out[l])
        h2 = rms_norm_2(x, norm_ffn_g[l])
        x = x + expert_choice_ffn(h2, w_router[l], w_gate_e[l], w_up_e[l], w_down_e[l])
    return rms_norm_2(x, norm_f_g)


def setup_inputs(seed=0):
    out = dict(first_inputs(seed))
    for name, value in second_inputs(seed + 1).items():
        if name != "x":
            out[name + "_2"] = value
    return out


def reference(
    x, p, norm_mix_g, w_in, b_merge, w_gk2, b_gk, gla_norm_g, conv_w, w_branch_a, w_branch_c,
    w_out, norm_ple_g, w_ple_gate, w_ple_proj, norm_final_g, norm_mix_g_2, w_in_2, b_mgate_2,
    conv_w_2, conv_b_2, mlstm_norm_g_2, diff_lam_2, diff_norm_g_2, w_up_a_2, w_up_b_2, w_out_2,
    norm_ffn_g_2, w_router_2, w_gate_e_2, w_up_e_2, w_down_e_2, norm_f_g_2,
):
    x = first_block(
        x, p, norm_mix_g, w_in, b_merge, w_gk2, b_gk, gla_norm_g, conv_w, w_branch_a,
        w_branch_c, w_out, norm_ple_g, w_ple_gate, w_ple_proj, norm_final_g,
    )
    return second_block(
        x, norm_mix_g_2, w_in_2, b_mgate_2, conv_w_2, conv_b_2, mlstm_norm_g_2, diff_lam_2,
        diff_norm_g_2, w_up_a_2, w_up_b_2, w_out_2, norm_ffn_g_2, w_router_2, w_gate_e_2,
        w_up_e_2, w_down_e_2, norm_f_g_2,
    )


_drawn_inputs = setup_inputs


def setup_inputs(seed=0):
    import zlib

    import numpy as np

    out = dict(_drawn_inputs(seed))
    spreads = {}
    factors = {'b_merge': 8.0,
     'b_gk': 8.0,
     'gla_norm_g': 2.814,
     'norm_ple_g': 4.002,
     'norm_mix_g_2': 4.399,
     'conv_b_2': 63.433,
     'mlstm_norm_g_2': 24.998,
     'diff_norm_g_2': 8.0,
     'norm_ffn_g_2': 5.709,
     'norm_f_g_2': 31.003}
    for name, (base, spread) in spreads.items():
        noise = np.random.default_rng([zlib.crc32(name.encode()), seed]).standard_normal(out[name].shape)
        drawn = base * np.exp(spread * noise) if base else spread * noise
        out[name] = __import__('jax').numpy.asarray(drawn.astype(out[name].dtype))
    for name, factor in factors.items():
        out[name] = (out[name] * factor).astype(out[name].dtype)
    return out
```

```python
import math
from contextlib import ExitStack

import concourse.bass as bass
from concourse import mybir

F32 = mybir.dt.float32
F32R = mybir.dt.float32r
I32 = mybir.dt.int32
ALU = mybir.AluOpType
ACT = mybir.ActivationFunctionType
AX = mybir.AxisListType.X

P = 128
S = 512
TT = S // P
D = 1024
KD = D // P
EPS = 1e-6
GH, GDK, GDV, GCH = 4, 128, 256, 64
RANK = 16
GATE_NORM = 16.0
PLE = 256
OFF_Q, OFF_K, OFF_V, OFF_ZA, OFF_GK = 0, 512, 1024, 2048, 3072
OFF_CB = OFF_GK + RANK
OFF_CC, OFF_XC, OFF_ZC, OFF_GA, OFF_GC = (OFF_CB + 1024 * n for n in range(1, 6))
MH, MD = 4, 128
OFF_MQ, OFF_MV, OFF_MO, OFF_MG = 0, 1024, 1536, 2048
OFF_DQ = OFF_MG + 4 * MH
OFF_DK, OFF_DV, OFF_G2 = OFF_DQ + 512, OFF_DQ + 1024, OFF_DQ + 1536
NH, DDH, DDV = 4, 64, 128
LAM_INIT = 0.8 - 0.6 * math.exp(-0.3 * 0)
NE, CAP, FF = 16, 64, 2048
BIG = 3.0e38
KB = 1024
RING = 12


class Steps:

    def __init__(self, sem, names):
        self.sem, self.names, self.next = sem, list(names), 0
        self.index = {n: k for k, n in enumerate(self.names)}
        assert len(self.index) == len(self.names)

    def done(self, instruction, name):
        want = self.names[self.next % len(self.names)]
        assert want == name, (name, want)
        self.next += 1
        instruction.then_inc(self.sem, 1)

    def wait(self, eng, name, i=0):
        eng.wait_ge(self.sem, i * len(self.names) + (self.index[name] + 1))


class Stage:

    def __init__(self, name, n, tiles, kind="T"):
        self.name, self.n, self.tiles, self.kind = name, n, tiles, kind
        self.use = self.before = None


def kernel_program(nc, x, p, norm_mix_g, w_in, b_merge, w_gk2, b_gk, gla_norm_g, conv_w, w_branch_a,
                   w_branch_c, w_out, norm_ple_g, w_ple_gate, w_ple_proj, norm_final_g, norm_mix_g_2,
                   w_in_2, b_mgate_2, conv_w_2, conv_b_2, mlstm_norm_g_2, diff_lam_2, diff_norm_g_2,
                   w_up_a_2, w_up_b_2, w_out_2, norm_ffn_g_2, w_router_2, w_gate_e_2, w_up_e_2,
                   w_down_e_2, norm_f_g_2, out):
    ctx = ExitStack()
    with ctx:
        base = (nc.sbuf_base + 31) // 32 * 32

        def at(name, shape, kb, dt=F32):
            n = 4
            for d in shape[1:]:
                n *= d
            assert base + kb * KB + n <= nc.sbuf_usable_end, (name, kb, n)
            return nc.alloc_sbuf_tensor_at(name, shape, dt, offset=base + int(kb * KB))

        def sem(name):
            return ctx.enter_context(nc.semaphore(name))

        raw = at("raw", [P, 4, KD, P], 0)
        w_hi = at("w_hi", [P, 4, KD, P], 16, F32R)
        w_lo = at("w_lo", [P, 4, KD, P], 32, F32R)
        xT = at("xT", [P, KD, S], 48)
        h_hi = at("h_hi", [P, KD, S], 64, F32R)
        h_lo = at("h_lo", [P, KD, S], 80, F32R)
        oa_hi = at("oa_hi", [P, KD, S], 96, F32R)
        oa_lo = at("oa_lo", [P, KD, S], 112, F32R)
        yc_hi = at("yc_hi", [P, KD, S], 128, F32R)
        yc_lo = at("yc_lo", [P, KD, S], 144, F32R)
        m_hi = at("m_hi", [P, KD, S], 160, F32R)
        m_lo = at("m_lo", [P, KD, S], 176, F32R)
        sq = at("sq", [P, KD, S], 96)
        x_tok = at("x_tok", [P, TT, D], 160)
        za = at("za", [P, KD, S], 112)
        v_tok = at("v_tok", [P, TT, GH * GDV], 128)
        kdT = at("kdT", [P, GH, S], 144)
        kd_tok = at("kd_tok", [P, TT, GH * GDK], 152)
        qT = at("qT", [P, GH, S], 160)
        kT = at("kT", [P, GH, S], 168)
        bT = at("bT", [P, GH, S], 176)
        ex = at("ex", [P, GH, S], 184)
        state = at("state", [P, GH, GDV], 176)
        scoresT = at("scoresT", [P, GH, P], 180)
        gla_mask = at("gla_mask", [P, GH, P], 182, I32)
        o_norm = at("o_norm", [P, GH * GDV], 184)
        maskf = at("maskf", [P, GH, P], 188)
        p_tok = at("p_tok", [P, TT, PLE], 112)
        pT_hi = at("pT_hi", [P, 2, S], 128, F32R)
        pT_lo = at("pT_lo", [P, 2, S], 132, F32R)
        hm_hi = at("hm_hi", [P, MH, S], 96, F32R)
        hm_lo = at("hm_lo", [P, MH, S], 104, F32R)
        hd_hi = at("hd_hi", [P, NH, S], 112, F32R)
        hd_lo = at("hd_lo", [P, NH, S], 120, F32R)
        mqkT = at("mqkT", [P, 2 * MH, S], 128)
        moT = at("moT", [P, MH, S], 144)
        dqT = at("dqT", [P, NH, S], 152)
        dkT = at("dkT", [P, NH, S], 160)
        d_tok = at("d_tok", [P, TT, NH * DDV], 168)
        m_tok = at("m_tok", [P, TT, MH, MD + 1], 176)
        gates = at("gates", [P, S], 184.25)
        rows = at("rows", [64, 4, S], 112)
        rowb = at("rowb", [64, S], 120)
        rowm = at("rowm", [64, S], 122)
        rowt = at("rowt", [64, S], 124)
        rowf = at("rowf", [64, S], 126)
        rstm = at("rstm", [64, S], 186.25)
        negm = at("negm", [64, S], 188.25)
        hsum = at("hsum", [P, MH, TT, MD], 0)
        ktok = at("ktok", [P, TT, MH * MD], 8)
        ni = at("ni", [P, TT, MD + 1], 16)
        nj = at("nj", [P, TT, MD + 1], 18.25)
        wv = at("wv", [P, TT, MD + 1], 20.5)
        cst = at("cst", [P, TT, MD + 1], 22.75)
        arg = at("arg", [P, TT, P], 25)
        pt = at("pt", [P, TT, P], 27)
        wt = at("wt", [P, TT, P], 29)
        cols = at("cols", [P, TT, 4, 64], 31)
        selr = at("selr", [64, 8, P], 35)
        spb = at("spb", [P, 64, TT], 39)
        spd = at("spd", [64, 64, TT], 40)
        m01 = at("m01", [P, 2, P], 41)
        hn = at("hn", [P, TT, MD], 42)
        msm = at("msm", [P, 512], 44)
        alibi = at("alibi", [P, S + 3 * P], 0)
        alih = at("alih", [P, S + 3 * P], 3.5)
        es = at("es", [P, 2, S], 8)
        pr = at("pr", [P, S], 12)
        aa = at("aa", [P, S], 14)
        aaT = at("aaT", [P, TT, P], 16)
        od = at("od", [P, TT, DDV], 18)
        dsm = at("dsm", [P, 512], 20)
        lam_sb = at("lam_sb", [P, 4, DDH], 190.25)
        ring = at("ring", [P, RING, FF], 64)
        x2 = at("x2", [P, TT, D], 160)
        h2 = at("h2", [P, TT, D], 176)
        hid = at("hid", [P, 2, S], 0)
        hidT = at("hidT", [P, 2, 4, P], 4)
        sg = at("sg", [P, 2, S], 8)
        xe = at("xe", [P, KD, CAP], 12)
        pick = at("pick", [P, TT, CAP], 14)
        pickg = at("pickg", [P, TT, 2, CAP], 15)
        place = at("place", [P, S], 17)
        ye = at("ye", [P, S], 19)
        gbc = at("gbc", [P, D], 21)
        rw = at("rw", [P, KD, NE], 205.25)
        rwg = at("rwg", [P, KD, NE], 204.75)
        lg = at("lg", [P, TT, NE], 26)
        aff = at("aff", [P, TT, NE], 26.25)
        pos = at("pos", [P, TT, NE], 26.5)
        esm = at("esm", [P, 64], 26.75)
        aw = at("aw", [NE, S], 28)
        awm = at("awm", [NE, S], 30)
        awc = at("awc", [NE, S], 32)
        awo = at("awo", [NE, S], 34)
        iot = at("iot", [P, CAP], 36)
        ioti = at("ioti", [P, CAP], 36.5, I32)
        top8 = at("top8", [NE, 8], 37)
        fin = at("fin", [P, 2, D], 38)
        ident = at("ident", [P, P], 192)
        ones = at("ones", [P, P], 192.5)
        vec = at("vec", [P, 144], 193)
        eps = at("eps", [P, 1], 193.625)
        mgb = at("mgb", [P, 1], 193.75)
        sm = at("sm", [P, 64], 194)
        scr = [at(f"scr{n}", [P, S + 4], 194.5 + 2.03125 * n) for n in range(5)]

        mgw = at("mgw", [P, KD, P], 116)
        gk_sb = at("gk_sb", [RANK, S], 204.75)
        wgk = at("wgk", [RANK, GH * GDK], 152)
        vrow = at("vrow", [P, 2, P], 156)
        reset = at("reset", [P, S], 158)
        ps = ctx.enter_context(nc.psum_tensor("ps", [P, 8, S], F32))

        groups = [
            [("mix", norm_mix_g[0], 8), ("merge", b_merge[0], 16), ("bgk", b_gk[0], 4),
             ("gla", gla_norm_g[0], 2), ("conv", conv_w[0].rearrange("j c -> (j c)"), 24),
             ("ple", norm_ple_g[0], 8), ("final", norm_final_g, 8)],
            [("mix2", norm_mix_g_2[0], 8), ("conv2", conv_w_2[0].rearrange("j c -> (j c)"), 40),
             ("cb2", conv_b_2[0], 8), ("mnorm", mlstm_norm_g_2[0], 4),
             ("dnorm", diff_norm_g_2[0], 1), ("ffn", norm_ffn_g_2[0], 8)]]
        col, nrow, vec_loads = {}, [0, 0], []
        for g, members in enumerate(groups):
            for name, src, n in members:
                col[name] = 72 * g + nrow[g]
                vec_loads.append((g, nrow[g], n, src.rearrange("(r c) -> r c", c=P)))
                nrow[g] += n
        assert max(nrow) <= 72

        def vcol(name, k=0):
            return vec[:, col[name] + k:col[name] + k + 1]

        def columns(w, off, n=1024):
            return w[0][:, off:off + n].rearrange("(k p) (i c) -> p k i c", p=P, c=P)

        def tile(w, off, stride, j, n=1024):
            v = columns(w, off, n)
            return lambda i: (KD, v[:, :, i * stride + j, :])

        def short(w, k0, nk):
            v = w[0].rearrange("(k p) (i c) -> p k i c", p=P, c=P)
            return lambda i: (nk, v[:, k0:k0 + nk, i, :])

        w_gk_cols = w_in[0][:, OFF_GK:OFF_GK + RANK].rearrange("(k p) c -> p k c", p=P)
        proj_v = w_ple_proj[0].rearrange("(k p) (i c) -> p k i c", p=P, c=P)
        stages = [
            Stage("q", 1, [tile(w_in, OFF_Q, 4, j, 512) for j in range(4)]),
            Stage("k", 1, [tile(w_in, OFF_K, 4, j, 512) for j in range(4)]),
            Stage("gk", 1, [lambda i: (KD, w_gk_cols)]),
            Stage("v", 2, [tile(w_in, OFF_V, 4, j) for j in range(4)], "tok"),
            Stage("za", 2, [tile(w_in, OFF_ZA, 4, j) for j in range(4)]),
            Stage("conv", 8, [tile(w_in, o, 1, 0) for o in (OFF_XC, OFF_CC, OFF_CB, OFF_ZC)]),
            Stage("merge", 8, [tile(w_in, OFF_GA, 1, 0), tile(w_in, OFF_GC, 1, 0),
                               tile(w_branch_a, 0, 1, 0), tile(w_branch_c, 0, 1, 0)]),
            Stage("out", 2, [tile(w_out, 0, 4, j) for j in range(4)]),
            Stage("ple", 4, [tile(w_ple_gate, 0, 2, 0), lambda i: (2, proj_v[:, :, 2 * i, :]),
                             tile(w_ple_gate, 0, 2, 1), lambda i: (2, proj_v[:, :, 2 * i + 1, :])]),
            Stage("mqk", 2, [tile(w_in_2, OFF_MQ, 4, j) for j in range(4)]),
            Stage("mv", 1, [tile(w_in_2, OFF_MV, 4, j, 512) for j in range(4)], "tok"),
            Stage("mo", 1, [tile(w_in_2, OFF_MO, 4, j, 512) for j in range(4)]),
            Stage("mg", 1, [None]),
            Stage("dq", 1, [tile(w_in_2, OFF_DQ, 4, j, 512) for j in range(4)]),
            Stage("dk", 1, [tile(w_in_2, OFF_DK, 4, j, 512) for j in range(4)]),
            Stage("dv", 1, [tile(w_in_2, OFF_DV, 4, j, 512) for j in range(4)], "tok"),
            Stage("merge2", 8, [tile(w_in_2, OFF_G2, 1, 0), tile(w_in_2, OFF_G2 + D, 1, 0),
                                short(w_up_a_2, 0, 4), short(w_up_b_2, 0, 4)]),
            Stage("out2", 2, [tile(w_out_2, 0, 4, j) for j in range(4)]),
        ]
        uses = [0] * 4
        loads = [0] * 4
        for n, st in enumerate(stages):
            st.use, st.load = list(uses), list(loads)
            st.before = stages[n - 1] if n else None
            st.after = stages[n + 1] if n + 1 < len(stages) else None
            for j, src in enumerate(st.tiles):
                uses[j] += st.n
                loads[j] += st.n if src else 0
        by = {st.name: st for st in stages}
        HELD = ("merge2",)

        s_raw = [sem(f"raw_in{j}") for j in range(4)]
        s_hi = [sem(f"hi_split{j}") for j in range(4)]
        s_lo = [sem(f"lo_split{j}") for j in range(4)]
        s_mm = [sem(f"bank_done{j}") for j in range(4)]
        s_ev = [sem(f"bank_read{j}") for j in range(4)]
        s_small = sem("vectors_in")
        s_x = sem("x_in")
        s_p = sem("p_in")
        s_mg = sem("mg_in")
        s_gw = sem("gate_rank_in")
        s_out = sem("stored")

        def width(st):
            return RANK if st.name == "gk" else P

        def span(st, j, i):
            return KD if st.tiles[j] is None else st.tiles[j](0)[0]

        set_pool = Steps(sem("constants"), ["ident0", "ident", "ones", "mgb0", "vrow0", "reset1", "reset"])
        set_pe = Steps(sem("setup_pe"), ["vec0", "vec1"] + [f"x{k}" for k in range(KD)])
        set_dve = Steps(sem("setup_dve"), ["eps", "vec0", "vec1"] + [f"x{k}" for k in range(1, KD, 2)])
        set_act = Steps(sem("setup_act"), [f"x{k}" for k in range(0, KD, 2)])
        norms = ["mix", "ple", "final", "mix2"]
        n_act = {n: Steps(sem(f"norm_act_{n}"), [f"sq{k}" for k in range(KD)] + ["root"]
                          + ([f"hi{k}" for k in range(KD)] if n != "final" else [])) for n in norms}
        n_pe = {n: Steps(sem(f"norm_pe_{n}"), ["sum"]) for n in norms}
        n_dve = {n: Steps(sem(f"norm_dve_{n}"), ["rstd"] + [f"h{k}" for k in range(KD)]
                          + ([f"lo{k}" for k in range(KD)] if n != "final" else [])) for n in norms}
        for n in norms:
            if n != "final":
                order = ["rstd", "h0"]
                for k in range(KD):
                    order += ([f"h{k + 1}"] if k + 1 < KD else []) + [f"lo{k}"]
                n_dve[n] = Steps(n_dve[n].sem, order)
        gp_pe = Steps(sem("gate_pe"), [f"gk{h}" for h in range(GH)] + [f"kd{t}" for t in range(TT)])
        gp_act = Steps(sem("gate_act"), [f"abs{h}" for h in range(GH)] + [f"e{h}" for h in range(GH)] + [f"ln{h}" for h in range(GH)]
                       + ["eb", "ekd", "enb", "kd0", "kd1", "kd2", "kd3"])
        gp_dve = Steps(sem("gate_dve"), [f"min{h}" for h in range(GH)]
                       + [f"{a}{h}" for h in range(GH) for a in ("sum", "scan")]
                       + ["argkd", "kd", "qin", "decay", "kin", "zero", "zero2", "mask"])
        gp_pool = Steps(sem("gate_pool"), ["m0", "m1", "m2", "m3"])
        g_pe = Steps(sem("gla_pe"), ["a", "kvA0", "kvB0", "kvA1", "kvB1", "oT"])
        g_dve = Steps(sem("gla_dve"), ["at", "st00", "st01", "st02", "st03", "st10", "st11", "st12",
                                       "st13", "rstd", "t0", "t1", "lo0", "lo1"])
        g_act = Steps(sem("gla_act"), ["ss0", "ss1", "ss2", "ss3", "root", "on0", "on1", "on2", "on3",
                                       "hi0", "hi1"])
        cv_dve = Steps(sem("conv_dve"), ["c0", "c1", "c2", "y", "lo"])
        cv_act = Steps(sem("conv_act"), ["hi"])
        cv_pad = Steps(sem("conv_pad"), ["pad"])
        mg_dve = {1: Steps(sem("merge_dve"), ["m", "lo"]), 2: Steps(sem("merge2_dve"), ["m", "lo"])}
        mg_act = {1: Steps(sem("merge_act"), ["hi"]), 2: Steps(sem("merge2_act"), ["hi"])}
        out_dve = {1: Steps(sem("out_dve"), [f"x{j}" for j in range(4)]),
                   2: Steps(sem("out2_dve"), [f"x{j}" for j in range(4)])}
        p_pe = Steps(sem("p_pe"), ["p0", "p1"])
        p_act = Steps(sem("p_act"), ["hi0", "hi1"])
        p_dve = Steps(sem("p_dve"), ["lo0", "lo1"])
        pl_dve = Steps(sem("ple_dve"), ["xa", "xb"])
        mq_dve = Steps(sem("mqk_dve"), [f"c{n}" for n in range(5)])
        mq_act = Steps(sem("mqk_act"), ["silu"])
        mq_pad = Steps(sem("mqk_pad"), ["pad", "ones", "col"])
        mgz = Steps(sem("mg_zero"), ["w"])

        r_pool = Steps(sem("rows_pool"), ["r1", "r2", "r3", "n1", "n2", "n3", "m0", "mf", "mb"])
        r_dve = Steps(sem("rows_dve"), ["f", "lf", "bf", "bb", "c", "mf", "mb", "g0", "g1", "l0", "l1", "am",
                                        "mo0", "mo1", "mi", "mi0", "mi1", "s0", "s1", "gm", "mt", "a1", "a2",
                                        "a3", "nm", "sel0", "sel1", "spd"])
        r_act = Steps(sem("rows_act"), ["abs", "exp", "ln", "sp", "e1", "e2", "e3", "cols0", "cols1", "spb"])
        r_pe = Steps(sem("rows_pe"), ["cols", "spb"])
        kt_pe = Steps(sem("keys_pe"), [f"kt{c}" for c in range(TT)])
        kt_act = Steps(sem("keys_act"), ["scaled"] + [f"kt{c}" for c in range(TT)])
        WAYS = [(h, d) for h in range(MH) for d in range(2)]
        l_pe = Steps(sem("mlstm_pe"), [f"{a}{n}" for n in range(2 * MH) for a in
                                       (("kq",) if n % 2 == 0 else ()) + ("nm", "kv", "intra", "inter")])
        l_act = Steps(sem("mlstm_act"), [f"{a}{n}" for n in range(2 * MH) for a in ("pt", "ni")])
        l_dve = Steps(sem("mlstm_dve"), [f"{a}{n}" for n in range(2 * MH) for a in
                                         ("wv", "arg", "msk", "z", "cs0_", "cs1_", "cs2_", "w", "tmp", "num", "ab",
                                          "den", "rd", "h") + (("hs",) + tuple(f"bn{c}_" for c in range(TT)) if n % 2 else ())]
                      + [f"ag{n}" for n in range(MH * TT)] + ["rstd"])
        f_act = Steps(sem("mlstm_out_act"), ["root"] + [f"hi{h}" for h in range(MH)])
        f_pe = Steps(sem("mlstm_out_pe"), [f"t{h}" for h in range(MH)])
        f_dve = Steps(sem("mlstm_out_dve"), [f"{a}{h}" for h in range(MH) for a in
                                             ("n0_", "n1_", "n2_", "n3_", "t", "lo")])
        DW = [(h, q) for h in range(NH) for q in range(TT)]
        d_pool = Steps(sem("alibi_pool"), ["iota"])
        d_pe = Steps(sem("diff_pe"), ["s0"] + [f"{a}" for n in range(len(DW)) for a in
                                      (f"t{n}", f"s{n + 1}", f"o{n}", f"oT{n}")
                                      if not (a[0] == "s" and n + 1 == len(DW)) and not (a[:2] == "oT" and n % TT < TT - 1)])
        d_act = Steps(sem("diff_act"), ["lam0", "lam1"] + [f"{a}{n}" for n in range(len(DW)) for a in
                                        (("al",) if n % TT == 0 else ()) + ("e0_", "e1_", "t")
                                        + (("q0_", "q1_", "q2_", "q3_", "root", "o0_", "o1_", "o2_", "o3_", "hi")
                                           if n % TT == TT - 1 else ())])
        d_dve = Steps(sem("diff_dve"), ["abs", "lam0", "lam1", "lam2", "lam3", "gain"] + [f"{a}{n}" for n in range(len(DW)) for a in
                                        ("m0_", "m1_", "neg", "rec", "rl", "p", "a")
                                        + (("rstd", "lo") if n % TT == TT - 1 else ())])
        s_lam = sem("lambda_in")
        s_rw = sem("router_in")
        s_g = sem("gain_in")
        t_pe = Steps(sem("route_pe"), [f"x{t}" for t in range(TT)] + ["logits", "affT", "posT"])
        t_act = Steps(sem("route_act"), [f"x{t}" for t in range(TT)] + [f"ss{t}" for t in range(TT)] + ["root", "exp"])
        t_dve = Steps(sem("route_dve"), ["rwg"] + [f"x{t}" for t in range(TT)] + ["rstd"]
                      + [f"h{t}" for t in range(TT)]
                      + ["lg", "mx", "sub", "sum", "rec", "aff", "aw"]
                      + [f"{a}{n}" for n in range(CAP // 8) for a in ("top", "rep")]
                      + ["one", "mask", "scan", "sel", "pos"])
        t_pool = Steps(sem("route_pool"), ["iota"])
        s_ring = [sem(f"ring_in{s}") for s in range(RING)]
        s_free = [sem(f"ring_used{s}") for s in range(RING)]
        x_pe = Steps(sem("gather_pe"), ["gather"])
        x_act = Steps(sem("gather_act"), ["xe"])
        x_dve = Steps(sem("gather_dve"), ["pick"])
        e_pe = Steps(sem("expert_pe"), ["hT", "place", "o0", "o1", "o2", "o3"])
        e_act = Steps(sem("expert_act"), ["s0", "s1", "hT0", "ye", "place"])
        e_dve = Steps(sem("expert_dve"), ["pg0", "pg1", "hid0", "hid1", "hT1", "o0", "o1", "o2", "o3"])
        z_act = Steps(sem("final_act"), [f"ss{t}" for t in range(TT)] + ["root"])
        z_dve = Steps(sem("final_dve"), ["rstd"] + [f"y{t}" for t in range(TT)])
        s_store = [sem(f"stored{t}") for t in range(2)]

        def rings_rest(eng):
            eng.wait_ge(s_mm[3], by["dv"].use[3] + 1)

        def state_chunks(d):
            return list(range(TT)) if d == 0 else list(range(TT))[::-1]

        def mrow(h, d):
            return 32 * d + h

        def pairs(b):
            return ps[:, b:b + 2, 0:2 * (MD + 1)].rearrange("p b (c v) -> p b c v", v=MD + 1)

        def paired(t):
            return t[:, :, :].rearrange("p (b c) v -> p b c v", b=2)

        def over(ap, shape):
            return ap.to_broadcast(shape)

        gate_v = w_gate_e_2[0].rearrange("e (k p) f -> p e k f", p=P)
        up_v = w_up_e_2[0].rearrange("e (k p) f -> p e k f", p=P)
        down_v = w_down_e_2[0].rearrange("e (c j p) d -> p e c j d", p=P, j=2)
        PER = 24

        def used(eng, e, n):
            eng.wait_ge(s_free[n % RING], e * 2 + (n // RING + 1))



        def source(st, j, nk, w):
            return mgw[:, :, :] if st.tiles[j] is None else raw[:, j, 0:nk, 0:w]

        def free_slot(eng, st, j, i):
            if st.use[j] == 0 and isinstance(i, int) and i == 0:
                return
            eng.wait_ge(s_mm[j], st.use[j] + i)
            before = st if not (isinstance(i, int) and i == 0) else st.before
            if before.kind == "tok":
                last = before.use[3] + before.n if before is not st else st.use[3] + i
                eng.wait_ge(s_mm[3], last)

        def run_stage(eng, st, split, evac, look):
            def body(nxt, ni, i):
                for j in range(4):
                    if nxt is not None and j < len(nxt.tiles):
                        split(nxt, j, ni)
                    if j < len(st.tiles):
                        evac(st, j, i)
            if st.n > 2:
                with eng.Fori(0, st.n - 1) as i:
                    body(st, i + 1, i)
            else:
                for i in range(st.n - 1):
                    body(st, i + 1, i)
            body(st.after if look else None, 0, st.n - 1)

        def norm_input(eng, n, k):
            if n == "mix":
                (set_dve if k % 2 else set_act).wait(eng, f"x{k}")
            elif n == "ple":
                st = by["out"]
                eng.wait_ge(s_ev[k % 4], st.use[k % 4] + k // 4 + 1)
            elif n == "final":
                pl_dve.wait(eng, "xb" if k % 2 else "xa", k // 2)
            else:
                n_dve["final"].wait(eng, f"h{k}")

        def tiles4(ap):
            return ap[:, 0:S].rearrange("p (h t) -> p h t", t=P)

        def by_parity(t, r):
            return t[:, :, :].rearrange("p (h r) s -> p h r s", r=2)[:, :, r, :]

        def ds1(base, i):
            return bass.ds(i + base, 1)

        block = ctx.enter_context(nc.Block())

        @block.sync
        def _(sp):
            for t in range(TT):
                sp.dma_start(x_tok[:, t, :], x[0, t * P:(t + 1) * P, :]).then_inc(s_x, 16)

            def load(st, j, i, first=False):
                if st.tiles[j] is None:
                    return
                nk, src = st.tiles[j](i)
                dst = raw[:, j, 0:nk, 0:width(st)]
                if isinstance(i, int):
                    if st.use[j] + i:
                        sp.wait_ge(s_lo[j], st.use[j] + i)
                    sp.dma_start(dst, src).then_inc(s_raw[j], 16)
                else:
                    free = sp.lower_val(i + st.use[j])
                    sp.dma_start(dst, src).wait_op(s_lo[j], free, "sem-ge").then_inc(s_raw[j], 16)

            def load_stage(name):
                st = by[name]
                if st.n <= 2:
                    for i in range(st.n):
                        for j in range(len(st.tiles)):
                            load(st, j, i)
                else:
                    with sp.Fori(1, st.n + 1) as n:
                        for j in range(len(st.tiles)):
                            load(st, j, n - 1)

            for name in ("q", "k", "gk", "v", "za", "conv", "merge", "out"):
                load_stage(name)
            mg_dve[1].wait(sp, "lo", 7)
            sp.dma_start(p_tok[:, :, :], p[0, 0].rearrange("(t p) c -> p t c", p=P)).then_inc(s_p, 16)
            mgz.wait(sp, "w")
            for n, c in enumerate((0, 32, 64, 96)):
                src = OFF_MG + (0, 8, 4, 12)[n]
                sp.dma_start(mgw[:, :, c:c + 4],
                             w_in_2[0][:, src:src + 4].rearrange("(k p) c -> p k c", p=P)).then_inc(s_mg, 16)
            for name in ("ple", "mqk", "mv", "mo", "dq", "dk", "dv"):
                load_stage(name)
            s_mm_out = by["out"].use[3] + by["out"].n
            sp.wait_ge(s_mm[3], s_mm_out)
            sp.dma_start(lam_sb[:, :, :], diff_lam_2[0].rearrange("a c -> (a c)").partition_broadcast(P)).then_inc(s_lam, 16)
            sp.dma_start(rw[:, :, :], w_router_2[0].rearrange("(k p) e -> p k e", p=P)).then_inc(s_rw, 16)
            d_dve.wait(sp, "lo15")
            load_stage("merge2")
            load_stage("out2")
            mg_dve[2].wait(sp, "lo", 7)

            def load_expert(e, first=0, last=PER):
                for n in range(first, last):
                    s, use = n % RING, e * 2 + n // RING
                    src = gate_v[:, e, n, :] if n < 8 else up_v[:, e, n - 8, :] if n < 16 else down_v[:, e, n - 16, :, :]
                    dst = ring[:, s, :] if n < 16 else ring[:, s, :].rearrange("p (j d) -> p j d", j=2)
                    if isinstance(e, int):
                        if use:
                            sp.wait_ge(s_free[s], use)
                        sp.dma_start(dst, src).then_inc(s_ring[s], 16)
                    else:
                        turn = sp.lower_val(use)
                        sp.dma_start(dst, src).wait_op(s_free[s], turn, "sem-ge").then_inc(s_ring[s], 16)

            load_expert(0, last=RING)
            for b in range(4):
                sp.wait_ge(s_mm[b], by["out2"].use[b] + 2)
            sp.dma_start(gbc[:, :], norm_ffn_g_2[0].partition_broadcast(P)).then_inc(s_g, 16)
            load_expert(0, first=RING)
            with sp.Fori(1, NE) as e:
                load_expert(e)
            sp.dma_start(gbc[:, :], norm_f_g_2.partition_broadcast(P)).then_inc(s_g, 16)
            for t in range(TT):
                z_dve.wait(sp, f"y{t}")
                sp.dma_start(out[0, t * P:(t + 1) * P, :], fin[:, t % 2, :]).then_inc(s_store[t % 2], 16)
            for t in range(2):
                sp.wait_ge(s_store[t], 32)

        @block.gpsimd
        def _(pool):
            set_pool.done(pool.memset(ident[:, :], 0.0), "ident0")
            set_pool.wait(pool, "ident0")
            set_pool.done(pool.affine_select(out=ident[:, :], in_=ident[:, :], compare_op=ALU.not_equal,
                                             fill=1.0, base=0, pattern=[[-1, P]], channel_multiplier=1),
                          "ident")
            set_pool.done(pool.memset(ones[:, :], 1.0), "ones")
            set_pool.done(pool.memset(mgb[:, :], 0.0), "mgb0")
            set_pool.done(pool.memset(vrow[:, :, :], 0.0), "vrow0")
            set_pool.done(pool.memset(reset[:, :], 1.0), "reset1")
            set_pool.wait(pool, "reset1")
            set_pool.done(pool.memset(reset[:, 0:S:GCH], 0.0), "reset")
            gp_dve.wait(pool, "kin")
            gp_pool.done(pool.memset(maskf[:, :, :], 1.0), "m0")
            gp_pool.wait(pool, "m0")
            gp_pool.done(pool.affine_select(out=maskf[:, :, :], in_=maskf[:, :, :], compare_op=ALU.is_ge,
                                            fill=0.0, base=0, pattern=[[0, GH], [1, P]],
                                            channel_multiplier=-1), "m1")
            gp_pool.wait(pool, "m1")
            gp_pool.done(pool.memset(maskf[0:GCH, :, GCH:P], 0.0), "m2")
            mg_dve[1].wait(pool, "lo", 7)
            mgz.done(pool.memset(mgw[:, :, :], 0.0), "w")
            for b in range(4):
                pool.wait_ge(s_mm[b], by["out"].use[b] + 2)
            r_pool.done(pool.memset(rstm[:, :], 1.0), "r1")
            r_pool.wait(pool, "r1")
            r_pool.done(pool.memset(rstm[0:32, 0:S:P], 0.0), "r2")
            r_pool.wait(pool, "r2")
            r_pool.done(pool.memset(rstm[32:64, P - 1:S:P], 0.0), "r3")
            r_pool.wait(pool, "r3")
            r_pool.done(pool.memset(negm[:, :], 0.0), "n1")
            r_pool.wait(pool, "n1")
            r_pool.done(pool.memset(negm[0:32, 0:S:P], -BIG), "n2")
            r_pool.wait(pool, "n2")
            r_pool.done(pool.memset(negm[32:64, P - 1:S:P], -BIG), "n3")
            r_pool.wait(pool, "n3")
            rings_rest(pool)
            r_pool.done(pool.memset(m01[:, :, :], 0.0), "m0")
            r_pool.wait(pool, "m0")
            for d, name in ((0, "mf"), (1, "mb")):
                sign = 1 - 2 * d
                r_pool.done(pool.affine_select(out=m01[:, d, :], in_=m01[:, d, :], compare_op=ALU.is_ge, fill=-1e30,
                                               base=0, pattern=[[sign, P]], channel_multiplier=-sign), name)
                r_pool.wait(pool, name)
            f_dve.wait(pool, "lo3")
            d_pool.done(pool.iota(alibi[:, :], pattern=[[-1, S + 3 * P]], base=3 * P, channel_multiplier=1,
                                  allow_small_or_imprecise_dtypes=True), "iota")
            for b in range(4):
                pool.wait_ge(s_mm[b], by["out2"].use[b] + 2)
            t_pool.done(pool.iota(iot[:, :], pattern=[[1, CAP]], base=1, channel_multiplier=0,
                                  allow_small_or_imprecise_dtypes=True), "iota")

        @block.scalar
        def _(act):
            set_pool.wait(act, "vrow0")
            for g, r, n, src in vec_loads:
                act.dma_start(vrow[r:r + n, g, :], src).then_inc(s_small, 16)
            for n, r in enumerate((0, 32, 64, 96)):
                src = (0, 8, 4, 12)[n]
                act.dma_start(mgb[r:r + 4, :], b_mgate_2[0, src:src + 4].rearrange("(a b) -> a b", b=1))\
                   .then_inc(s_small, 16)
            act.dma_start(wgk[:, :], w_gk2[0]).then_inc(s_gw, 16)

            def split(st, j, i):
                nk, w = span(st, j, i), width(st)
                if st.tiles[j] is None:
                    act.wait_ge(s_mg, 64)
                else:
                    act.wait_ge(s_raw[j], (st.load[j] + i + 1) * 16)
                free_slot(act, st, j, i)
                act.activation(w_hi[:, j, 0:nk, 0:w], source(st, j, nk, w), ACT.Copy).then_inc(s_hi[j], 1)

            def setup():
                for k in range(0, KD, 2):
                    set_pe.wait(act, f"x{k}")
                    set_act.done(act.activation(xT[:, k, :], ps[:, k, :], ACT.Copy), f"x{k}")

            def norm(n):
                s = n_act[n]
                for k in range(KD):
                    norm_input(act, n, k)
                    s.done(act.activation(sq[:, k, :], xT[:, k, :], ACT.Square), f"sq{k}")
                n_pe[n].wait(act, "sum")
                if n == "mix":
                    set_dve.wait(act, "eps")
                s.done(act.activation(scr[0][:, 0:S], ps[:, 4, :], ACT.Sqrt, bias=eps[:, :], scale=1.0 / D), "root")
                if n != "final":
                    for k in range(KD):
                        n_dve[n].wait(act, f"h{k}")
                        s.done(act.activation(h_hi[:, k, :], scr[2 + k % 2][:, 0:S], ACT.Copy), f"hi{k}")

            def run(name, evac, look=True):
                run_stage(act, by[name], split, evac, look)

            def read(st, j, i, out, func, **kw):
                act.wait_ge(s_mm[j], st.use[j] + i + 1)
                act.activation(out, ps[:, j, :], func, **kw).then_inc(s_ev[j], 1)

            setup()
            for j in range(4):
                split(by["q"], j, 0)
            norm("mix")
            run("q", lambda st, j, i: read(st, j, i, qT[:, j, :], ACT.Copy, scale=GDK ** -0.5))
            run("k", lambda st, j, i: read(st, j, i, kT[:, j, :], ACT.Copy))

            def read_gk(st, j, i):
                act.wait_ge(s_mm[0], st.use[0] + 1)
                act.activation(gk_sb[:, :], ps[0:RANK, 0, :], ACT.Copy).then_inc(s_ev[0], 1)

            run("gk", read_gk)
            run("v", lambda st, j, i: read(st, j, i, v_tok[:, j, i * S:(i + 1) * S], ACT.Copy))
            run("za", lambda st, j, i: read(st, j, i, za[:, 4 * i + j, :], ACT.Silu))

            for h in range(GH):
                gp_pe.wait(act, f"gk{h}")
                gp_act.done(act.activation(ex[:, h, :], ps[:, 4 + h, :], ACT.Abs, bias=vcol("bgk", h)), f"abs{h}")
            for h in range(GH):
                gp_act.wait(act, f"abs{h}")
                gp_act.done(act.activation(ex[:, h, :], ex[:, h, :], ACT.Exp, scale=-1.0), f"e{h}")
            for h in range(GH):
                gp_act.wait(act, f"e{h}")
                gp_act.done(act.activation(ex[:, h, :], ex[:, h, :], ACT.Ln, bias=1.0), f"ln{h}")
            gp_dve.wait(act, "scan3")
            gp_act.done(act.activation(ex[:, :, :], bT[:, :, :], ACT.Exp, scale=1 / GATE_NORM), "eb")
            gp_dve.wait(act, "argkd")
            gp_act.done(act.activation(kdT[:, :, :], kdT[:, :, :], ACT.Exp, scale=1 / GATE_NORM), "ekd")
            gp_dve.wait(act, "decay")
            gp_act.done(act.activation(ex[:, :, :], bT[:, :, :], ACT.Exp, scale=-1 / GATE_NORM), "enb")
            for t in range(TT):
                gp_pe.wait(act, f"kd{t}")
                gp_act.done(act.activation(kd_tok[:, t, :], ps[:, 4 + t, :], ACT.Copy), f"kd{t}")
            for i in range(TT):
                g_pe.wait(act, "kvB1", i)
                for h in range(GH):
                    g_act.done(act.activation(scr[h // 2 * 3][:, h % 2 * GDV:(h % 2 + 1) * GDV], ps[:, 5 + h // 2, h % 2 * GDV:(h % 2 + 1) * GDV],
                                              ACT.Square, accum_out=sm[:, 32 + h:33 + h]), f"ss{h}")
                g_act.wait(act, "ss3", i)
                g_act.done(act.activation(sm[:, 36:40], sm[:, 32:36], ACT.Sqrt, bias=eps[:, :], scale=1 / GDV), "root")
                g_dve.wait(act, "rstd", i)
                for h in range(GH):
                    g_act.done(act.activation(o_norm[:, h * GDV:(h + 1) * GDV],
                                              ps[:, 5 + h // 2, h % 2 * GDV:(h % 2 + 1) * GDV],
                                              ACT.Copy, scale=sm[:, 40 + h:41 + h]), f"on{h}")
                for r in range(2):
                    g_dve.wait(act, f"t{r}", i)
                    g_act.done(act.activation(by_parity(oa_hi, r)[:, :, i * P:(i + 1) * P], tiles4(scr[1 + r]),
                                              ACT.Copy), f"hi{r}")

            def conv(st, j, i):
                if j == 0:
                    act.wait_ge(s_ev[1], st.use[1] + i)
                    read(st, 0, i, scr[0][:, 0:S], ACT.Copy)
                elif j == 3:
                    read(st, 3, i, scr[3][:, 0:S], ACT.Silu)
                    cv_dve.wait(act, "y", i)
                    cv_act.done(act.activation(yc_hi[:, i, :], scr[4][:, 0:S], ACT.Copy), "hi")

            run("conv", conv)

            def merge(which):
                hi = m_hi

                def evac(st, j, i):
                    if j < 2:
                        bias = {"bias": vec[:, ds1(col["merge"] + 8 * j, i)]} if which == 1 else {}
                        read(st, j, i, scr[j][:, 0:S], ACT.Sigmoid, **bias)
                    elif j == 3:
                        mg_dve[which].wait(act, "m", i)
                        mg_act[which].done(act.activation(hi[:, i, :], scr[3][:, 0:S], ACT.Copy), "hi")
                return evac

            run("merge", merge(1))
            run("out", lambda st, j, i: None)
            for k in range(2):
                p_pe.wait(act, f"p{k}")
                p_act.done(act.activation(pT_hi[:, k, :], ps[:, 5 + k, :], ACT.Copy), f"hi{k}")
            norm("ple")

            def ple(st, j, i):
                if j % 2 == 0:
                    act.wait_ge(s_ev[j + 1], st.use[j + 1] + i)
                    read(st, j, i, scr[j][:, 0:S], ACT.Sigmoid)

            run("ple", ple)
            norm("final")
            norm("mix2")

            def mqk(st, j, i):
                n = 4 * i + j
                if n:
                    mq_dve.wait(act, "c4", n - 1)
                read(st, j, i, scr[0][:, 2:S + 2], ACT.Copy)
                mq_dve.wait(act, "c4", n)
                mq_act.done(act.activation(mqkT[:, n, :], scr[1 + n % 2][:, 0:S], ACT.Silu, bias=vcol("cb2", n)), "silu")

            run("mqk", mqk)
            run("mv", lambda st, j, i: read(st, j, i, m_tok[:, j, :, 0:MD], ACT.Copy))
            run("mo", lambda st, j, i: read(st, j, i, moT[:, j, :], ACT.Sigmoid))
            run("mg", lambda st, j, i: read(st, j, i, gates[:, :], ACT.Identity, bias=mgb[:, :]))
            run("dq", lambda st, j, i: read(st, j, i, dqT[:, j, :], ACT.Copy))
            run("dk", lambda st, j, i: read(st, j, i, dkT[:, j, :], ACT.Copy))
            run("dv", lambda st, j, i: read(st, j, i, d_tok[:, j, :], ACT.Copy), look=False)
            r_dve.wait(act, "f")
            r_act.done(act.activation(rowt[:, :], rowf[:, :], ACT.Abs), "abs")
            r_act.wait(act, "abs")
            r_act.done(act.activation(rowt[:, :], rowt[:, :], ACT.Exp, scale=-1.0), "exp")
            r_act.wait(act, "exp")
            r_act.done(act.activation(rowt[:, :], rowt[:, :], ACT.Ln, bias=1.0), "ln")
            for n in range(4):
                mq_act.wait(act, "silu", 7)
            kt_act.done(act.activation(mqkT[:, MH:2 * MH, :], mqkT[:, MH:2 * MH, :], ACT.Copy, scale=MD ** -0.5), "scaled")
            r_dve.wait(act, "s1")
            r_act.done(act.activation(msm[0:64, 20:24], msm[0:64, 20:24], ACT.Exp), "sp")
            for n, scale in ((1, 1.0), (2, -1.0), (3, 1.0)):
                r_dve.wait(act, f"a{n}")
                r_act.done(act.activation(rows[:, n, :], rows[:, n, :], ACT.Exp, scale=scale), f"e{n}")
            for c in range(TT):
                kt_pe.wait(act, f"kt{c}")
                kt_act.done(act.activation(ktok[:, c, :], ps[:, c, :], ACT.Copy), f"kt{c}")
            r_pe.wait(act, "cols")
            for b in range(2):
                r_act.done(act.activation(cols[:, 2 * b:2 * b + 2, :, :], ps[:, 4 + b, :], ACT.Copy), f"cols{b}")
            r_pe.wait(act, "spb")
            r_act.done(act.activation(spb[:, :, :], ps[:, 6, 0:256], ACT.Copy), "spb")
            for n, (h, d) in enumerate(WAYS):
                l_dve.wait(act, f"msk{n}")
                l_act.done(act.activation(pt[:, :, :], arg[:, :, :], ACT.Exp), f"pt{n}")
                l_pe.wait(act, f"intra{n}")
                if n:
                    l_dve.wait(act, f"num{n - 1}")
                l_act.done(act.activation(paired(ni), pairs(6), ACT.Copy), f"ni{n}")
            l_dve.wait(act, "ag15")
            f_act.done(act.activation(msm[:, 240:256], msm[:, 200:232].rearrange("p (n a) -> p n a", a=2)[:, :, 1],
                                      ACT.Sqrt, bias=eps[:, :]), "root")
            for h in range(MH):
                f_dve.wait(act, f"t{h}")
                f_act.done(act.activation(hm_hi[:, h, :], scr[1 + h % 2][:, 0:S], ACT.Copy), f"hi{h}")

            d_dve.wait(act, "lam1")
            d_act.done(act.activation(dsm[:, 2:3], dsm[:, 0:1], ACT.Exp), "lam0")
            d_act.done(act.activation(dsm[:, 3:4], dsm[:, 1:2], ACT.Exp), "lam1")
            d_dve.wait(act, "abs")
            for n, (h, q) in enumerate(DW):
                if q == 0:
                    if n:
                        d_dve.wait(act, f"m1_{n - 1}")
                    d_act.done(act.activation(alih[:, :], alibi[:, :], ACT.Copy,
                                              scale=-(2.0 ** (-8 * (h + 1) / NH)) * DDH ** 0.5), f"al{n}")
                d_dve.wait(act, f"neg{n}")
                for i in range(2):
                    d_act.done(act.activation(es[:, i, :], es[:, i, :], ACT.Exp, bias=dsm[:, 12 + i:13 + i],
                                              accum_out=dsm[:, 14 + i:15 + i]), f"e{i}_{n}")
                d_pe.wait(act, f"t{n}")
                d_act.done(act.activation(aaT[:, :, :], ps[:, 4, :], ACT.Copy), f"t{n}")
                if q == TT - 1:
                    d_pe.wait(act, f"o{n}")
                    for c in range(TT):
                        d_act.done(act.activation(scr[0][:, c * P:(c + 1) * P], ps[:, 5 + h % 2, c * P:(c + 1) * P],
                                                  ACT.Square, accum_out=dsm[:, 20 + c:21 + c]), f"q{c}_{n}")
                    d_act.wait(act, f"q3_{n}")
                    d_act.done(act.activation(dsm[:, 24:28], dsm[:, 20:24], ACT.Sqrt, bias=eps[:, :], scale=1 / DDV), f"root{n}")
                    d_dve.wait(act, f"rstd{n}")
                    for c in range(TT):
                        d_act.done(act.activation(od[:, c, :], ps[:, 5 + h % 2, c * P:(c + 1) * P], ACT.Copy,
                                                  scale=dsm[:, 28 + c:29 + c]), f"o{c}_{n}")
                    d_pe.wait(act, f"oT{n}")
                    d_act.done(act.activation(hd_hi[:, h, :], ps[:, 7, :], ACT.Copy, scale=dsm[:, 8:9]), f"hi{n}")

            for j in range(4):
                split(by["merge2"], j, 0)
            run("merge2", merge(2))
            run("out2", lambda st, j, i: None)

            for t in range(TT):
                t_pe.wait(act, f"x{t}")
                t_act.done(act.activation(x2[:, t, 0:S], ps[:, 2 * t, :], ACT.Copy), f"x{t}")
            for t in range(TT):
                t_dve.wait(act, f"x{t}")
                t_act.wait(act, f"x{t}")
                t_act.done(act.activation(h2[:, t, :], x2[:, t, :], ACT.Square, accum_out=esm[:, t:t + 1]), f"ss{t}")
            t_act.wait(act, "ss3")
            t_act.done(act.activation(esm[:, 4:8], esm[:, 0:4], ACT.Sqrt, bias=eps[:, :], scale=1 / D), "root")
            t_dve.wait(act, "sub")
            t_act.done(act.activation(lg[:, :, :], lg[:, :, :], ACT.Exp), "exp")

            def gathered(e):
                x_pe.wait(act, "gather", e)
                x_act.done(act.activation(xe[:, :, :], ps[:, 7, :], ACT.Copy), "xe")

            def expert(e, more=True):
                used(act, e, 7)
                for q in range(2):
                    e_act.done(act.activation(sg[:, q, :], ps[:, q, :], ACT.Silu), f"s{q}")
                if more:
                    gathered(e + 1)
                e_pe.wait(act, "hT", e)
                e_act.done(act.activation(hidT[:, 0, :, :], ps[:, 5, :], ACT.Copy), "hT0")
                used(act, e, 23)
                e_act.done(act.activation(ye[:, :], ps[:, 4, :], ACT.Copy), "ye")
                e_pe.wait(act, "place", e)
                e_act.done(act.activation(place[:, :], ps[:, 7, :], ACT.Copy), "place")

            gathered(0)
            with act.Fori(0, NE - 1) as e:
                expert(e)
            expert(NE - 1, more=False)
            for t in range(TT):
                e_dve.wait(act, f"o{t}", NE - 1)
                z_act.done(act.activation(h2[:, t, :], x2[:, t, :], ACT.Square, accum_out=esm[:, 16 + t:17 + t]), f"ss{t}")
            z_act.wait(act, "ss3")
            z_act.done(act.activation(esm[:, 20:24], esm[:, 16:20], ACT.Sqrt, bias=eps[:, :], scale=1 / D), "root")

        @block.vector
        def _(dve):
            def split(st, j, i):
                nk, w = span(st, j, i), width(st)
                dve.wait_ge(s_hi[j], st.use[j] + i + 1)
                dve.tensor_tensor(w_lo[:, j, 0:nk, 0:w], source(st, j, nk, w),
                                  w_hi[:, j, 0:nk, 0:w].bitcast(F32), ALU.subtract).then_inc(s_lo[j], 1)

            def run(name, evac, look=True):
                run_stage(dve, by[name], split, evac, look)

            def norm(n):
                s = n_dve[n]
                n_act[n].wait(dve, "root")
                s.done(dve.reciprocal(scr[1][:, 0:S], scr[0][:, 0:S]), "rstd")
                s.wait(dve, "rstd")

                def part(k):
                    if n != "final" and k >= 2:
                        s.wait(dve, f"lo{k - 2}")
                    if n == "final":
                        s.done(dve.scalar_tensor_tensor(out=xT[:, k, :], in0=xT[:, k, :], scalar=vcol(n, k),
                                                        in1=scr[1][:, 0:S], op0=ALU.mult, op1=ALU.mult), f"h{k}")
                        return
                    s.done(dve.scalar_tensor_tensor(out=scr[2 + k % 2][:, 0:S], in0=xT[:, k, :], scalar=vcol(n, k),
                                                    in1=scr[1][:, 0:S], op0=ALU.mult, op1=ALU.mult), f"h{k}")

                def low(k):
                    n_act[n].wait(dve, f"hi{k}")
                    s.done(dve.tensor_tensor(h_lo[:, k, :], scr[2 + k % 2][:, 0:S], h_hi[:, k, :].bitcast(F32),
                                             ALU.subtract), f"lo{k}")

                part(0)
                for k in range(KD):
                    if k + 1 < KD:
                        part(k + 1)
                    if n != "final":
                        low(k)

            def nothing(st, j, i):
                return None

            set_dve.done(dve.memset(eps[:, :], EPS), "eps")
            set_pe.wait(dve, "vec0")
            set_dve.done(dve.tensor_copy(vec[:, 0:72], ps[:, 0, 0:72]), "vec0")
            set_pe.wait(dve, "vec1")
            set_dve.done(dve.tensor_copy(vec[:, 72:144], ps[:, 1, 0:72]), "vec1")
            for k in range(1, KD, 2):
                set_pe.wait(dve, f"x{k}")
                set_dve.done(dve.tensor_copy(xT[:, k, :], ps[:, k, :]), f"x{k}")
            for j in range(4):
                split(by["q"], j, 0)
            set_dve.wait(dve, "vec1")
            norm("mix")
            for name in ("q", "k", "gk", "v", "za"):
                run(name, nothing)

            for h in range(GH):
                gp_act.wait(dve, f"abs{h}")
                gp_dve.done(dve.tensor_scalar(bT[:, h, :], ps[:, 4 + h, :], vcol("bgk", h), 0.0, ALU.add, ALU.min), f"min{h}")
            set_pool.wait(dve, "reset")
            for h in range(GH):
                gp_act.wait(dve, f"ln{h}")
                gp_dve.wait(dve, f"min{h}")
                gp_dve.done(dve.tensor_tensor(ex[:, h, :], bT[:, h, :], ex[:, h, :], ALU.subtract), f"sum{h}")
                gp_dve.wait(dve, f"sum{h}")
                gp_dve.done(dve.tensor_tensor_scan(bT[:, h, :], reset[:, :], ex[:, h, :], 0.0, ALU.mult, ALU.add), f"scan{h}")
            gp_dve.wait(dve, "scan3")
            chunks = bT[:, :, :].rearrange("p h (n c) -> p (h n) c", c=GCH)
            last = chunks[:, :, GCH - 1:GCH].to_broadcast([P, GH * S // GCH, GCH])
            gp_dve.done(dve.tensor_tensor(kdT[:, :, :].rearrange("p h (n c) -> p (h n) c", c=GCH), last, chunks,
                                          ALU.subtract), "argkd")
            gp_act.wait(dve, "ekd")
            gp_dve.done(dve.tensor_tensor(kdT[:, :, :], kdT[:, :, :], kT[:, :, :], ALU.mult), "kd")
            gp_dve.done(dve.tensor_tensor(qT[:, :, :], qT[:, :, :], ex[:, :, :], ALU.mult), "qin")
            gp_dve.done(dve.tensor_copy(sm[:, 0:32], ex[:, :, :].rearrange("p h (n c) -> p (h n) c", c=GCH)[:, :, GCH - 1]), "decay")
            gp_act.wait(dve, "enb")
            gp_dve.done(dve.tensor_tensor(kT[:, :, :], kT[:, :, :], ex[:, :, :], ALU.mult), "kin")
            gp_dve.wait(dve, "kin")
            gp_dve.done(dve.memset(state[:, :, :], 0.0), "zero")
            gp_dve.done(dve.memset(scoresT[:, :, :], 0.0), "zero2")
            gp_pool.wait(dve, "m2")
            gp_dve.done(dve.tensor_copy(gla_mask[:, :, :], maskf[:, :, :]), "mask")
            gp_dve.wait(dve, "mask")
            for i in range(TT):
                g_pe.wait(dve, "a", i)
                g_dve.done(dve.copy_predicated(scoresT[:, :, :], gla_mask[:, :, :], tiles4(ps[:, 4, :])), "at")
                for c in range(2):
                    for h in range(GH):
                        if h % 2 == 0:
                            g_pe.wait(dve, f"kv{'AB'[h // 2]}{c}", i)
                        n = h * (S // GCH) + 2 * i + c
                        g_dve.done(dve.scalar_tensor_tensor(
                            out=state[:, h, :], in0=state[:, h, :], scalar=sm[:, n:n + 1],
                            in1=ps[:, 7 if h < 2 else 4, h % 2 * GDV:(h % 2 + 1) * GDV],
                            op0=ALU.mult, op1=ALU.add), f"st{c}{h}")
                    g_dve.wait(dve, f"st{c}3", i)
                g_act.wait(dve, "root", i)
                g_dve.done(dve.reciprocal(sm[:, 40:44], sm[:, 36:40]), "rstd")
                g_pe.wait(dve, "oT", i)
                for r in range(2):
                    oT = ps[:, 5:7, :].rearrange("p b (q r t) -> p (b q) r t", q=2, r=2)[:, :, r, :]
                    g_dve.done(dve.scalar_tensor_tensor(
                        out=tiles4(scr[1 + r]), in0=oT, scalar=vcol("gla", r),
                        in1=by_parity(za, r)[:, :, i * P:(i + 1) * P], op0=ALU.mult, op1=ALU.mult), f"t{r}")
                for r in range(2):
                    g_act.wait(dve, f"hi{r}", i)
                    g_dve.done(dve.tensor_tensor(by_parity(oa_lo, r)[:, :, i * P:(i + 1) * P], tiles4(scr[1 + r]),
                                                 by_parity(oa_hi, r)[:, :, i * P:(i + 1) * P].bitcast(F32),
                                                 ALU.subtract), f"lo{r}")
            g_dve.wait(dve, "lo1", 3)
            cv_pad.done(dve.memset(scr[1][:, 0:2], 0.0), "pad")

            def conv(st, j, i):
                u, t, y = scr[1], scr[2], scr[4]
                if j == 1:
                    dve.wait_ge(s_mm[1], st.use[1] + i + 1)
                    dve.wait_ge(s_ev[0], st.use[0] + i + 1)
                    dve.tensor_tensor(u[:, 2:S + 2], scr[0][:, 0:S], ps[:, 1, :], ALU.mult).then_inc(s_ev[1], 1)
                    dve.wait_ge(s_ev[1], st.use[1] + i + 1)
                    cv_pad.wait(dve, "pad")
                    cv_dve.done(dve.tensor_scalar(t[:, 0:S], u[:, 0:S], vec[:, ds1(col["conv"], i)], None, ALU.mult), "c0")
                    for n in (1, 2):
                        cv_dve.wait(dve, f"c{n - 1}", i)
                        cv_dve.done(dve.scalar_tensor_tensor(
                            out=t[:, 0:S], in0=u[:, n:S + n], scalar=vec[:, ds1(col["conv"] + 8 * n, i)],
                            in1=t[:, 0:S], op0=ALU.mult, op1=ALU.add), f"c{n}")
                elif j == 2:
                    dve.wait_ge(s_mm[2], st.use[2] + i + 1)
                    cv_dve.wait(dve, "c2", i)
                    dve.tensor_tensor(t[:, 0:S], t[:, 0:S], ps[:, 2, :], ALU.mult).then_inc(s_ev[2], 1)
                elif j == 3:
                    dve.wait_ge(s_ev[3], st.use[3] + i + 1)
                    dve.wait_ge(s_ev[2], st.use[2] + i + 1)
                    cv_dve.done(dve.tensor_tensor(y[:, 0:S], t[:, 0:S], scr[3][:, 0:S], ALU.mult), "y")
                    cv_act.wait(dve, "hi", i)
                    cv_dve.done(dve.tensor_tensor(yc_lo[:, i, :], y[:, 0:S], yc_hi[:, i, :].bitcast(F32),
                                                  ALU.subtract), "lo")
                    cv_dve.wait(dve, "lo", i)

            run("conv", conv)

            def merge(which):
                def evac(st, j, i):
                    if j < 2:
                        return
                    dve.wait_ge(s_mm[j], st.use[j] + i + 1)
                    dve.wait_ge(s_ev[j - 2], st.use[j - 2] + i + 1)
                    dve.tensor_tensor(scr[j][:, 0:S], scr[j - 2][:, 0:S], ps[:, j, :], ALU.mult).then_inc(s_ev[j], 1)
                    if j == 3:
                        dve.wait_ge(s_ev[2], st.use[2] + i + 1)
                        dve.wait_ge(s_ev[3], st.use[3] + i + 1)
                        mg_dve[which].done(dve.tensor_tensor(scr[3][:, 0:S], scr[2][:, 0:S], scr[3][:, 0:S], ALU.add), "m")
                        mg_act[which].wait(dve, "hi", i)
                        mg_dve[which].done(dve.tensor_tensor(m_lo[:, i, :], scr[3][:, 0:S], m_hi[:, i, :].bitcast(F32),
                                                             ALU.subtract), "lo")
                        mg_dve[which].wait(dve, "lo", i)
                return evac

            def residual(which):
                def evac(st, j, i):
                    dve.wait_ge(s_mm[j], st.use[j] + i + 1)
                    dve.tensor_tensor(xT[:, 4 * i + j, :], xT[:, 4 * i + j, :], ps[:, j, :], ALU.add).then_inc(s_ev[j], 1)
                return evac

            run("merge", merge(1))
            run("out", residual(1))
            for k in range(2):
                p_act.wait(dve, f"hi{k}")
                p_dve.done(dve.tensor_tensor(pT_lo[:, k, :], ps[:, 5 + k, :], pT_hi[:, k, :].bitcast(F32), ALU.subtract), f"lo{k}")
            norm("ple")

            def ple(st, j, i):
                if j % 2:
                    dve.wait_ge(s_mm[j], st.use[j] + i + 1)
                    dve.wait_ge(s_ev[j - 1], st.use[j - 1] + i + 1)
                    dve.tensor_tensor(scr[j][:, 0:S], scr[j - 1][:, 0:S], ps[:, j, :], ALU.mult).then_inc(s_ev[j], 1)
                    dve.wait_ge(s_ev[j], st.use[j] + i + 1)
                    xk = xT[:, 2 * i + j // 2, :]
                    pl_dve.done(dve.tensor_tensor(xk, xk, scr[j][:, 0:S], ALU.add), "xa" if j == 1 else "xb")
                    pl_dve.wait(dve, "xa" if j == 1 else "xb", i)

            run("ple", ple)
            norm("final")
            norm("mix2")
            n_dve["mix2"].wait(dve, "lo7")
            mq_pad.done(dve.memset(scr[0][:, 0:2], 0.0), "pad")
            mq_pad.done(dve.memset(scr[0][:, S + 2:S + 4], 0.0), "ones")

            mq_pad.done(dve.memset(m_tok[:, :, :, MD:MD + 1], 1.0), "col")

            def mqk(st, j, i):
                n = 4 * i + j
                t = scr[1 + n % 2]
                dve.wait_ge(s_ev[j], st.use[j] + i + 1)
                if n == 0:
                    mq_pad.wait(dve, "ones")
                if n >= 2:
                    mq_act.wait(dve, "silu", n - 2)
                mq_dve.done(dve.tensor_scalar(t[:, 0:S], scr[0][:, 0:S], vcol("conv2", n), None, ALU.mult), "c0")
                for m in range(1, 5):
                    mq_dve.wait(dve, f"c{m - 1}", n)
                    mq_dve.done(dve.scalar_tensor_tensor(
                        out=t[:, 0:S], in0=scr[0][:, m:S + m], scalar=vcol("conv2", 8 * m + n),
                        in1=t[:, 0:S], op0=ALU.mult, op1=ALU.add), f"c{m}")

            run("mqk", mqk)
            for name in ("mv", "mo", "mg", "dq", "dk"):
                run(name, nothing)
            run("dv", nothing, look=False)
            def mul(out, a, b):
                return dve.tensor_tensor(out, a, b, ALU.mult)

            def link(steps, ins, name):
                steps.done(ins, name)
                steps.wait(dve, name)

            def way(t, d):
                return t[0:32] if d == 0 else t[32:64, ::-1]

            rings_rest(dve)
            dve.wait_ge(s_ev[0], by["mg"].use[0] + 1)
            link(r_dve, dve.tensor_copy(rowf[:, :], gates[64:128, :]), "f")
            r_act.wait(dve, "ln")
            link(r_dve, dve.scalar_tensor_tensor(out=rowf[:, :], in0=rowf[:, :], scalar=0.0, in1=rowt[:, :],
                                                 op0=ALU.min, op1=ALU.subtract), "lf")
            r_pool.wait(dve, "n3")
            for d, name in ((0, "bf"), (1, "bb")):
                link(r_dve, dve.tensor_tensor_scan(way(rowb, d), way(rstm, d), way(rowf, d), 0.0, ALU.mult, ALU.add), name)
            link(r_dve, dve.tensor_tensor(rows[:, 0, :], gates[0:64, :], rowb[:, :], ALU.subtract), "c")
            for d, name in ((0, "mf"), (1, "mb")):
                c_way = rows[0:32, 0, :] if d == 0 else rows[32:64, 0, ::-1]
                link(r_dve, dve.tensor_tensor_scan(way(rowm, d), way(negm, d), c_way, -BIG, ALU.add, ALU.max), name)
            g_, cl, am, mo, mi, sp_, gm = (msm[0:64, 4 * n:4 * n + 4] for n in range(7))
            for src, dst, tag in ((rowb, 0, "g"), (rowm, 4, "l")):
                link(r_dve, dve.tensor_copy(msm[0:32, dst:dst + 4], src[0:32, P - 1:S:P]), tag + "0")
                link(r_dve, dve.tensor_copy(msm[32:64, dst:dst + 4], src[32:64, 0:S:P]), tag + "1")
            link(r_dve, dve.tensor_tensor(am, g_, cl, ALU.add), "am")
            link(r_dve, dve.tensor_tensor_scan(msm[0:32, 12:16], msm[0:32, 0:4], msm[0:32, 8:12], 0.0, ALU.add, ALU.max), "mo0")
            link(r_dve, dve.tensor_tensor_scan(msm[32:64, 12:16][:, ::-1], msm[32:64, 0:4][:, ::-1],
                                               msm[32:64, 8:12][:, ::-1], 0.0, ALU.add, ALU.max), "mo1")
            link(r_dve, dve.memset(mi, 0.0), "mi")
            link(r_dve, dve.tensor_copy(msm[0:32, 17:20], msm[0:32, 12:15]), "mi0")
            link(r_dve, dve.tensor_copy(msm[32:64, 16:19], msm[32:64, 13:16]), "mi1")
            link(r_dve, dve.tensor_tensor(sp_, g_, mi, ALU.add), "s0")
            link(r_dve, dve.tensor_tensor(sp_, sp_, mo, ALU.subtract), "s1")
            link(r_dve, dve.tensor_tensor(gm, g_, mo, ALU.subtract), "gm")

            def chunked(t):
                return t.rearrange("p (c t) -> p c t", t=P)

            def per_chunk(t):
                return t.unsqueeze(2).to_broadcast([64, TT, P])

            link(r_dve, dve.tensor_tensor(chunked(rowm[:, :]), chunked(rowm[:, :]), per_chunk(mi), ALU.max), "mt")
            link(r_dve, dve.tensor_tensor(chunked(rows[:, 1, :]), per_chunk(mi), chunked(rowm[:, :]), ALU.subtract), "a1")
            link(r_dve, dve.tensor_tensor(rows[:, 2, :], rowb[:, :], rowm[:, :], ALU.add), "a2")
            link(r_dve, dve.tensor_tensor(chunked(rows[:, 3, :]), chunked(rows[:, 0, :]), per_chunk(gm), ALU.add), "a3")
            link(r_dve, dve.tensor_scalar(rowt[:, :], rowm[:, :], -1.0, None, ALU.mult), "nm")
            for d in range(2):
                link(r_dve, dve.tensor_copy(selr[:, 4 * d:4 * d + 4, :],
                                            ident[0:64, 32 * d:32 * d + 4].unsqueeze(2).to_broadcast([64, 4, P])), f"sel{d}")
            r_act.wait(dve, "sp")
            link(r_dve, mul(spd[:, :, :], ident[0:64, 0:64].unsqueeze(2).to_broadcast([64, 64, TT]),
                            sp_.unsqueeze(1).to_broadcast([64, 64, TT])), "spd")
            r_act.wait(dve, "spb")
            r_pool.wait(dve, "mb")
            mq_pad.wait(dve, "col")

            for n, (h, d) in enumerate(WAYS):
                r = mrow(h, d)

                def col4(q, width):
                    return cols[:, :, q, r:r + 1].to_broadcast([P, TT, width])

                if n:
                    l_pe.wait(dve, f"kv{n - 1}")
                link(l_dve, mul(wv[:, :, :], m_tok[:, :, h, :], col4(3, MD + 1)), f"wv{n}")
                l_pe.wait(dve, f"nm{n}")
                link(l_dve, dve.tensor_tensor(arg[:, :, :], tiles4(ps[:, 4, :]), col4(0, P), ALU.add), f"arg{n}")
                link(l_dve, dve.tensor_tensor(arg[:, :, :], arg[:, :, :],
                                              m01[:, d, :].unsqueeze(1).to_broadcast([P, TT, P]), ALU.min), f"msk{n}")
                order = state_chunks(d)
                if n:
                    l_pe.wait(dve, f"inter{n - 1}")
                l_dve.done(dve.memset(cst[:, order[0], :], 0.0), f"z{n}")
                l_pe.wait(dve, f"kv{n}")
                for m in range(3):
                    kv = ps[:, 3, m * (MD + 1):(m + 1) * (MD + 1)]
                    if m == 0:
                        link(l_dve, dve.tensor_copy(cst[:, order[1], :], kv), f"cs0_{n}")
                    else:
                        link(l_dve, dve.scalar_tensor_tensor(
                            out=cst[:, order[m + 1], :], in0=cst[:, order[m], :], scalar=spb[:, r, order[m]:order[m] + 1],
                            in1=kv, op0=ALU.mult, op1=ALU.add), f"cs{m}_{n}")
                l_act.wait(dve, f"pt{n}")
                if n:
                    l_pe.wait(dve, f"intra{n - 1}")
                l_dve.done(mul(wt[:, :, :], pt[:, :, :], tiles4(ps[:, 5, :])), f"w{n}")
                l_pe.wait(dve, f"inter{n}")
                link(l_dve, mul(paired(nj), pairs(0), paired(cols[:, :, 1, r:r + 1]).to_broadcast([P, 2, 2, MD + 1])), f"tmp{n}")
                l_act.wait(dve, f"ni{n}")
                link(l_dve, dve.tensor_tensor(nj[:, :, :], nj[:, :, :], ni[:, :, :], ALU.add), f"num{n}")
                dn = msm[:, 64:68]
                link(l_dve, dve.scalar_tensor_tensor(out=dn, in0=nj[:, :, MD], scalar=-1.0, in1=nj[:, :, MD],
                                                     op0=ALU.mult, op1=ALU.max), f"ab{n}")
                link(l_dve, dve.tensor_tensor(dn, dn, cols[:, :, 2, r], ALU.max), f"den{n}")
                link(l_dve, dve.reciprocal(msm[:, 68:72], dn), f"rd{n}")
                rd = msm[:, 68:72].unsqueeze(2).to_broadcast([P, TT, MD])
                link(l_dve, mul(hsum[:, h, :, :] if d == 0 else nj[:, :, 0:MD], nj[:, :, 0:MD], rd), f"h{n}")
                if d:
                    link(l_dve, dve.tensor_tensor(hsum[:, h, :, :], hsum[:, h, :, :], nj[:, :, 0:MD], ALU.add), f"hs{n}")
                    for c in range(TT):
                        m = 100 + 6 * (h * TT + c)
                        l_dve.done(dve.bn_stats(msm[:, m:m + 6], hsum[:, h, c, :]), f"bn{c}_{n}")
            l_dve.wait(dve, "bn3_7")
            for m in range(MH * TT):
                l_dve.done(dve.bn_aggr(msm[:, 200 + 2 * m:202 + 2 * m], msm[:, 100 + 6 * m:106 + 6 * m]), f"ag{m}")
            f_act.wait(dve, "root")
            link(l_dve, dve.reciprocal(msm[:, 256:272], msm[:, 240:256]), "rstd")
            for h in range(MH):
                if h:
                    f_pe.wait(dve, f"t{h - 1}")
                for c in range(TT):
                    m = h * TT + c
                    f_dve.done(dve.tensor_scalar(hn[:, c, :], hsum[:, h, c, :], msm[:, 200 + 2 * m:201 + 2 * m],
                                                 msm[:, 256 + m:257 + m], ALU.subtract, ALU.mult), f"n{c}_{h}")
                f_pe.wait(dve, f"t{h}")
                if h >= 2:
                    f_dve.wait(dve, f"lo{h - 2}")
                f_dve.done(dve.scalar_tensor_tensor(out=scr[1 + h % 2][:, 0:S], in0=ps[:, 4 + h % 2, :], scalar=vcol("mnorm", h),
                                                    in1=moT[:, h, :], op0=ALU.mult, op1=ALU.mult), f"t{h}")
                f_act.wait(dve, f"hi{h}")
                f_dve.done(dve.tensor_tensor(hm_lo[:, h, :], scr[1 + h % 2][:, 0:S], hm_hi[:, h, :].bitcast(F32),
                                             ALU.subtract), f"lo{h}")

            f_dve.wait(dve, "lo3")
            d_pool.wait(dve, "iota")
            link(d_dve, dve.scalar_tensor_tensor(out=alibi[:, :], in0=alibi[:, :], scalar=-1.0, in1=alibi[:, :],
                                                 op0=ALU.mult, op1=ALU.max), "abs")
            dve.wait_ge(s_lam, 16)
            for m in range(2):
                link(d_dve, dve.tensor_tensor_reduce(pr[:, 0:DDH], lam_sb[:, 2 * m, :], lam_sb[:, 2 * m + 1, :], 1.0, 0.0,
                                                     ALU.mult, ALU.add, dsm[:, m:m + 1]), f"lam{m}")
            d_act.wait(dve, "lam1")
            link(d_dve, dve.tensor_tensor(dsm[:, 4:5], dsm[:, 3:4], dsm[:, 2:3], ALU.subtract), "lam2")
            link(d_dve, dve.tensor_scalar(dsm[:, 4:5], dsm[:, 4:5], -LAM_INIT, None, ALU.add), "lam3")
            link(d_dve, dve.tensor_scalar(dsm[:, 8:9], vcol("dnorm"), 1.0 - LAM_INIT, None, ALU.mult), "gain")
            for n, (h, q) in enumerate(DW):
                if q == 0:
                    d_act.wait(dve, f"al{n}")
                d_pe.wait(dve, f"s{n}")
                bias = alih[:, (TT - 1 - q) * P:(TT - 1 - q) * P + S]
                for i in range(2):
                    d_dve.done(dve.tensor_tensor_reduce(es[:, i, :], ps[:, n % 2 * 2 + i, :], bias, DDH ** -0.5, -BIG,
                                                        ALU.add, ALU.max, dsm[:, 10 + i:11 + i]), f"m{i}_{n}")
                d_dve.wait(dve, f"m1_{n}")
                d_dve.done(dve.tensor_scalar(dsm[:, 12:14], dsm[:, 10:12], -1.0, None, ALU.mult), f"neg{n}")
                d_act.wait(dve, f"e1_{n}")
                link(d_dve, dve.reciprocal(dsm[:, 16:18], dsm[:, 14:16]), f"rec{n}")
                link(d_dve, mul(dsm[:, 18:19], dsm[:, 17:18], dsm[:, 4:5]), f"rl{n}")
                link(d_dve, dve.tensor_scalar(pr[:, :], es[:, 0, :], dsm[:, 16:17], None, ALU.mult), f"p{n}")
                if n:
                    d_pe.wait(dve, f"t{n - 1}")
                link(d_dve, dve.scalar_tensor_tensor(out=aa[:, :], in0=es[:, 1, :], scalar=dsm[:, 18:19], in1=pr[:, :],
                                                     op0=ALU.mult, op1=ALU.add), f"a{n}")
                if q == TT - 1:
                    d_act.wait(dve, f"root{n}")
                    d_dve.done(dve.reciprocal(dsm[:, 28:32], dsm[:, 24:28]), f"rstd{n}")
                    d_act.wait(dve, f"hi{n}")
                    d_dve.done(dve.scalar_tensor_tensor(out=hd_lo[:, h, :], in0=ps[:, 7, :], scalar=dsm[:, 8:9],
                                                        in1=hd_hi[:, h, :].bitcast(F32), op0=ALU.mult,
                                                        op1=ALU.subtract), f"lo{n}")

            for j in range(4):
                split(by["merge2"], j, 0)
            run("merge2", merge(2))
            run("out2", residual(2))

            dve.wait_ge(s_rw, 16)
            fg = vec[:, col["ffn"]:col["ffn"] + KD].unsqueeze(2).to_broadcast([P, KD, NE])
            t_dve.done(mul(rwg[:, :, :], rw[:, :, :], fg), "rwg")
            for t in range(TT):
                t_pe.wait(dve, f"x{t}")
                t_dve.done(dve.tensor_copy(x2[:, t, S:D], ps[:, 2 * t + 1, :]), f"x{t}")
            t_act.wait(dve, "root")
            link(t_dve, dve.reciprocal(esm[:, 8:12], esm[:, 4:8]), "rstd")
            dve.wait_ge(s_g, 16)
            for t in range(TT):
                t_dve.done(dve.scalar_tensor_tensor(out=h2[:, t, :], in0=x2[:, t, :], scalar=esm[:, 8 + t:9 + t],
                                                    in1=gbc[:, :], op0=ALU.mult, op1=ALU.mult), f"h{t}")
            t_pe.wait(dve, "logits")

            def per_token(c):
                return esm[:, c:c + 4].unsqueeze(2).to_broadcast([P, TT, NE])

            link(t_dve, mul(lg[:, :, :], ps[:, 0, 0:TT * NE].rearrange("p (t e) -> p t e", e=NE), per_token(8)), "lg")
            link(t_dve, dve.tensor_reduce(esm[:, 12:16], lg[:, :, :], AX, ALU.max), "mx")
            link(t_dve, dve.tensor_tensor(lg[:, :, :], lg[:, :, :], per_token(12), ALU.subtract), "sub")
            t_act.wait(dve, "exp")
            link(t_dve, dve.tensor_reduce(esm[:, 24:28], lg[:, :, :], AX, ALU.add), "sum")
            link(t_dve, dve.reciprocal(esm[:, 28:32], esm[:, 24:28]), "rec")
            link(t_dve, mul(aff[:, :, :], lg[:, :, :], per_token(28)), "aff")
            t_pe.wait(dve, "affT")
            link(t_dve, dve.tensor_copy(aw[:, :], ps[0:NE, 1, :]), "aw")
            for n in range(CAP // 8):
                link(t_dve, dve.max(top8[:, :], aw[:, :]), f"top{n}")
                link(t_dve, dve.match_replace(aw[:, :], top8[:, :], aw[:, :], -1.0), f"rep{n}")
            link(t_dve, dve.memset(awo[:, :], 1.0), "one")
            link(t_dve, dve.tensor_scalar(awm[:, :], aw[:, :], 0.0, None, ALU.is_lt), "mask")
            link(t_dve, dve.tensor_tensor_scan(awc[:, :], awo[:, :], awm[:, :], 0.0, ALU.mult, ALU.add), "scan")
            link(t_dve, mul(awc[:, :], awc[:, :], awm[:, :]), "sel")
            t_pe.wait(dve, "posT")
            link(t_dve, dve.tensor_copy(pos[:, :, :], ps[:, 2, 0:TT * NE].rearrange("p (t e) -> p t e", e=NE)), "pos")
            t_pool.wait(dve, "iota")

            def choose(e):
                slot = pos[:, :, bass.ds(e, 1)].to_broadcast([P, TT, CAP])
                number = iot[:, :].unsqueeze(1).to_broadcast([P, TT, CAP])
                x_dve.done(dve.tensor_tensor(pick[:, :, :], slot, number, ALU.is_equal), "pick")
                x_dve.wait(dve, "pick", e)

            def expert(e, more=True):
                weight = aff[:, :, bass.ds(e, 1)].to_broadcast([P, TT, CAP])
                for r in range(2):
                    e_dve.done(mul(pickg[:, :, r, :], pick[:, :, :], weight), f"pg{r}")
                if more:
                    x_pe.wait(dve, "gather", e)
                    e_dve.wait(dve, "pg1", e)
                    choose(e + 1)
                used(dve, e, 15)
                e_act.wait(dve, "s1", e)
                for q in range(2):
                    e_dve.done(mul(hid[:, q, :], sg[:, q, :], ps[:, 2 + q, :]), f"hid{q}")
                e_pe.wait(dve, "hT", e)
                e_dve.done(dve.tensor_copy(hidT[:, 1, :, :], tiles4(ps[:, 6, :])), "hT1")
                for t, b in enumerate((5, 0, 2, 5)):
                    e_pe.wait(dve, f"o{t}", e)
                    row = x2[:, t, :].rearrange("p (d c) -> p d c", d=2)
                    e_dve.done(dve.tensor_tensor(row, row, ps[:, b:b + 2, :], ALU.add), f"o{t}")

            choose(0)
            with dve.Fori(0, NE - 1) as e:
                expert(e)
            expert(NE - 1, more=False)
            z_act.wait(dve, "root")
            link(z_dve, dve.reciprocal(esm[:, 32:36], esm[:, 20:24]), "rstd")
            dve.wait_ge(s_g, 32)
            for t in range(TT):
                if t >= 2:
                    dve.wait_ge(s_store[t % 2], 16)
                z_dve.done(dve.scalar_tensor_tensor(out=fin[:, t % 2, :], in0=x2[:, t, :], scalar=esm[:, 32 + t:33 + t],
                                                    in1=gbc[:, :], op0=ALU.mult, op1=ALU.mult), f"y{t}")

        @block.tensor
        def _(pe):
            def group(st, j, i, rhs_hi, rhs_lo, k0=0):
                pe.wait_ge(s_lo[j], st.use[j] + i + 1)
                if not (isinstance(i, int) and st.use[j] + i == 0):
                    pe.wait_ge(s_ev[j], st.use[j] + i)
                nk, w = span(st, j, i), width(st)
                dst = ps[0:w, j, :]
                for k in range(nk):
                    for n, (lt, rt) in enumerate(((w_hi, rhs_hi), (w_hi, rhs_lo), (w_lo, rhs_hi))):
                        mm = pe.matmul(dst, lt[:, j, k, 0:w], rt[:, k0 + k, :], start=k == 0 and n == 0,
                                       stop=k == nk - 1 and n == 2)
                mm.then_inc(s_mm[j], 1)

            def group_tok(st, i):
                for j in range(4):
                    pe.wait_ge(s_lo[j], st.use[j] + i + 1)
                for t in range(TT):
                    pe.wait_ge(s_ev[t], st.use[t] + i)
                    for k in range(KD):
                        for n, (lt, rt) in enumerate(((h_hi, w_hi), (h_hi, w_lo), (h_lo, w_hi))):
                            mm = pe.matmul(ps[:, t, :], lt[:, k, t * P:(t + 1) * P], rt[:, :, k, :],
                                           start=k == 0 and n == 0, stop=k == KD - 1 and n == 2)
                    mm.then_inc(s_mm[t], 1)

            def run(name, rhs=None):
                st = by[name]
                rhs = rhs or [(h_hi, h_lo)] * 4

                def body(i):
                    if st.kind == "tok":
                        group_tok(st, i)
                    else:
                        for j in range(len(st.tiles)):
                            group(st, j, i, *rhs[j])
                if st.n <= 2:
                    for i in range(st.n):
                        body(i)
                else:
                    with pe.Fori(0, st.n) as i:
                        body(i)

            def norm(n):
                for k in range(KD):
                    n_act[n].wait(pe, f"sq{k}")
                    mm = pe.matmul(ps[:, 4, :], ones[:, :], sq[:, k, :], start=k == 0, stop=k == KD - 1)
                n_pe[n].done(mm, "sum")

            set_pool.wait(pe, "ones")
            pe.wait_ge(s_small, 16 * (len(vec_loads) + 4))
            for g in range(2):
                set_pe.done(pe.transpose(ps[:, g, 0:P], vrow[:, g, :], ident[:, :]), f"vec{g}")
            pe.wait_ge(s_x, 16 * TT)
            set_dve.wait(pe, "vec1")
            for k in range(KD):
                for t in range(TT):
                    mm = pe.transpose(ps[:, k, t * P:(t + 1) * P], x_tok[:, t, k * P:(k + 1) * P], ident[:, :])
                set_pe.done(mm, f"x{k}")
            set_dve.wait(pe, "x7")
            set_act.wait(pe, "x6")
            norm("mix")
            n_dve["mix"].wait(pe, "lo7")
            run("q")
            run("k")
            run("gk")
            pe.wait_ge(s_gw, 16)
            pe.wait_ge(s_ev[0], by["gk"].use[0] + 1)
            for h in range(GH):
                gp_pe.done(pe.matmul(ps[:, 4 + h, :], wgk[:, h * GDK:(h + 1) * GDK], gk_sb[:, :],
                                     start=True, stop=True), f"gk{h}")
            run("v")
            run("za")
            gp_dve.wait(pe, "kd")
            for t in range(TT):
                for h in range(GH):
                    mm = pe.transpose(ps[:, 4 + t, h * P:(h + 1) * P], kdT[:, h, t * P:(t + 1) * P], ident[:, :])
                gp_pe.done(mm, f"kd{t}")
            gp_act.wait(pe, "kd3")
            gp_dve.wait(pe, "mask")
            for i in range(TT):
                tok = slice(i * P, (i + 1) * P)
                if i:
                    g_dve.wait(pe, "st13", i - 1)
                for h in range(GH):
                    mm = pe.matmul(ps[:, 4, h * P:(h + 1) * P], kT[:, h, tok], qT[:, h, tok], start=h == 0,
                                   stop=True, skip_group_check=True)
                g_pe.done(mm, "a")
                g_dve.wait(pe, "at", i)
                if i:
                    g_dve.wait(pe, "t1", i - 1)
                for h in range(GH):
                    pe.matmul(ps[:, 5 + h // 2, h % 2 * GDV:(h % 2 + 1) * GDV], scoresT[:, h, :],
                              v_tok[:, i, h * GDV:(h + 1) * GDV], start=h % 2 == 0, stop=False, skip_group_check=True)
                for c in range(2):
                    half = slice(c * GCH, (c + 1) * GCH)
                    tokc = slice(i * P + c * GCH, i * P + (c + 1) * GCH)
                    if c:
                        g_dve.wait(pe, "st03", i)
                    for h in range(GH):
                        pe.matmul(ps[half, 5 + h // 2, h % 2 * GDV:(h % 2 + 1) * GDV], qT[:, h, tokc],
                                  state[:, h, :], start=False, stop=c == 1, skip_group_check=True)
                    for h in range(GH):
                        mm = pe.matmul(ps[:, 7 if h < 2 else 4, h % 2 * GDV:(h % 2 + 1) * GDV],
                                       kd_tok[half, i, h * GDK:(h + 1) * GDK], v_tok[half, i, h * GDV:(h + 1) * GDV],
                                       start=h % 2 == 0, stop=True, skip_group_check=True)
                        if h % 2:
                            g_pe.done(mm, f"kv{'AB'[h // 2]}{c}")
                g_act.wait(pe, "on3", i)
                for n in range(KD):
                    mm = pe.transpose(ps[:, 5 + n // 4, n % 4 * P:(n % 4 + 1) * P], o_norm[:, n * P:(n + 1) * P], ident[:, :])
                g_pe.done(mm, "oT")
            run("conv")
            g_dve.wait(pe, "lo1", 3)
            cv_dve.wait(pe, "lo", 7)
            run("merge", [(h_hi, h_lo), (h_hi, h_lo), (oa_hi, oa_lo), (yc_hi, yc_lo)])
            mg_dve[1].wait(pe, "lo", 7)
            run("out", [(m_hi, m_lo)] * 4)
            pe.wait_ge(s_p, 16)
            for k in range(2):
                for t in range(TT):
                    mm = pe.transpose(ps[:, 5 + k, t * P:(t + 1) * P], p_tok[:, t, k * P:(k + 1) * P], ident[:, :])
                p_pe.done(mm, f"p{k}")
            norm("ple")
            n_dve["ple"].wait(pe, "lo7")
            p_dve.wait(pe, "lo1")
            run("ple", [(h_hi, h_lo), (pT_hi, pT_lo), (h_hi, h_lo), (pT_hi, pT_lo)])
            norm("final")
            norm("mix2")
            n_dve["mix2"].wait(pe, "lo7")
            for name in ("mqk", "mv", "mo", "mg", "dq", "dk", "dv"):
                run(name)
            kt_act.wait(pe, "scaled")
            for c in range(TT):
                pe.wait_ge(s_ev[c], by["dv"].use[c] + 1)
                for h in range(MH):
                    mm = pe.transpose(ps[:, c, h * P:(h + 1) * P], mqkT[:, MH + h, c * P:(c + 1) * P], ident[:, :])
                kt_pe.done(mm, f"kt{c}")
            r_act.wait(pe, "e3")
            for c in range(TT):
                for q in range(4):
                    k = c % 2 * 256 + q * 64
                    mm = pe.transpose(ps[:, 4 + c // 2, k:k + 64], rows[:, q, c * P:(c + 1) * P], ident[0:64, 0:64])
            r_pe.done(mm, "cols")
            r_dve.wait(pe, "spd")
            r_pe.done(pe.matmul(ps[:, 6, 0:256], ones[0:64, :], spd[:, :, :], start=True, stop=True), "spb")
            kt_act.wait(pe, "kt3")
            r_act.wait(pe, "spb")
            for n, (h, d) in enumerate(WAYS):
                if d == 0:
                    if n:
                        l_dve.wait(pe, f"w{n - 1}")
                    for c in range(TT):
                        tok = slice(c * P, (c + 1) * P)
                        mm = pe.matmul(ps[:, 5, tok], mqkT[:, MH + h, tok], mqkT[:, h, tok], start=True, stop=True)
                    l_pe.done(mm, f"kq{n}")
                if n:
                    l_dve.wait(pe, f"arg{n - 1}")
                l_pe.done(pe.matmul(ps[:, 4, :], selr[:, 4 * d + h, :], rowt[:, :], start=True, stop=True), f"nm{n}")
                l_dve.wait(pe, f"wv{n}")
                if n:
                    l_dve.wait(pe, f"cs2_{n - 1}")
                for m, c in enumerate(state_chunks(d)[:3]):
                    mm = pe.matmul(ps[:, 3, m * (MD + 1):(m + 1) * (MD + 1)], ktok[:, c, h * MD:(h + 1) * MD],
                                   wv[:, c, :], start=True, stop=True)
                l_pe.done(mm, f"kv{n}")
                l_dve.wait(pe, f"w{n}")
                if n:
                    l_act.wait(pe, f"ni{n - 1}")
                for c in range(TT):
                    mm = pe.matmul(ps[:, 6 + c // 2, c % 2 * (MD + 1):(c % 2 + 1) * (MD + 1)], wt[:, c, :],
                                   m_tok[:, c, h, :], start=True, stop=True)
                l_pe.done(mm, f"intra{n}")
                l_dve.wait(pe, f"tmp{n - 1}" if n else f"cs2_{n}")
                for c in range(TT):
                    mm = pe.matmul(ps[:, c // 2, c % 2 * (MD + 1):(c % 2 + 1) * (MD + 1)], mqkT[:, h, c * P:(c + 1) * P],
                                   cst[:, c, :], start=True, stop=True)
                l_pe.done(mm, f"inter{n}")
            l_dve.wait(pe, "arg7")
            for h in range(MH):
                f_dve.wait(pe, f"n3_{h}")
                if h >= 2:
                    f_dve.wait(pe, f"t{h - 2}")
                for c in range(TT):
                    mm = pe.transpose(ps[:, 4 + h % 2, c * P:(c + 1) * P], hn[:, c, :], ident[:, :])
                f_pe.done(mm, f"t{h}")
            f_dve.wait(pe, "t3")

            def scores(n):
                h, q = DW[n]
                if n >= 2:
                    d_dve.wait(pe, f"m1_{n - 2}")
                for i in range(2):
                    half = slice(i * DDH, (i + 1) * DDH)
                    mm = pe.matmul(ps[:, n % 2 * 2 + i, :], dqT[half, h, q * P:(q + 1) * P], dkT[half, h, :],
                                   start=True, stop=True)
                d_pe.done(mm, f"s{n}")

            scores(0)
            for n, (h, q) in enumerate(DW):
                d_dve.wait(pe, f"a{n}")
                if n:
                    d_act.wait(pe, f"t{n - 1}")
                for c in range(TT):
                    mm = pe.transpose(ps[:, 4, c * P:(c + 1) * P], aa[:, c * P:(c + 1) * P], ident[:, :])
                d_pe.done(mm, f"t{n}")
                if n + 1 < len(DW):
                    scores(n + 1)
                d_act.wait(pe, f"t{n}")
                for c in range(TT):
                    mm = pe.matmul(ps[:, 5 + h % 2, q * P:(q + 1) * P], aaT[:, c, :], d_tok[:, c, h * DDV:(h + 1) * DDV],
                                   start=c == 0, stop=c == TT - 1)
                d_pe.done(mm, f"o{n}")
                if q == TT - 1:
                    d_act.wait(pe, f"o3_{n}")
                    if n >= TT:
                        d_dve.wait(pe, f"lo{n - TT}")
                    for c in range(TT):
                        mm = pe.transpose(ps[:, 7, c * P:(c + 1) * P], od[:, c, :], ident[:, :])
                    d_pe.done(mm, f"oT{n}")
            d_dve.wait(pe, "lo15")
            run("merge2", [(h_hi, h_lo), (h_hi, h_lo), (hm_hi, hm_lo), (hd_hi, hd_lo)])
            mg_dve[2].wait(pe, "lo", 7)
            run("out2", [(m_hi, m_lo)] * 4)

            for b in range(4):
                pe.wait_ge(s_ev[b], by["out2"].use[b] + 2)
            for t in range(TT):
                for k in range(KD):
                    mm = pe.transpose(ps[:, 2 * t + k // 4, k % 4 * P:(k % 4 + 1) * P], xT[:, k, t * P:(t + 1) * P], ident[:, :])
                t_pe.done(mm, f"x{t}")
            t_dve.wait(pe, "x0")
            t_act.wait(pe, "x0")
            for t in range(TT):
                for k in range(KD):
                    mm = pe.matmul(ps[:, 0, t * NE:(t + 1) * NE], xT[:, k, t * P:(t + 1) * P], rwg[:, k, :],
                                   start=k == 0, stop=k == KD - 1)
            t_pe.done(mm, "logits")
            t_dve.wait(pe, "aff")
            for t in range(TT):
                mm = pe.transpose(ps[0:NE, 1, t * P:(t + 1) * P], aff[:, t, :], ident[:, :])
            t_pe.done(mm, "affT")
            t_dve.wait(pe, "sel")
            for t in range(TT):
                mm = pe.transpose(ps[:, 2, t * NE:(t + 1) * NE], awc[:, t * P:(t + 1) * P], ident[0:NE, 0:NE])
            t_pe.done(mm, "posT")
            t_dve.wait(pe, "pos")

            def gather(e):
                x_dve.wait(pe, "pick", e)
                for k in range(KD):
                    for t in range(TT):
                        mm = pe.matmul(ps[:, 7, k * CAP:(k + 1) * CAP], h2[:, t, k * P:(k + 1) * P], pick[:, t, :],
                                       start=t == 0, stop=t == TT - 1)
                x_pe.done(mm, "gather")

            def chunk(e, n):
                pe.wait_ge(s_ring[n % RING], (e * 2 + (n // RING + 1)) * 16)

            def expert(e, more=True):
                x_act.wait(pe, "xe", e)
                for m in range(2):
                    for k in range(KD):
                        n = m * KD + k
                        chunk(e, n)
                        for q in range(2):
                            for half in range(2):
                                mm = pe.matmul(ps[half * CAP:(half + 1) * CAP, 2 * m + q, :], xe[:, k, :],
                                               ring[:, n % RING, (2 * q + half) * S:(2 * q + half + 1) * S],
                                               start=k == 0, stop=k == KD - 1, skip_group_check=True)
                        mm.then_inc(s_free[n % RING], 1)
                if more:
                    gather(e + 1)
                e_dve.wait(pe, "hid1", e)
                for q in range(2):
                    for c in range(4):
                        mm = pe.transpose(ps[:, 5 + q, c * P:(c + 1) * P], hid[:, q, c * P:(c + 1) * P], ident[:, :])
                e_pe.done(mm, "hT")
                e_act.wait(pe, "hT0", e)
                e_dve.wait(pe, "hT1", e)
                for i in range(8):
                    n = 16 + i
                    chunk(e, n)
                    for j in range(2):
                        q, half, c = i // 4, i // 2 % 2, 2 * i % 4 + j
                        for d in range(2):
                            mm = pe.matmul(ps[d * CAP:(d + 1) * CAP, 4, :], hidT[:, q, c, half * CAP:(half + 1) * CAP],
                                           ring[:, n % RING, j * D + d * S:j * D + (d + 1) * S],
                                           start=i == 0 and j == 0, stop=i == 7 and j == 1, skip_group_check=True)
                    mm.then_inc(s_free[n % RING], 1)
                if more:
                    x_act.wait(pe, "xe", e + 1)
                e_dve.wait(pe, "pg1", e)
                for t in range(TT):
                    mm = pe.transpose(ps[:, 7, t * P:(t + 1) * P], pickg[:, t, :, :], ident[:, :])
                e_pe.done(mm, "place")
                e_act.wait(pe, "place", e)
                for t, b in enumerate((5, 0, 2, 5)):
                    if t == 3:
                        e_dve.wait(pe, "o0", e)
                    for d in range(2):
                        half = slice(d * CAP, (d + 1) * CAP)
                        mm = pe.matmul(ps[:, b + d, :], place[half, t * P:(t + 1) * P], ye[half, :], start=True, stop=True)
                    e_pe.done(mm, f"o{t}")
                e_dve.wait(pe, "o2", e)

            gather(0)
            with pe.Fori(0, NE - 1) as e:
                expert(e)
            expert(NE - 1, more=False)


_INS = ["x", "p", "norm_mix_g", "w_in", "b_merge", "w_gk2", "b_gk", "gla_norm_g", "conv_w",
        "w_branch_a", "w_branch_c", "w_out", "norm_ple_g", "w_ple_gate", "w_ple_proj", "norm_final_g",
        "norm_mix_g_2", "w_in_2", "b_mgate_2", "conv_w_2", "conv_b_2", "mlstm_norm_g_2", "diff_lam_2",
        "diff_norm_g_2", "w_up_a_2", "w_up_b_2", "w_out_2", "norm_ffn_g_2", "w_router_2", "w_gate_e_2",
        "w_up_e_2", "w_down_e_2", "norm_f_g_2"]


def kernel(**inputs):
    import numpy as np
    import concourse.bacc as bacc
    from concourse.bass_utils import run_bass_kernel_spmd

    nc = bacc.Bacc("TRN2", target_bir_lowering=False, num_devices=1)
    arrays, args = {}, {}
    for name in _INS:
        array = np.ascontiguousarray(inputs[name])
        arrays[f"in_{name}"] = array
        args[name] = nc.dram_tensor(f"in_{name}", array.shape, mybir.dt.from_np(array.dtype), kind="ExternalInput").ap()
    args["out"] = nc.dram_tensor("out_y", (1, S, D), F32, kind="ExternalOutput").ap()
    kernel_program(nc, **args)
    result = run_bass_kernel_spmd(nc, [arrays], core_ids=[0])
    return result.results[0]["out_y"]
```

```python
import math
from contextlib import ExitStack

import concourse.bass as bass
from concourse import mybir

F32 = mybir.dt.float32
F32R = mybir.dt.float32r
I32 = mybir.dt.int32
ALU = mybir.AluOpType
ACT = mybir.ActivationFunctionType
AX = mybir.AxisListType.X

P = 128
S = 512
TT = S // P
D = 1024
KD = D // P
EPS = 1e-6
GH, GDK, GDV, GCH = 4, 128, 256, 64
RANK = 16
GATE_NORM = 16.0
PLE = 256
OFF_Q, OFF_K, OFF_V, OFF_ZA, OFF_GK = 0, 512, 1024, 2048, 3072
OFF_CB = OFF_GK + RANK
OFF_CC, OFF_XC, OFF_ZC, OFF_GA, OFF_GC = (OFF_CB + 1024 * n for n in range(1, 6))
MH, MD = 4, 128
OFF_MQ, OFF_MV, OFF_MO, OFF_MG = 0, 1024, 1536, 2048
OFF_DQ = OFF_MG + 4 * MH
OFF_DK, OFF_DV, OFF_G2 = OFF_DQ + 512, OFF_DQ + 1024, OFF_DQ + 1536
NH, DDH, DDV = 4, 64, 128
LAM_INIT = 0.8 - 0.6 * math.exp(-0.3 * 0)
NE, CAP, FF = 16, 64, 2048
BIG = 3.0e38
KB = 1024
RING = 12


class Steps:

    def __init__(self, sem, names):
        self.sem, self.names, self.next = sem, list(names), 0
        self.index = {n: k for k, n in enumerate(self.names)}
        assert len(self.index) == len(self.names)

    def done(self, instruction, name):
        want = self.names[self.next % len(self.names)]
        assert want == name, (name, want)
        self.next += 1
        instruction.then_inc(self.sem, 1)

    def wait(self, eng, name, i=0):
        eng.wait_ge(self.sem, i * len(self.names) + (self.index[name] + 1))


class Stage:

    def __init__(self, name, n, tiles, kind="T"):
        self.name, self.n, self.tiles, self.kind = name, n, tiles, kind
        self.use = self.before = None


def kernel_program(nc, x, p, norm_mix_g, w_in, b_merge, w_gk2, b_gk, gla_norm_g, conv_w, w_branch_a,
                   w_branch_c, w_out, norm_ple_g, w_ple_gate, w_ple_proj, norm_final_g, norm_mix_g_2,
                   w_in_2, b_mgate_2, conv_w_2, conv_b_2, mlstm_norm_g_2, diff_lam_2, diff_norm_g_2,
                   w_up_a_2, w_up_b_2, w_out_2, norm_ffn_g_2, w_router_2, w_gate_e_2, w_up_e_2,
                   w_down_e_2, norm_f_g_2, out):
    ctx = ExitStack()
    with ctx:
        base = (nc.sbuf_base + 31) // 32 * 32

        def at(name, shape, kb, dt=F32):
            n = 4
            for d in shape[1:]:
                n *= d
            assert base + kb * KB + n <= nc.sbuf_usable_end, (name, kb, n)
            return nc.alloc_sbuf_tensor_at(name, shape, dt, offset=base + int(kb * KB))

        def sem(name):
            return ctx.enter_context(nc.semaphore(name))

        raw = at("raw", [P, 4, KD, P], 0)
        w_hi = at("w_hi", [P, 4, KD, P], 16, F32R)
        w_lo = at("w_lo", [P, 4, KD, P], 32, F32R)
        xT = at("xT", [P, KD, S], 48)
        h_hi = at("h_hi", [P, KD, S], 64, F32R)
        h_lo = at("h_lo", [P, KD, S], 80, F32R)
        oa_hi = at("oa_hi", [P, KD, S], 96, F32R)
        oa_lo = at("oa_lo", [P, KD, S], 112, F32R)
        yc_hi = at("yc_hi", [P, KD, S], 128, F32R)
        yc_lo = at("yc_lo", [P, KD, S], 144, F32R)
        m_hi = at("m_hi", [P, KD, S], 160, F32R)
        m_lo = at("m_lo", [P, KD, S], 176, F32R)
        sq = at("sq", [P, KD, S], 96)
        x_tok = at("x_tok", [P, TT, D], 160)
        za = at("za", [P, KD, S], 112)
        v_tok = at("v_tok", [P, TT, GH * GDV], 128)
        kdT = at("kdT", [P, GH, S], 144)
        kd_tok = at("kd_tok", [P, TT, GH * GDK], 152)
        qT = at("qT", [P, GH, S], 160)
        kT = at("kT", [P, GH, S], 168)
        bT = at("bT", [P, GH, S], 176)
        ex = at("ex", [P, GH, S], 184)
        state = at("state", [P, GH, GDV], 176)
        scoresT = at("scoresT", [P, GH, P], 180)
        gla_mask = at("gla_mask", [P, GH, P], 182, I32)
        o_norm = at("o_norm", [P, GH * GDV], 184)
        maskf = at("maskf", [P, GH, P], 188)
        p_tok = at("p_tok", [P, TT, PLE], 112)
        pT_hi = at("pT_hi", [P, 2, S], 128, F32R)
        pT_lo = at("pT_lo", [P, 2, S], 132, F32R)
        hm_hi = at("hm_hi", [P, MH, S], 96, F32R)
        hm_lo = at("hm_lo", [P, MH, S], 104, F32R)
        hd_hi = at("hd_hi", [P, NH, S], 112, F32R)
        hd_lo = at("hd_lo", [P, NH, S], 120, F32R)
        mqkT = at("mqkT", [P, 2 * MH, S], 128)
        moT = at("moT", [P, MH, S], 144)
        dqT = at("dqT", [P, NH, S], 152)
        dkT = at("dkT", [P, NH, S], 160)
        d_tok = at("d_tok", [P, TT, NH * DDV], 168)
        m_tok = at("m_tok", [P, TT, MH, MD + 1], 176)
        gates = at("gates", [P, S], 184.25)
        rows = at("rows", [64, 4, S], 112)
        rowb = at("rowb", [64, S], 120)
        rowm = at("rowm", [64, S], 122)
        rowt = at("rowt", [64, S], 124)
        rowf = at("rowf", [64, S], 126)
        rstm = at("rstm", [64, S], 186.25)
        negm = at("negm", [64, S], 188.25)
        hsum = at("hsum", [P, MH, TT, MD], 0)
        ktok = at("ktok", [P, TT, MH * MD], 8)
        ni = at("ni", [P, TT, MD + 1], 16)
        nj = at("nj", [P, TT, MD + 1], 18.25)
        wv = at("wv", [P, TT, MD + 1], 20.5)
        cst = at("cst", [P, 2, TT, MD + 1], 22.75)
        arg = at("arg", [P, TT, P], 46)
        pt = at("pt", [P, TT, P], 27)
        wt = at("wt", [P, TT, P], 29)
        cols = at("cols", [P, TT, 4, 64], 96)
        selr = at("selr", [64, 8, P], 100)
        spb = at("spb", [P, 64, TT], 104)
        spd = at("spd", [64, 64, TT], 105)
        m01 = at("m01", [P, 2, P], 106)
        hn = at("hn", [P, 2, TT, MD], 40)
        msm = at("msm", [P, 512], 200.625)
        alibi = at("alibi", [P, S + 3 * P], 32)
        alih = at("alih", [P, S + 3 * P], 35.5)
        aa = at("aa", [P, 2, S], 20)
        pr = at("pr", [P, S], 44)
        es = at("es", [P, 2, 2, S], 24)
        aaT = at("aaT", [P, 2, TT, P], 16)
        od = at("od", [P, TT, DDV], 186.25)
        dsm = at("dsm", [P, 512], 188.25)
        lam_sb = at("lam_sb", [P, 4, DDH], 190.25)
        ring = at("ring", [P, RING, FF], 64)
        x2 = at("x2", [P, TT, D], 160)
        h2 = at("h2", [P, TT, D], 176)
        hid = at("hid", [P, 2, S], 0)
        hidT = at("hidT", [P, 2, 4, P], 4)
        sg = at("sg", [P, 2, S], 8)
        xe = at("xe", [P, KD, CAP], 12)
        pick = at("pick", [P, TT, CAP], 14)
        pickg = at("pickg", [P, TT, 2, CAP], 15)
        place = at("place", [P, S], 17)
        ye = at("ye", [P, S], 19)
        gbc = at("gbc", [P, D], 21)
        rw = at("rw", [P, KD, NE], 205.25)
        rwg = at("rwg", [P, KD, NE], 204.75)
        lg = at("lg", [P, TT, NE], 26)
        aff = at("aff", [P, TT, NE], 26.25)
        pos = at("pos", [P, TT, NE], 26.5)
        esm = at("esm", [P, 64], 26.75)
        aw = at("aw", [NE, S], 28)
        awm = at("awm", [NE, S], 30)
        awc = at("awc", [NE, S], 32)
        awo = at("awo", [NE, S], 34)
        iot = at("iot", [P, CAP], 36)
        ioti = at("ioti", [P, CAP], 36.5, I32)
        top8 = at("top8", [NE, 8], 37)
        fin = at("fin", [P, 2, D], 38)
        ident = at("ident", [P, P], 192)
        ones = at("ones", [P, P], 192.5)
        vec = at("vec", [P, 144], 193)
        eps = at("eps", [P, 1], 193.625)
        mgb = at("mgb", [P, 1], 193.75)
        sm = at("sm", [P, 64], 194)
        scr = [at(f"scr{n}", [P, S + 4], 194.5 + 2.03125 * n) for n in range(5)]

        mgw = at("mgw", [P, KD, P], 116)
        gk_sb = at("gk_sb", [RANK, S], 204.75)
        wgk = at("wgk", [RANK, GH * GDK], 152)
        vrow = at("vrow", [P, 2, P], 156)
        reset = at("reset", [P, S], 158)
        ps = ctx.enter_context(nc.psum_tensor("ps", [P, 8, S], F32))

        groups = [
            [("mix", norm_mix_g[0], 8), ("merge", b_merge[0], 16), ("bgk", b_gk[0], 4),
             ("gla", gla_norm_g[0], 2), ("conv", conv_w[0].rearrange("j c -> (j c)"), 24),
             ("ple", norm_ple_g[0], 8), ("final", norm_final_g, 8)],
            [("mix2", norm_mix_g_2[0], 8), ("conv2", conv_w_2[0].rearrange("j c -> (j c)"), 40),
             ("cb2", conv_b_2[0], 8), ("mnorm", mlstm_norm_g_2[0], 4),
             ("dnorm", diff_norm_g_2[0], 1), ("ffn", norm_ffn_g_2[0], 8)]]
        col, nrow, vec_loads = {}, [0, 0], []
        for g, members in enumerate(groups):
            for name, src, n in members:
                col[name] = 72 * g + nrow[g]
                vec_loads.append((g, nrow[g], n, src.rearrange("(r c) -> r c", c=P)))
                nrow[g] += n
        assert max(nrow) <= 72

        def vcol(name, k=0):
            return vec[:, col[name] + k:col[name] + k + 1]

        def columns(w, off, n=1024):
            return w[0][:, off:off + n].rearrange("(k p) (i c) -> p k i c", p=P, c=P)

        def tile(w, off, stride, j, n=1024):
            v = columns(w, off, n)
            return lambda i: (KD, v[:, :, i * stride + j, :])

        def short(w, k0, nk):
            v = w[0].rearrange("(k p) (i c) -> p k i c", p=P, c=P)
            return lambda i: (nk, v[:, k0:k0 + nk, i, :])

        w_gk_cols = w_in[0][:, OFF_GK:OFF_GK + RANK].rearrange("(k p) c -> p k c", p=P)
        proj_v = w_ple_proj[0].rearrange("(k p) (i c) -> p k i c", p=P, c=P)
        stages = [
            Stage("q", 1, [tile(w_in, OFF_Q, 4, j, 512) for j in range(4)]),
            Stage("k", 1, [tile(w_in, OFF_K, 4, j, 512) for j in range(4)]),
            Stage("gk", 1, [lambda i: (KD, w_gk_cols)]),
            Stage("v", 2, [tile(w_in, OFF_V, 4, j) for j in range(4)], "tok"),
            Stage("za", 2, [tile(w_in, OFF_ZA, 4, j) for j in range(4)]),
            Stage("conv", 8, [tile(w_in, o, 1, 0) for o in (OFF_XC, OFF_CC, OFF_CB, OFF_ZC)]),
            Stage("merge", 8, [tile(w_in, OFF_GA, 1, 0), tile(w_in, OFF_GC, 1, 0),
                               tile(w_branch_a, 0, 1, 0), tile(w_branch_c, 0, 1, 0)]),
            Stage("out", 2, [tile(w_out, 0, 4, j) for j in range(4)]),
            Stage("ple", 4, [tile(w_ple_gate, 0, 2, 0), lambda i: (2, proj_v[:, :, 2 * i, :]),
                             tile(w_ple_gate, 0, 2, 1), lambda i: (2, proj_v[:, :, 2 * i + 1, :])]),
            Stage("mqk", 2, [tile(w_in_2, OFF_MQ, 4, j) for j in range(4)]),
            Stage("mv", 1, [tile(w_in_2, OFF_MV, 4, j, 512) for j in range(4)], "tok"),
            Stage("mo", 1, [tile(w_in_2, OFF_MO, 4, j, 512) for j in range(4)]),
            Stage("mg", 1, [None]),
            Stage("dq", 1, [tile(w_in_2, OFF_DQ, 4, j, 512) for j in range(4)]),
            Stage("dk", 1, [tile(w_in_2, OFF_DK, 4, j, 512) for j in range(4)]),
            Stage("dv", 1, [tile(w_in_2, OFF_DV, 4, j, 512) for j in range(4)], "tok"),
            Stage("merge2", 8, [tile(w_in_2, OFF_G2, 1, 0), tile(w_in_2, OFF_G2 + D, 1, 0),
                                short(w_up_a_2, 0, 4), short(w_up_b_2, 0, 4)]),
            Stage("out2", 2, [tile(w_out_2, 0, 4, j) for j in range(4)]),
        ]
        uses = [0] * 4
        loads = [0] * 4
        for n, st in enumerate(stages):
            st.use, st.load = list(uses), list(loads)
            st.before = stages[n - 1] if n else None
            st.after = stages[n + 1] if n + 1 < len(stages) else None
            for j, src in enumerate(st.tiles):
                uses[j] += st.n
                loads[j] += st.n if src else 0
        by = {st.name: st for st in stages}
        HELD = ("merge2",)

        s_raw = [sem(f"raw_in{j}") for j in range(4)]
        s_hi = [sem(f"hi_split{j}") for j in range(4)]
        s_lo = [sem(f"lo_split{j}") for j in range(4)]
        s_mm = [sem(f"bank_done{j}") for j in range(4)]
        s_ev = [sem(f"bank_read{j}") for j in range(4)]
        s_small = sem("vectors_in")
        s_x = sem("x_in")
        s_p = sem("p_in")
        s_mg = sem("mg_in")
        s_gw = sem("gate_rank_in")
        s_out = sem("stored")

        def width(st):
            return RANK if st.name == "gk" else P

        def span(st, j, i):
            return KD if st.tiles[j] is None else st.tiles[j](0)[0]

        set_pool = Steps(sem("constants"), ["ident0", "ident", "ones", "mgb0", "vrow0", "reset1", "reset"])
        set_pe = Steps(sem("setup_pe"), ["vec0", "vec1"] + [f"x{k}" for k in range(KD)])
        set_dve = Steps(sem("setup_dve"), ["eps", "vec0", "vec1"] + [f"x{k}" for k in range(1, KD, 2)])
        set_act = Steps(sem("setup_act"), [f"x{k}" for k in range(0, KD, 2)])
        norms = ["mix", "ple", "final", "mix2"]
        n_act = {n: Steps(sem(f"norm_act_{n}"), [f"sq{k}" for k in range(KD)] + ["root"]
                          + ([f"hi{k}" for k in range(KD)] if n != "final" else [])) for n in norms}
        n_pe = {n: Steps(sem(f"norm_pe_{n}"), ["sum"]) for n in norms}
        n_dve = {n: Steps(sem(f"norm_dve_{n}"), ["rstd"] + [f"h{k}" for k in range(KD)]
                          + ([f"lo{k}" for k in range(KD)] if n != "final" else [])) for n in norms}
        for n in norms:
            if n != "final":
                order = ["rstd", "h0"]
                for k in range(KD):
                    order += ([f"h{k + 1}"] if k + 1 < KD else []) + [f"lo{k}"]
                n_dve[n] = Steps(n_dve[n].sem, order)
        gp_pe = Steps(sem("gate_pe"), [f"gk{h}" for h in range(GH)] + [f"kd{t}" for t in range(TT)])
        gp_act = Steps(sem("gate_act"), [f"abs{h}" for h in range(GH)] + [f"e{h}" for h in range(GH)] + [f"ln{h}" for h in range(GH)]
                       + ["eb", "ekd", "enb", "kd0", "kd1", "kd2", "kd3"])
        gp_dve = Steps(sem("gate_dve"), [f"min{h}" for h in range(GH)]
                       + [f"{a}{h}" for h in range(GH) for a in ("sum", "scan")]
                       + ["argkd", "kd", "qin", "decay", "kin", "zero", "zero2", "mask"])
        gp_pool = Steps(sem("gate_pool"), ["m0", "m1", "m2", "m3"])
        g_pe = Steps(sem("gla_pe"), ["a", "kvA0", "kvB0", "kvA1", "kvB1", "oT"])
        g_dve = Steps(sem("gla_dve"), ["at", "st00", "st01", "st02", "st03", "st10", "st11", "st12",
                                       "st13", "rstd", "t0", "t1", "lo0", "lo1"])
        g_act = Steps(sem("gla_act"), ["ss0", "ss1", "ss2", "ss3", "root", "on0", "on1", "on2", "on3",
                                       "hi0", "hi1"])
        cv_dve = Steps(sem("conv_dve"), ["c0", "c1", "c2", "y", "lo"])
        cv_act = Steps(sem("conv_act"), ["hi"])
        cv_pad = Steps(sem("conv_pad"), ["pad"])
        mg_dve = {1: Steps(sem("merge_dve"), ["m", "lo"]), 2: Steps(sem("merge2_dve"), ["m", "lo"])}
        mg_act = {1: Steps(sem("merge_act"), ["hi"]), 2: Steps(sem("merge2_act"), ["hi"])}
        out_dve = {1: Steps(sem("out_dve"), [f"x{j}" for j in range(4)]),
                   2: Steps(sem("out2_dve"), [f"x{j}" for j in range(4)])}
        p_pe = Steps(sem("p_pe"), ["p0", "p1"])
        p_act = Steps(sem("p_act"), ["hi0", "hi1"])
        p_dve = Steps(sem("p_dve"), ["lo0", "lo1"])
        pl_dve = Steps(sem("ple_dve"), ["xa", "xb"])
        mq_dve = Steps(sem("mqk_dve"), [f"c{n}" for n in range(5)])
        mq_act = Steps(sem("mqk_act"), ["silu"])
        mq_pad = Steps(sem("mqk_pad"), ["before0", "after0", "before1", "after1", "col"])
        mgz = Steps(sem("mg_zero"), ["w"])

        r_pool = Steps(sem("rows_pool"), ["r1", "r2", "r3", "n1", "n2", "n3", "m0", "mf", "mb"])
        r_dve = Steps(sem("rows_dve"), ["f", "lf", "bf", "bb", "c", "mf", "mb", "g0", "g1", "l0", "l1", "am",
                                        "mo0", "mo1", "mi", "mi0", "mi1", "s0", "s1", "gm", "mt", "a1", "a2",
                                        "a3", "nm", "sel0", "sel1", "spd"])
        r_act = Steps(sem("rows_act"), ["abs", "exp", "ln", "sp", "e1", "e2", "e3", "cols0", "cols1", "spb"])
        r_pe = Steps(sem("rows_pe"), ["cols", "spb"])
        kt_pe = Steps(sem("keys_pe"), [f"kt{c}" for c in range(TT)])
        kt_act = Steps(sem("keys_act"), ["scaled"] + [f"kt{c}" for c in range(TT)])
        WAYS = [(h, d) for h in range(MH) for d in range(2)]

        def in_turns(turns, count, *parts):
            names = []
            for k in range(turns):
                for tags, late, when in parts:
                    if 0 <= k - late < count and (when is None or when(k - late)):
                        names += [f"{tag}{k - late}" for tag in tags]
            return names

        NW = len(WAYS)
        LTURNS = NW + 2

        def forward(n):
            return WAYS[n][1] == 0

        def backward(n):
            return WAYS[n][1] == 1

        def kq_bank(n):
            return 2 if WAYS[n][0] % 2 else 5

        l_pe = Steps(sem("mlstm_pe"), ["kq0", "nm0", "kv0"] + in_turns(
            LTURNS, NW, (("kq",), -1, lambda n: n > 0 and forward(n)), (("nm", "kv"), -1, lambda n: n > 0),
            (("intra", "inter"), 1, None)))
        l_act = Steps(sem("mlstm_act"), in_turns(LTURNS, NW, (("pt",), 0, None), (("ni",), 1, None)))
        l_dve = Steps(sem("mlstm_dve"), ["wv0"] + in_turns(
            LTURNS, NW, (("arg", "msk", "z", "cs0_", "cs1_", "cs2_"), 0, None), (("wv",), -1, lambda n: n > 0),
            (("w",), 1, None), (("tmp", "num", "ab", "den", "rd", "h"), 2, None),
            (("hs", "bn0_", "bn1_", "bn2_", "bn3_"), 2, backward))
            + [f"ag{n}" for n in range(MH * TT)] + ["rstd"])
        f_act = Steps(sem("mlstm_out_act"), ["root"] + [f"hi{h}" for h in range(MH)])
        f_pe = Steps(sem("mlstm_out_pe"), [f"t{h}" for h in range(MH)])
        f_dve = Steps(sem("mlstm_out_dve"), in_turns(
            MH + 2, MH, (("t",), 2, None), (("n0_", "n1_", "n2_", "n3_"), 0, None), (("lo",), 2, None)))
        DW = [(h, q) for h in range(NH) for q in range(TT)]
        d_pool = Steps(sem("alibi_pool"), ["iota"])
        ND = len(DW)
        TURNS = ND + 4

        def starts(n):
            return n % TT == 0

        def ends(n):
            return 0 <= n < ND and n % TT == TT - 1

        d_pe = Steps(sem("diff_pe"), ["s0", "s1"] + in_turns(TURNS, ND, (("t",), 1, None), (("s",), -2, None), (("o",), 1, None),
                                                         (("oT",), 3, ends)))
        d_act = Steps(sem("diff_act"), ["lam0", "lam1"] + in_turns(TURNS, ND, 
            (("al",), 0, starts), (("e0_", "e1_"), 0, None), (("t",), 1, None),
            (("q0_", "q1_", "q2_", "q3_", "root", "o0_", "o1_", "o2_", "o3_"), 2, ends), (("hi",), 4, ends)))
        d_dve = Steps(sem("diff_dve"), ["abs", "lam0", "lam1", "lam2", "lam3", "gain"] + in_turns(TURNS, ND, 
            (("m0_", "m1_", "neg"), 0, None), (("rec", "rl", "p", "a"), 1, None), (("rstd",), 2, ends),
            (("lo",), 4, ends)))
        s_lam = sem("lambda_in")
        s_rw = sem("router_in")
        s_g = sem("gain_in")
        t_pe = Steps(sem("route_pe"), [f"x{t}" for t in range(TT)] + ["logits", "affT", "posT"])
        t_act = Steps(sem("route_act"), [f"x{t}" for t in range(TT)] + ["ss0", "ss1", "root", "exp"]
                      + [f"h{t}" for t in range(TT)])
        t_dve = Steps(sem("route_dve"), ["rwg"] + [f"x{t}" for t in range(TT)] + ["ss2", "ss3", "rstd", "lg", "mx", "sub", "sum", "rec", "aff", "aw"]
                      + [f"{a}{n}" for n in range(CAP // 8) for a in ("top", "rep")]
                      + ["one", "mask", "scan", "sel", "pos"])
        t_pool = Steps(sem("route_pool"), ["iota"] + [f"h{t}" for t in range(TT)])
        s_ring = [sem(f"ring_in{s}") for s in range(RING)]
        s_free = [sem(f"ring_used{s}") for s in range(RING)]
        x_pe = Steps(sem("gather_pe"), ["gather"])
        x_act = Steps(sem("gather_act"), ["xe"])
        x_dve = Steps(sem("gather_dve"), ["pick"])
        e_pe = Steps(sem("expert_pe"), ["hT", "place", "o0", "o1", "o2", "o3"])
        e_act = Steps(sem("expert_act"), ["s0", "s1", "hT0", "ye", "place"])
        e_dve = Steps(sem("expert_dve"), ["pg0", "pg1", "hid0", "hid1", "hT1", "o0", "o1", "o2", "o3"])
        z_act = Steps(sem("final_act"), [f"ss{t}" for t in range(TT)] + ["root"])
        z_dve = Steps(sem("final_dve"), ["rstd"] + [f"y{t}" for t in range(TT)])
        s_store = [sem(f"stored{t}") for t in range(2)]

        def rings_rest(eng):
            eng.wait_ge(s_mm[3], by["dv"].use[3] + 1)

        def small(n, at, width):
            c = 12 + n % 2 * 12 + at
            return dsm[:, c:c + width]

        def state_chunks(d):
            return list(range(TT)) if d == 0 else list(range(TT))[::-1]

        def mrow(h, d):
            return 32 * d + h

        def pairs(b):
            return ps[:, b:b + 2, 0:2 * (MD + 1)].rearrange("p b (c v) -> p b c v", v=MD + 1)

        def paired(t):
            return t[:, :, :].rearrange("p (b c) v -> p b c v", b=2)

        def over(ap, shape):
            return ap.to_broadcast(shape)

        gate_v = w_gate_e_2[0].rearrange("e (k p) f -> p e k f", p=P)
        up_v = w_up_e_2[0].rearrange("e (k p) f -> p e k f", p=P)
        down_v = w_down_e_2[0].rearrange("e (c j p) d -> p e c j d", p=P, j=2)
        PER = 24

        def used(eng, e, n):
            eng.wait_ge(s_free[n % RING], e * 2 + (n // RING + 1))



        def source(st, j, nk, w):
            return mgw[:, :, :] if st.tiles[j] is None else raw[:, j, 0:nk, 0:w]

        def free_slot(eng, st, j, i):
            if st.use[j] == 0 and isinstance(i, int) and i == 0:
                return
            eng.wait_ge(s_mm[j], st.use[j] + i)
            before = st if not (isinstance(i, int) and i == 0) else st.before
            if before.kind == "tok":
                last = before.use[3] + before.n if before is not st else st.use[3] + i
                eng.wait_ge(s_mm[3], last)

        def run_stage(eng, st, split, evac, look, then):
            def body(nxt, ni, i):
                for j in range(4):
                    if nxt is not None and j < len(nxt.tiles):
                        split(nxt, j, ni)
                    if j < len(st.tiles):
                        evac(st, j, i)
            if st.n > 2:
                with eng.Fori(0, st.n - 1) as i:
                    body(st, i + 1, i)
            else:
                for i in range(st.n - 1):
                    body(st, i + 1, i)
                    if i in then:
                        then[i]()
            body(st.after if look else None, 0, st.n - 1)
            if st.n - 1 in then:
                then[st.n - 1]()

        def norm_input(eng, n, k):
            if n == "mix":
                (set_dve if k % 2 else set_act).wait(eng, f"x{k}")
            elif n == "ple":
                st = by["out"]
                eng.wait_ge(s_ev[k % 4], st.use[k % 4] + k // 4 + 1)
            elif n == "final":
                pl_dve.wait(eng, "xb" if k % 2 else "xa", k // 2)
            else:
                n_dve["final"].wait(eng, f"h{k}")

        def tiles4(ap):
            return ap[:, 0:S].rearrange("p (h t) -> p h t", t=P)

        def by_parity(t, r):
            return t[:, :, :].rearrange("p (h r) s -> p h r s", r=2)[:, :, r, :]

        def ds1(base, i):
            return bass.ds(i + base, 1)

        block = ctx.enter_context(nc.Block())

        @block.sync
        def _(sp):
            for t in range(TT):
                sp.dma_start(x_tok[:, t, :], x[0, t * P:(t + 1) * P, :]).then_inc(s_x, 16)

            def load(st, j, i, first=False):
                if st.tiles[j] is None:
                    return
                nk, src = st.tiles[j](i)
                dst = raw[:, j, 0:nk, 0:width(st)]
                if isinstance(i, int):
                    if st.use[j] + i:
                        sp.wait_ge(s_lo[j], st.use[j] + i)
                    sp.dma_start(dst, src).then_inc(s_raw[j], 16)
                else:
                    free = sp.lower_val(i + st.use[j])
                    sp.dma_start(dst, src).wait_op(s_lo[j], free, "sem-ge").then_inc(s_raw[j], 16)

            def load_stage(name):
                st = by[name]
                if st.n <= 2:
                    for i in range(st.n):
                        for j in range(len(st.tiles)):
                            load(st, j, i)
                else:
                    with sp.Fori(1, st.n + 1) as n:
                        for j in range(len(st.tiles)):
                            load(st, j, n - 1)

            for name in ("q", "k", "gk", "v", "za", "conv", "merge", "out"):
                load_stage(name)
            mg_dve[1].wait(sp, "lo", 7)
            sp.dma_start(p_tok[:, :, :], p[0, 0].rearrange("(t p) c -> p t c", p=P)).then_inc(s_p, 16)
            mgz.wait(sp, "w")
            for n, c in enumerate((0, 32, 64, 96)):
                src = OFF_MG + (0, 8, 4, 12)[n]
                sp.dma_start(mgw[:, :, c:c + 4],
                             w_in_2[0][:, src:src + 4].rearrange("(k p) c -> p k c", p=P)).then_inc(s_mg, 16)
            for name in ("ple", "mqk", "mv", "mo", "dq", "dk", "dv"):
                load_stage(name)
            s_mm_out = by["out"].use[3] + by["out"].n
            sp.wait_ge(s_mm[3], s_mm_out)
            sp.dma_start(lam_sb[:, :, :], diff_lam_2[0].rearrange("a c -> (a c)").partition_broadcast(P)).then_inc(s_lam, 16)
            sp.dma_start(rw[:, :, :], w_router_2[0].rearrange("(k p) e -> p k e", p=P)).then_inc(s_rw, 16)
            f_dve.wait(sp, "lo3")
            load_stage("merge2")
            load_stage("out2")
            mg_dve[2].wait(sp, "lo", 7)

            def load_expert(e, first=0, last=PER):
                for n in range(first, last):
                    s, use = n % RING, e * 2 + n // RING
                    src = gate_v[:, e, n, :] if n < 8 else up_v[:, e, n - 8, :] if n < 16 else down_v[:, e, n - 16, :, :]
                    dst = ring[:, s, :] if n < 16 else ring[:, s, :].rearrange("p (j d) -> p j d", j=2)
                    if isinstance(e, int):
                        if use:
                            sp.wait_ge(s_free[s], use)
                        sp.dma_start(dst, src).then_inc(s_ring[s], 16)
                    else:
                        turn = sp.lower_val(use)
                        sp.dma_start(dst, src).wait_op(s_free[s], turn, "sem-ge").then_inc(s_ring[s], 16)

            load_expert(0, last=RING)
            for b in range(4):
                sp.wait_ge(s_mm[b], by["out2"].use[b] + 2)
            sp.dma_start(gbc[:, :], norm_ffn_g_2[0].partition_broadcast(P)).then_inc(s_g, 16)
            load_expert(0, first=RING)
            with sp.Fori(1, NE) as e:
                load_expert(e)
            sp.dma_start(gbc[:, :], norm_f_g_2.partition_broadcast(P)).then_inc(s_g, 16)
            for t in range(TT):
                z_dve.wait(sp, f"y{t}")
                sp.dma_start(out[0, t * P:(t + 1) * P, :], fin[:, t % 2, :]).then_inc(s_store[t % 2], 16)
            for t in range(2):
                sp.wait_ge(s_store[t], 32)

        @block.gpsimd
        def _(pool):
            set_pool.done(pool.memset(ident[:, :], 0.0), "ident0")
            set_pool.wait(pool, "ident0")
            set_pool.done(pool.affine_select(out=ident[:, :], in_=ident[:, :], compare_op=ALU.not_equal,
                                             fill=1.0, base=0, pattern=[[-1, P]], channel_multiplier=1),
                          "ident")
            set_pool.done(pool.memset(ones[:, :], 1.0), "ones")
            set_pool.done(pool.memset(mgb[:, :], 0.0), "mgb0")
            set_pool.done(pool.memset(vrow[:, :, :], 0.0), "vrow0")
            set_pool.done(pool.memset(reset[:, :], 1.0), "reset1")
            set_pool.wait(pool, "reset1")
            set_pool.done(pool.memset(reset[:, 0:S:GCH], 0.0), "reset")
            gp_dve.wait(pool, "kin")
            gp_pool.done(pool.memset(maskf[:, :, :], 1.0), "m0")
            gp_pool.wait(pool, "m0")
            gp_pool.done(pool.affine_select(out=maskf[:, :, :], in_=maskf[:, :, :], compare_op=ALU.is_ge,
                                            fill=0.0, base=0, pattern=[[0, GH], [1, P]],
                                            channel_multiplier=-1), "m1")
            gp_pool.wait(pool, "m1")
            gp_pool.done(pool.memset(maskf[0:GCH, :, GCH:P], 0.0), "m2")
            mg_dve[1].wait(pool, "lo", 7)
            mgz.done(pool.memset(mgw[:, :, :], 0.0), "w")
            for b in range(4):
                pool.wait_ge(s_mm[b], by["out"].use[b] + 2)
            r_pool.done(pool.memset(rstm[:, :], 1.0), "r1")
            r_pool.wait(pool, "r1")
            r_pool.done(pool.memset(rstm[0:32, 0:S:P], 0.0), "r2")
            r_pool.wait(pool, "r2")
            r_pool.done(pool.memset(rstm[32:64, P - 1:S:P], 0.0), "r3")
            r_pool.wait(pool, "r3")
            r_pool.done(pool.memset(negm[:, :], 0.0), "n1")
            r_pool.wait(pool, "n1")
            r_pool.done(pool.memset(negm[0:32, 0:S:P], -BIG), "n2")
            r_pool.wait(pool, "n2")
            r_pool.done(pool.memset(negm[32:64, P - 1:S:P], -BIG), "n3")
            r_pool.wait(pool, "n3")
            n_pe["mix2"].wait(pool, "sum")
            r_pool.done(pool.memset(m01[:, :, :], 0.0), "m0")
            r_pool.wait(pool, "m0")
            for d, name in ((0, "mf"), (1, "mb")):
                sign = 1 - 2 * d
                r_pool.done(pool.affine_select(out=m01[:, d, :], in_=m01[:, d, :], compare_op=ALU.is_ge, fill=-1e30,
                                               base=0, pattern=[[sign, P]], channel_multiplier=-sign), name)
                r_pool.wait(pool, name)
            rings_rest(pool)
            d_pool.done(pool.iota(alibi[:, :], pattern=[[-1, S + 3 * P]], base=3 * P, channel_multiplier=1,
                                  allow_small_or_imprecise_dtypes=True), "iota")
            for b in range(4):
                pool.wait_ge(s_mm[b], by["out2"].use[b] + 2)
            t_pool.done(pool.iota(iot[:, :], pattern=[[1, CAP]], base=1, channel_multiplier=0,
                                  allow_small_or_imprecise_dtypes=True), "iota")
            pool.wait_ge(s_g, 16)
            for t in range(TT):
                t_act.wait(pool, f"h{t}")
                t_pool.done(pool.tensor_tensor(h2[:, t, :], h2[:, t, :], gbc[:, :], ALU.mult), f"h{t}")

        @block.scalar
        def _(act):
            set_pool.wait(act, "vrow0")
            for g, r, n, src in vec_loads:
                act.dma_start(vrow[r:r + n, g, :], src).then_inc(s_small, 16)
            for n, r in enumerate((0, 32, 64, 96)):
                src = (0, 8, 4, 12)[n]
                act.dma_start(mgb[r:r + 4, :], b_mgate_2[0, src:src + 4].rearrange("(a b) -> a b", b=1))\
                   .then_inc(s_small, 16)
            act.dma_start(wgk[:, :], w_gk2[0]).then_inc(s_gw, 16)

            def split(st, j, i):
                nk, w = span(st, j, i), width(st)
                if st.tiles[j] is None:
                    act.wait_ge(s_mg, 64)
                else:
                    act.wait_ge(s_raw[j], (st.load[j] + i + 1) * 16)
                free_slot(act, st, j, i)
                act.activation(w_hi[:, j, 0:nk, 0:w], source(st, j, nk, w), ACT.Copy).then_inc(s_hi[j], 1)

            def setup():
                for k in range(0, KD, 2):
                    set_pe.wait(act, f"x{k}")
                    set_act.done(act.activation(xT[:, k, :], ps[:, k, :], ACT.Copy), f"x{k}")

            def norm(n):
                s = n_act[n]
                for k in range(KD):
                    norm_input(act, n, k)
                    s.done(act.activation(sq[:, k, :], xT[:, k, :], ACT.Square), f"sq{k}")
                n_pe[n].wait(act, "sum")
                if n == "mix":
                    set_dve.wait(act, "eps")
                s.done(act.activation(scr[0][:, 0:S], ps[:, 4, :], ACT.Sqrt, bias=eps[:, :], scale=1.0 / D), "root")
                if n != "final":
                    for k in range(KD):
                        n_dve[n].wait(act, f"h{k}")
                        s.done(act.activation(h_hi[:, k, :], scr[2 + k % 2][:, 0:S], ACT.Copy), f"hi{k}")

            def run(name, evac, look=True, then={}):
                run_stage(act, by[name], split, evac, look, then)

            def read(st, j, i, out, func, **kw):
                act.wait_ge(s_mm[j], st.use[j] + i + 1)
                act.activation(out, ps[:, j, :], func, **kw).then_inc(s_ev[j], 1)

            setup()
            for j in range(4):
                split(by["q"], j, 0)
            norm("mix")
            run("q", lambda st, j, i: read(st, j, i, qT[:, j, :], ACT.Copy, scale=GDK ** -0.5))
            run("k", lambda st, j, i: read(st, j, i, kT[:, j, :], ACT.Copy))

            def read_gk(st, j, i):
                act.wait_ge(s_mm[0], st.use[0] + 1)
                act.activation(gk_sb[:, :], ps[0:RANK, 0, :], ACT.Copy).then_inc(s_ev[0], 1)

            run("gk", read_gk)
            def log_gates():
                for h in range(GH):
                    gp_pe.wait(act, f"gk{h}")
                    gp_act.done(act.activation(ex[:, h, :], ps[:, 4 + h, :], ACT.Abs, bias=vcol("bgk", h)), f"abs{h}")
                for h in range(GH):
                    gp_act.wait(act, f"abs{h}")
                    gp_act.done(act.activation(ex[:, h, :], ex[:, h, :], ACT.Exp, scale=-1.0), f"e{h}")
                for h in range(GH):
                    gp_act.wait(act, f"e{h}")
                    gp_act.done(act.activation(ex[:, h, :], ex[:, h, :], ACT.Ln, bias=1.0), f"ln{h}")

            def decays():
                gp_dve.wait(act, "scan3")
                gp_act.done(act.activation(ex[:, :, :], bT[:, :, :], ACT.Exp, scale=1 / GATE_NORM), "eb")
                gp_dve.wait(act, "argkd")
                gp_act.done(act.activation(kdT[:, :, :], kdT[:, :, :], ACT.Exp, scale=1 / GATE_NORM), "ekd")
                gp_dve.wait(act, "decay")
                gp_act.done(act.activation(ex[:, :, :], bT[:, :, :], ACT.Exp, scale=-1 / GATE_NORM), "enb")

            run("v", lambda st, j, i: read(st, j, i, v_tok[:, j, i * S:(i + 1) * S], ACT.Copy), then={0: log_gates, 1: decays})
            run("za", lambda st, j, i: read(st, j, i, za[:, 4 * i + j, :], ACT.Silu))
            for t in range(TT):
                gp_pe.wait(act, f"kd{t}")
                gp_act.done(act.activation(kd_tok[:, t, :], ps[:, 4 + t, :], ACT.Copy), f"kd{t}")
            for i in range(TT):
                g_pe.wait(act, "kvB1", i)
                for h in range(GH):
                    g_act.done(act.activation(scr[h // 2 * 3][:, h % 2 * GDV:(h % 2 + 1) * GDV], ps[:, 5 + h // 2, h % 2 * GDV:(h % 2 + 1) * GDV],
                                              ACT.Square, accum_out=sm[:, 32 + h:33 + h]), f"ss{h}")
                g_act.wait(act, "ss3", i)
                g_act.done(act.activation(sm[:, 36:40], sm[:, 32:36], ACT.Sqrt, bias=eps[:, :], scale=1 / GDV), "root")
                g_dve.wait(act, "rstd", i)
                for h in range(GH):
                    g_act.done(act.activation(o_norm[:, h * GDV:(h + 1) * GDV],
                                              ps[:, 5 + h // 2, h % 2 * GDV:(h % 2 + 1) * GDV],
                                              ACT.Copy, scale=sm[:, 40 + h:41 + h]), f"on{h}")
                for r in range(2):
                    g_dve.wait(act, f"t{r}", i)
                    g_act.done(act.activation(by_parity(oa_hi, r)[:, :, i * P:(i + 1) * P], tiles4(scr[1 + r]),
                                              ACT.Copy), f"hi{r}")

            def conv(st, j, i):
                if j == 0:
                    act.wait_ge(s_ev[1], st.use[1] + i)
                    read(st, 0, i, scr[0][:, 0:S], ACT.Copy)
                elif j == 3:
                    read(st, 3, i, scr[3][:, 0:S], ACT.Silu)
                    cv_dve.wait(act, "y", i)
                    cv_act.done(act.activation(yc_hi[:, i, :], scr[4][:, 0:S], ACT.Copy), "hi")

            run("conv", conv)

            def merge(which):
                hi = m_hi

                def evac(st, j, i):
                    if j < 2:
                        bias = {"bias": vec[:, ds1(col["merge"] + 8 * j, i)]} if which == 1 else {}
                        read(st, j, i, scr[j][:, 0:S], ACT.Sigmoid, **bias)
                    elif j == 3:
                        mg_dve[which].wait(act, "m", i)
                        mg_act[which].done(act.activation(hi[:, i, :], scr[3][:, 0:S], ACT.Copy), "hi")
                return evac

            run("merge", merge(1))
            run("out", lambda st, j, i: None)
            for k in range(2):
                p_pe.wait(act, f"p{k}")
                p_act.done(act.activation(pT_hi[:, k, :], ps[:, 5 + k, :], ACT.Copy), f"hi{k}")
            norm("ple")

            def ple(st, j, i):
                if j % 2 == 0:
                    act.wait_ge(s_ev[j + 1], st.use[j + 1] + i)
                    read(st, j, i, scr[j][:, 0:S], ACT.Sigmoid)

            run("ple", ple)
            norm("final")
            norm("mix2")

            def mqk(st, j, i):
                n = 4 * i + j
                if n >= 2:
                    mq_dve.wait(act, "c4", n - 2)
                read(st, j, i, scr[n % 2 * 4][:, 2:S + 2], ACT.Copy)
                if n:
                    convolved(n - 1)

            def convolved(n):
                mq_dve.wait(act, "c4", n)
                mq_act.done(act.activation(mqkT[:, n, :], scr[1 + n % 2][:, 0:S], ACT.Silu, bias=vcol("cb2", n)), "silu")

            run("mqk", mqk, then={1: lambda: convolved(7)})
            run("mv", lambda st, j, i: read(st, j, i, m_tok[:, j, :, 0:MD], ACT.Copy))
            run("mo", lambda st, j, i: read(st, j, i, moT[:, j, :], ACT.Sigmoid))
            run("mg", lambda st, j, i: read(st, j, i, gates[:, :], ACT.Identity, bias=mgb[:, :]))
            def gate_logs():
                r_dve.wait(act, "f")
                r_act.done(act.activation(rowt[:, :], rowf[:, :], ACT.Abs), "abs")
                r_act.wait(act, "abs")
                r_act.done(act.activation(rowt[:, :], rowt[:, :], ACT.Exp, scale=-1.0), "exp")
                r_act.wait(act, "exp")
                r_act.done(act.activation(rowt[:, :], rowt[:, :], ACT.Ln, bias=1.0), "ln")

            def gate_rows():
                mq_act.wait(act, "silu", 7)
                kt_act.done(act.activation(mqkT[:, MH:2 * MH, :], mqkT[:, MH:2 * MH, :], ACT.Copy, scale=MD ** -0.5), "scaled")
                r_dve.wait(act, "s1")
                r_act.done(act.activation(msm[0:64, 20:24], msm[0:64, 20:24], ACT.Exp), "sp")
                for n, scale in ((1, 1.0), (2, -1.0), (3, 1.0)):
                    r_dve.wait(act, f"a{n}")
                    r_act.done(act.activation(rows[:, n, :], rows[:, n, :], ACT.Exp, scale=scale), f"e{n}")

            run("dq", lambda st, j, i: read(st, j, i, dqT[:, j, :], ACT.Copy), then={0: gate_logs})
            run("dk", lambda st, j, i: read(st, j, i, dkT[:, j, :], ACT.Copy), then={0: gate_rows})
            run("dv", lambda st, j, i: read(st, j, i, d_tok[:, j, :], ACT.Copy), look=False)
            for c in range(TT):
                kt_pe.wait(act, f"kt{c}")
                kt_act.done(act.activation(ktok[:, c, :], ps[:, c, :], ACT.Copy), f"kt{c}")
            r_pe.wait(act, "cols")
            for b in range(2):
                r_act.done(act.activation(cols[:, 2 * b:2 * b + 2, :, :], ps[:, 4 + b, :], ACT.Copy), f"cols{b}")
            r_pe.wait(act, "spb")
            r_act.done(act.activation(spb[:, :, :], ps[:, 6, 0:256], ACT.Copy), "spb")
            for k in range(LTURNS):
                if k < NW:
                    l_dve.wait(act, f"msk{k}")
                    if k:
                        l_dve.wait(act, f"w{k - 1}")
                    l_act.done(act.activation(pt[:, :, :], arg[:, :, :], ACT.Exp), f"pt{k}")
                if 0 <= k - 1 < NW:
                    n = k - 1
                    l_pe.wait(act, f"intra{n}")
                    if n:
                        l_dve.wait(act, f"num{n - 1}")
                    l_act.done(act.activation(paired(ni), pairs(6), ACT.Copy), f"ni{n}")
            d_dve.wait(act, "lam1")
            d_act.done(act.activation(dsm[:, 2:3], dsm[:, 0:1], ACT.Exp), "lam0")
            d_act.done(act.activation(dsm[:, 3:4], dsm[:, 1:2], ACT.Exp), "lam1")
            d_dve.wait(act, "abs")
            l_dve.wait(act, "ag15")
            f_act.done(act.activation(msm[:, 240:256], msm[:, 200:232].rearrange("p (n a) -> p n a", a=2)[:, :, 1],
                                      ACT.Sqrt, bias=eps[:, :]), "root")
            for h in range(MH):
                f_dve.wait(act, f"t{h}")
                f_act.done(act.activation(hm_hi[:, h, :], scr[1 + h % 2][:, 0:S], ACT.Copy), f"hi{h}")

            for k in range(TURNS):
                if k < ND:
                    n, (h, q) = k, DW[k]
                    if q == 0:
                        if n:
                            d_dve.wait(act, f"m1_{n - 1}")
                        d_act.done(act.activation(alih[:, :], alibi[:, :], ACT.Copy,
                                                  scale=-(2.0 ** (-8 * (h + 1) / NH)) * DDH ** 0.5), f"al{n}")
                    d_dve.wait(act, f"neg{n}")
                    for i in range(2):
                        d_act.done(act.activation(es[:, n % 2, i, :], es[:, n % 2, i, :], ACT.Exp, bias=small(n, 2 + i, 1),
                                                  accum_out=small(n, 4 + i, 1)), f"e{i}_{n}")
                if 0 <= k - 1 < ND:
                    n = k - 1
                    d_pe.wait(act, f"t{n}")
                    if n >= 2:
                        d_pe.wait(act, f"o{n - 2}")
                    d_act.done(act.activation(aaT[:, n % 2, :, :], ps[:, 4, :], ACT.Copy), f"t{n}")
                if k - 2 == ND - 1:
                    d_pe.wait(act, f"o{ND - 1}")
                    for j in range(4):
                        split(by["merge2"], j, 0)
                if ends(k - 2):
                    n, h = k - 2, DW[k - 2][0]
                    d_pe.wait(act, f"o{n}")
                    for c in range(TT):
                        d_act.done(act.activation(scr[0][:, c * P:(c + 1) * P], ps[:, 5 + h % 2, c * P:(c + 1) * P],
                                                  ACT.Square, accum_out=dsm[:, 40 + c:41 + c]), f"q{c}_{n}")
                    d_act.wait(act, f"q3_{n}")
                    d_act.done(act.activation(dsm[:, 44:48], dsm[:, 40:44], ACT.Sqrt, bias=eps[:, :], scale=1 / DDV), f"root{n}")
                    d_dve.wait(act, f"rstd{n}")
                    for c in range(TT):
                        d_act.done(act.activation(od[:, c, :], ps[:, 5 + h % 2, c * P:(c + 1) * P], ACT.Copy,
                                                  scale=dsm[:, 48 + c:49 + c]), f"o{c}_{n}")
                if ends(k - 4):
                    n, h = k - 4, DW[k - 4][0]
                    d_pe.wait(act, f"oT{n}")
                    d_act.done(act.activation(hd_hi[:, h, :], ps[:, 7, :], ACT.Copy, scale=dsm[:, 8:9]), f"hi{n}")

            run("merge2", merge(2))
            run("out2", lambda st, j, i: None)

            for t in range(TT):
                t_pe.wait(act, f"x{t}")
                t_act.done(act.activation(x2[:, t, 0:S], ps[:, 2 * t, :], ACT.Copy), f"x{t}")
            for t in range(2):
                t_dve.wait(act, f"x{t}")
                t_act.wait(act, f"x{t}")
                t_act.done(act.activation(h2[:, t, :], x2[:, t, :], ACT.Square, accum_out=esm[:, t:t + 1]), f"ss{t}")
            t_act.wait(act, "ss1")
            t_dve.wait(act, "ss3")
            t_act.done(act.activation(esm[:, 4:8], esm[:, 0:4], ACT.Sqrt, bias=eps[:, :], scale=1 / D), "root")
            t_dve.wait(act, "sub")
            t_act.done(act.activation(lg[:, :, :], lg[:, :, :], ACT.Exp), "exp")
            for t in range(TT):
                t_act.done(act.activation(h2[:, t, :], x2[:, t, :], ACT.Copy, scale=esm[:, 8 + t:9 + t]), f"h{t}")

            def gathered(e):
                x_pe.wait(act, "gather", e)
                x_act.done(act.activation(xe[:, :, :], ps[:, 7, :], ACT.Copy), "xe")

            def expert(e, more=True):
                used(act, e, 7)
                for q in range(2):
                    e_act.done(act.activation(sg[:, q, :], ps[:, q, :], ACT.Silu), f"s{q}")
                if more:
                    gathered(e + 1)
                e_pe.wait(act, "hT", e)
                e_act.done(act.activation(hidT[:, 0, :, :], ps[:, 5, :], ACT.Copy), "hT0")
                used(act, e, 23)
                e_act.done(act.activation(ye[:, :], ps[:, 4, :], ACT.Copy), "ye")
                e_pe.wait(act, "place", e)
                e_act.done(act.activation(place[:, :], ps[:, 7, :], ACT.Copy), "place")

            gathered(0)
            with act.Fori(0, NE - 1) as e:
                expert(e)
            expert(NE - 1, more=False)
            for t in range(TT):
                e_dve.wait(act, f"o{t}", NE - 1)
                z_act.done(act.activation(h2[:, t, :], x2[:, t, :], ACT.Square, accum_out=esm[:, 16 + t:17 + t]), f"ss{t}")
            z_act.wait(act, "ss3")
            z_act.done(act.activation(esm[:, 20:24], esm[:, 16:20], ACT.Sqrt, bias=eps[:, :], scale=1 / D), "root")

        @block.vector
        def _(dve):
            def split(st, j, i):
                nk, w = span(st, j, i), width(st)
                dve.wait_ge(s_hi[j], st.use[j] + i + 1)
                dve.tensor_tensor(w_lo[:, j, 0:nk, 0:w], source(st, j, nk, w),
                                  w_hi[:, j, 0:nk, 0:w].bitcast(F32), ALU.subtract).then_inc(s_lo[j], 1)

            def run(name, evac, look=True, then={}):
                run_stage(dve, by[name], split, evac, look, then)

            def norm(n):
                s = n_dve[n]
                n_act[n].wait(dve, "root")
                s.done(dve.reciprocal(scr[1][:, 0:S], scr[0][:, 0:S]), "rstd")
                s.wait(dve, "rstd")

                def part(k):
                    if n != "final" and k >= 2:
                        s.wait(dve, f"lo{k - 2}")
                    if n == "final":
                        s.done(dve.scalar_tensor_tensor(out=xT[:, k, :], in0=xT[:, k, :], scalar=vcol(n, k),
                                                        in1=scr[1][:, 0:S], op0=ALU.mult, op1=ALU.mult), f"h{k}")
                        return
                    s.done(dve.scalar_tensor_tensor(out=scr[2 + k % 2][:, 0:S], in0=xT[:, k, :], scalar=vcol(n, k),
                                                    in1=scr[1][:, 0:S], op0=ALU.mult, op1=ALU.mult), f"h{k}")

                def low(k):
                    n_act[n].wait(dve, f"hi{k}")
                    s.done(dve.tensor_tensor(h_lo[:, k, :], scr[2 + k % 2][:, 0:S], h_hi[:, k, :].bitcast(F32),
                                             ALU.subtract), f"lo{k}")

                part(0)
                for k in range(KD):
                    if k + 1 < KD:
                        part(k + 1)
                    if n != "final":
                        low(k)

            def nothing(st, j, i):
                return None

            set_dve.done(dve.memset(eps[:, :], EPS), "eps")
            set_pe.wait(dve, "vec0")
            set_dve.done(dve.tensor_copy(vec[:, 0:72], ps[:, 0, 0:72]), "vec0")
            set_pe.wait(dve, "vec1")
            set_dve.done(dve.tensor_copy(vec[:, 72:144], ps[:, 1, 0:72]), "vec1")
            for k in range(1, KD, 2):
                set_pe.wait(dve, f"x{k}")
                set_dve.done(dve.tensor_copy(xT[:, k, :], ps[:, k, :]), f"x{k}")
            for j in range(4):
                split(by["q"], j, 0)
            set_dve.wait(dve, "vec1")
            norm("mix")
            for name in ("q", "k", "gk"):
                run(name, nothing)

            def log_gates():
                for h in range(GH):
                    gp_act.wait(dve, f"abs{h}")
                    gp_dve.done(dve.tensor_scalar(bT[:, h, :], ps[:, 4 + h, :], vcol("bgk", h), 0.0, ALU.add, ALU.min), f"min{h}")
                set_pool.wait(dve, "reset")
                for h in range(GH):
                    gp_act.wait(dve, f"ln{h}")
                    gp_dve.wait(dve, f"min{h}")
                    gp_dve.done(dve.tensor_tensor(ex[:, h, :], bT[:, h, :], ex[:, h, :], ALU.subtract), f"sum{h}")
                    gp_dve.wait(dve, f"sum{h}")
                    gp_dve.done(dve.tensor_tensor_scan(bT[:, h, :], reset[:, :], ex[:, h, :], 0.0, ALU.mult, ALU.add), f"scan{h}")

            def decays():
                gp_dve.wait(dve, "scan3")
                chunks = bT[:, :, :].rearrange("p h (n c) -> p (h n) c", c=GCH)
                last = chunks[:, :, GCH - 1:GCH].to_broadcast([P, GH * S // GCH, GCH])
                gp_dve.done(dve.tensor_tensor(kdT[:, :, :].rearrange("p h (n c) -> p (h n) c", c=GCH), last, chunks,
                                              ALU.subtract), "argkd")
                gp_act.wait(dve, "ekd")
                gp_dve.done(dve.tensor_tensor(kdT[:, :, :], kdT[:, :, :], kT[:, :, :], ALU.mult), "kd")
                gp_dve.done(dve.tensor_tensor(qT[:, :, :], qT[:, :, :], ex[:, :, :], ALU.mult), "qin")
                gp_dve.done(dve.tensor_copy(sm[:, 0:32], ex[:, :, :].rearrange("p h (n c) -> p (h n) c", c=GCH)[:, :, GCH - 1]), "decay")
                gp_act.wait(dve, "enb")
                gp_dve.done(dve.tensor_tensor(kT[:, :, :], kT[:, :, :], ex[:, :, :], ALU.mult), "kin")
                gp_dve.wait(dve, "kin")
                gp_dve.done(dve.memset(state[:, :, :], 0.0), "zero")
                gp_dve.done(dve.memset(scoresT[:, :, :], 0.0), "zero2")
                gp_pool.wait(dve, "m2")
                gp_dve.done(dve.tensor_copy(gla_mask[:, :, :], maskf[:, :, :]), "mask")

            run("v", nothing, then={0: log_gates, 1: decays})
            run("za", nothing)
            gp_dve.wait(dve, "mask")
            for i in range(TT):
                g_pe.wait(dve, "a", i)
                g_dve.done(dve.copy_predicated(scoresT[:, :, :], gla_mask[:, :, :], tiles4(ps[:, 4, :])), "at")
                for c in range(2):
                    for h in range(GH):
                        if h % 2 == 0:
                            g_pe.wait(dve, f"kv{'AB'[h // 2]}{c}", i)
                        n = h * (S // GCH) + 2 * i + c
                        g_dve.done(dve.scalar_tensor_tensor(
                            out=state[:, h, :], in0=state[:, h, :], scalar=sm[:, n:n + 1],
                            in1=ps[:, 7 if h < 2 else 4, h % 2 * GDV:(h % 2 + 1) * GDV],
                            op0=ALU.mult, op1=ALU.add), f"st{c}{h}")
                    g_dve.wait(dve, f"st{c}3", i)
                g_act.wait(dve, "root", i)
                g_dve.done(dve.reciprocal(sm[:, 40:44], sm[:, 36:40]), "rstd")
                g_pe.wait(dve, "oT", i)
                for r in range(2):
                    oT = ps[:, 5:7, :].rearrange("p b (q r t) -> p (b q) r t", q=2, r=2)[:, :, r, :]
                    g_dve.done(dve.scalar_tensor_tensor(
                        out=tiles4(scr[1 + r]), in0=oT, scalar=vcol("gla", r),
                        in1=by_parity(za, r)[:, :, i * P:(i + 1) * P], op0=ALU.mult, op1=ALU.mult), f"t{r}")
                for r in range(2):
                    g_act.wait(dve, f"hi{r}", i)
                    g_dve.done(dve.tensor_tensor(by_parity(oa_lo, r)[:, :, i * P:(i + 1) * P], tiles4(scr[1 + r]),
                                                 by_parity(oa_hi, r)[:, :, i * P:(i + 1) * P].bitcast(F32),
                                                 ALU.subtract), f"lo{r}")
            g_dve.wait(dve, "lo1", 3)
            cv_pad.done(dve.memset(scr[1][:, 0:2], 0.0), "pad")

            def conv(st, j, i):
                u, t, y = scr[1], scr[2], scr[4]
                if j == 1:
                    dve.wait_ge(s_mm[1], st.use[1] + i + 1)
                    dve.wait_ge(s_ev[0], st.use[0] + i + 1)
                    dve.tensor_tensor(u[:, 2:S + 2], scr[0][:, 0:S], ps[:, 1, :], ALU.mult).then_inc(s_ev[1], 1)
                    dve.wait_ge(s_ev[1], st.use[1] + i + 1)
                    cv_pad.wait(dve, "pad")
                    cv_dve.done(dve.tensor_scalar(t[:, 0:S], u[:, 0:S], vec[:, ds1(col["conv"], i)], None, ALU.mult), "c0")
                    for n in (1, 2):
                        cv_dve.wait(dve, f"c{n - 1}", i)
                        cv_dve.done(dve.scalar_tensor_tensor(
                            out=t[:, 0:S], in0=u[:, n:S + n], scalar=vec[:, ds1(col["conv"] + 8 * n, i)],
                            in1=t[:, 0:S], op0=ALU.mult, op1=ALU.add), f"c{n}")
                elif j == 2:
                    dve.wait_ge(s_mm[2], st.use[2] + i + 1)
                    cv_dve.wait(dve, "c2", i)
                    dve.tensor_tensor(t[:, 0:S], t[:, 0:S], ps[:, 2, :], ALU.mult).then_inc(s_ev[2], 1)
                elif j == 3:
                    dve.wait_ge(s_ev[3], st.use[3] + i + 1)
                    dve.wait_ge(s_ev[2], st.use[2] + i + 1)
                    cv_dve.done(dve.tensor_tensor(y[:, 0:S], t[:, 0:S], scr[3][:, 0:S], ALU.mult), "y")
                    cv_act.wait(dve, "hi", i)
                    cv_dve.done(dve.tensor_tensor(yc_lo[:, i, :], y[:, 0:S], yc_hi[:, i, :].bitcast(F32),
                                                  ALU.subtract), "lo")
                    cv_dve.wait(dve, "lo", i)

            run("conv", conv)

            def merge(which):
                def evac(st, j, i):
                    if j < 2:
                        return
                    dve.wait_ge(s_mm[j], st.use[j] + i + 1)
                    dve.wait_ge(s_ev[j - 2], st.use[j - 2] + i + 1)
                    dve.tensor_tensor(scr[j][:, 0:S], scr[j - 2][:, 0:S], ps[:, j, :], ALU.mult).then_inc(s_ev[j], 1)
                    if j == 3:
                        dve.wait_ge(s_ev[2], st.use[2] + i + 1)
                        dve.wait_ge(s_ev[3], st.use[3] + i + 1)
                        mg_dve[which].done(dve.tensor_tensor(scr[3][:, 0:S], scr[2][:, 0:S], scr[3][:, 0:S], ALU.add), "m")
                        mg_act[which].wait(dve, "hi", i)
                        mg_dve[which].done(dve.tensor_tensor(m_lo[:, i, :], scr[3][:, 0:S], m_hi[:, i, :].bitcast(F32),
                                                             ALU.subtract), "lo")
                        mg_dve[which].wait(dve, "lo", i)
                return evac

            def residual(which):
                def evac(st, j, i):
                    dve.wait_ge(s_mm[j], st.use[j] + i + 1)
                    dve.tensor_tensor(xT[:, 4 * i + j, :], xT[:, 4 * i + j, :], ps[:, j, :], ALU.add).then_inc(s_ev[j], 1)
                return evac

            run("merge", merge(1))
            run("out", residual(1))
            for k in range(2):
                p_act.wait(dve, f"hi{k}")
                p_dve.done(dve.tensor_tensor(pT_lo[:, k, :], ps[:, 5 + k, :], pT_hi[:, k, :].bitcast(F32), ALU.subtract), f"lo{k}")
            norm("ple")

            def ple(st, j, i):
                if j % 2:
                    dve.wait_ge(s_mm[j], st.use[j] + i + 1)
                    dve.wait_ge(s_ev[j - 1], st.use[j - 1] + i + 1)
                    dve.tensor_tensor(scr[j][:, 0:S], scr[j - 1][:, 0:S], ps[:, j, :], ALU.mult).then_inc(s_ev[j], 1)
                    dve.wait_ge(s_ev[j], st.use[j] + i + 1)
                    xk = xT[:, 2 * i + j // 2, :]
                    pl_dve.done(dve.tensor_tensor(xk, xk, scr[j][:, 0:S], ALU.add), "xa" if j == 1 else "xb")
                    pl_dve.wait(dve, "xa" if j == 1 else "xb", i)

            run("ple", ple)
            norm("final")
            norm("mix2")
            n_dve["mix2"].wait(dve, "lo7")
            for n in range(2):
                mq_pad.done(dve.memset(scr[4 * n][:, 0:2], 0.0), f"before{n}")
                mq_pad.done(dve.memset(scr[4 * n][:, S + 2:S + 4], 0.0), f"after{n}")

            mq_pad.done(dve.memset(m_tok[:, :, :, MD:MD + 1], 1.0), "col")

            def mqk(st, j, i):
                n = 4 * i + j
                t = scr[1 + n % 2]
                dve.wait_ge(s_ev[j], st.use[j] + i + 1)
                if n == 0:
                    mq_pad.wait(dve, "after1")
                if n >= 2:
                    mq_act.wait(dve, "silu", n - 2)
                mq_dve.done(dve.tensor_scalar(t[:, 0:S], scr[n % 2 * 4][:, 0:S], vcol("conv2", n), None, ALU.mult), "c0")
                for m in range(1, 5):
                    mq_dve.wait(dve, f"c{m - 1}", n)
                    mq_dve.done(dve.scalar_tensor_tensor(
                        out=t[:, 0:S], in0=scr[n % 2 * 4][:, m:S + m], scalar=vcol("conv2", 8 * m + n),
                        in1=t[:, 0:S], op0=ALU.mult, op1=ALU.add), f"c{m}")

            run("mqk", mqk)
            for name in ("mv", "mo", "mg"):
                run(name, nothing)

            def mul(out, a, b):
                return dve.tensor_tensor(out, a, b, ALU.mult)

            def link(steps, ins, name):
                steps.done(ins, name)
                steps.wait(dve, name)

            def way(t, d):
                return t[0:32] if d == 0 else t[32:64, ::-1]

            def gate_logs():
                dve.wait_ge(s_ev[0], by["mg"].use[0] + 1)
                link(r_dve, dve.tensor_copy(rowf[:, :], gates[64:128, :]), "f")
                r_act.wait(dve, "ln")
                link(r_dve, dve.scalar_tensor_tensor(out=rowf[:, :], in0=rowf[:, :], scalar=0.0, in1=rowt[:, :],
                                                     op0=ALU.min, op1=ALU.subtract), "lf")
                r_pool.wait(dve, "n3")
                for d, name in ((0, "bf"), (1, "bb")):
                    link(r_dve, dve.tensor_tensor_scan(way(rowb, d), way(rstm, d), way(rowf, d), 0.0, ALU.mult, ALU.add), name)
                link(r_dve, dve.tensor_tensor(rows[:, 0, :], gates[0:64, :], rowb[:, :], ALU.subtract), "c")
                for d, name in ((0, "mf"), (1, "mb")):
                    c_way = rows[0:32, 0, :] if d == 0 else rows[32:64, 0, ::-1]
                    link(r_dve, dve.tensor_tensor_scan(way(rowm, d), way(negm, d), c_way, -BIG, ALU.add, ALU.max), name)

            def gate_rows():
                g_, cl, am, mo, mi, sp_, gm = (msm[0:64, 4 * n:4 * n + 4] for n in range(7))
                for src, dst, tag in ((rowb, 0, "g"), (rowm, 4, "l")):
                    link(r_dve, dve.tensor_copy(msm[0:32, dst:dst + 4], src[0:32, P - 1:S:P]), tag + "0")
                    link(r_dve, dve.tensor_copy(msm[32:64, dst:dst + 4], src[32:64, 0:S:P]), tag + "1")
                link(r_dve, dve.tensor_tensor(am, g_, cl, ALU.add), "am")
                link(r_dve, dve.tensor_tensor_scan(msm[0:32, 12:16], msm[0:32, 0:4], msm[0:32, 8:12], 0.0, ALU.add, ALU.max), "mo0")
                link(r_dve, dve.tensor_tensor_scan(msm[32:64, 12:16][:, ::-1], msm[32:64, 0:4][:, ::-1],
                                                   msm[32:64, 8:12][:, ::-1], 0.0, ALU.add, ALU.max), "mo1")
                link(r_dve, dve.memset(mi, 0.0), "mi")
                link(r_dve, dve.tensor_copy(msm[0:32, 17:20], msm[0:32, 12:15]), "mi0")
                link(r_dve, dve.tensor_copy(msm[32:64, 16:19], msm[32:64, 13:16]), "mi1")
                link(r_dve, dve.tensor_tensor(sp_, g_, mi, ALU.add), "s0")
                link(r_dve, dve.tensor_tensor(sp_, sp_, mo, ALU.subtract), "s1")
                link(r_dve, dve.tensor_tensor(gm, g_, mo, ALU.subtract), "gm")

                def chunked(t):
                    return t.rearrange("p (c t) -> p c t", t=P)

                def per_chunk(t):
                    return t.unsqueeze(2).to_broadcast([64, TT, P])

                link(r_dve, dve.tensor_tensor(chunked(rowm[:, :]), chunked(rowm[:, :]), per_chunk(mi), ALU.max), "mt")
                link(r_dve, dve.tensor_tensor(chunked(rows[:, 1, :]), per_chunk(mi), chunked(rowm[:, :]), ALU.subtract), "a1")
                link(r_dve, dve.tensor_tensor(rows[:, 2, :], rowb[:, :], rowm[:, :], ALU.add), "a2")
                link(r_dve, dve.tensor_tensor(chunked(rows[:, 3, :]), chunked(rows[:, 0, :]), per_chunk(gm), ALU.add), "a3")
                link(r_dve, dve.tensor_scalar(rowt[:, :], rowm[:, :], -1.0, None, ALU.mult), "nm")
                for d in range(2):
                    link(r_dve, dve.tensor_copy(selr[:, 4 * d:4 * d + 4, :],
                                                ident[0:64, 32 * d:32 * d + 4].unsqueeze(2).to_broadcast([64, 4, P])), f"sel{d}")
                r_act.wait(dve, "sp")
                link(r_dve, mul(spd[:, :, :], ident[0:64, 0:64].unsqueeze(2).to_broadcast([64, 64, TT]),
                                sp_.unsqueeze(1).to_broadcast([64, 64, TT])), "spd")

            run("dq", nothing, then={0: gate_logs})
            run("dk", nothing, then={0: gate_rows})
            run("dv", nothing, look=False)
            rings_rest(dve)
            r_act.wait(dve, "spb")
            r_pool.wait(dve, "mb")
            mq_pad.wait(dve, "col")

            def col4(n, q, width):
                r = mrow(*WAYS[n])
                return cols[:, :, q, r:r + 1].to_broadcast([P, TT, width])

            def weighted_values(n):
                if n:
                    l_pe.wait(dve, f"kv{n - 1}")
                link(l_dve, mul(wv[:, :, :], m_tok[:, :, WAYS[n][0], :], col4(n, 3, MD + 1)), f"wv{n}")

            def states(n):
                h, d = WAYS[n]
                r = mrow(h, d)
                l_pe.wait(dve, f"nm{n}")
                if n:
                    l_act.wait(dve, f"pt{n - 1}")
                link(l_dve, dve.tensor_tensor(arg[:, :, :], tiles4(ps[:, 4, :]), col4(n, 0, P), ALU.add), f"arg{n}")
                link(l_dve, dve.tensor_tensor(arg[:, :, :], arg[:, :, :],
                                              m01[:, d, :].unsqueeze(1).to_broadcast([P, TT, P]), ALU.min), f"msk{n}")
                order = state_chunks(d)
                if n >= 2:
                    l_pe.wait(dve, f"inter{n - 2}")
                l_dve.done(dve.memset(cst[:, n % 2, order[0], :], 0.0), f"z{n}")
                l_pe.wait(dve, f"kv{n}")
                for m in range(3):
                    kv = ps[:, 3, m * (MD + 1):(m + 1) * (MD + 1)]
                    if m == 0:
                        link(l_dve, dve.tensor_copy(cst[:, n % 2, order[1], :], kv), f"cs0_{n}")
                    else:
                        link(l_dve, dve.scalar_tensor_tensor(
                            out=cst[:, n % 2, order[m + 1], :], in0=cst[:, n % 2, order[m], :],
                            scalar=spb[:, r, order[m]:order[m] + 1], in1=kv, op0=ALU.mult, op1=ALU.add), f"cs{m}_{n}")

            def outputs(n):
                h, d = WAYS[n]
                r = mrow(h, d)
                l_pe.wait(dve, f"inter{n}")
                link(l_dve, mul(paired(nj), pairs(0), paired(cols[:, :, 1, r:r + 1]).to_broadcast([P, 2, 2, MD + 1])), f"tmp{n}")
                l_act.wait(dve, f"ni{n}")
                link(l_dve, dve.tensor_tensor(nj[:, :, :], nj[:, :, :], ni[:, :, :], ALU.add), f"num{n}")
                dn = msm[:, 64:68]
                link(l_dve, dve.scalar_tensor_tensor(out=dn, in0=nj[:, :, MD], scalar=-1.0, in1=nj[:, :, MD],
                                                     op0=ALU.mult, op1=ALU.max), f"ab{n}")
                link(l_dve, dve.tensor_tensor(dn, dn, cols[:, :, 2, r], ALU.max), f"den{n}")
                link(l_dve, dve.reciprocal(msm[:, 68:72], dn), f"rd{n}")
                rd = msm[:, 68:72].unsqueeze(2).to_broadcast([P, TT, MD])
                link(l_dve, mul(hsum[:, h, :, :] if d == 0 else nj[:, :, 0:MD], nj[:, :, 0:MD], rd), f"h{n}")
                if d:
                    link(l_dve, dve.tensor_tensor(hsum[:, h, :, :], hsum[:, h, :, :], nj[:, :, 0:MD], ALU.add), f"hs{n}")
                    for c in range(TT):
                        m = 100 + 6 * (h * TT + c)
                        l_dve.done(dve.bn_stats(msm[:, m:m + 6], hsum[:, h, c, :]), f"bn{c}_{n}")

            weighted_values(0)
            for k in range(LTURNS):
                if k < NW:
                    states(k)
                if k + 1 < NW:
                    weighted_values(k + 1)
                if 0 <= k - 1 < NW:
                    n = k - 1
                    l_act.wait(dve, f"pt{n}")
                    if n:
                        l_pe.wait(dve, f"intra{n - 1}")
                    l_dve.done(mul(wt[:, :, :], pt[:, :, :], tiles4(ps[:, kq_bank(n), :])), f"w{n}")
                if k >= 2:
                    outputs(k - 2)
            d_pool.wait(dve, "iota")
            link(d_dve, dve.scalar_tensor_tensor(out=alibi[:, :], in0=alibi[:, :], scalar=-1.0, in1=alibi[:, :],
                                                 op0=ALU.mult, op1=ALU.max), "abs")
            dve.wait_ge(s_lam, 16)
            for m in range(2):
                link(d_dve, dve.tensor_tensor_reduce(pr[:, 0:DDH], lam_sb[:, 2 * m, :], lam_sb[:, 2 * m + 1, :], 1.0, 0.0,
                                                     ALU.mult, ALU.add, dsm[:, m:m + 1]), f"lam{m}")
            l_dve.wait(dve, "bn3_7")
            for m in range(MH * TT):
                l_dve.done(dve.bn_aggr(msm[:, 200 + 2 * m:202 + 2 * m], msm[:, 100 + 6 * m:106 + 6 * m]), f"ag{m}")
            d_act.wait(dve, "lam1")
            link(d_dve, dve.tensor_tensor(dsm[:, 4:5], dsm[:, 3:4], dsm[:, 2:3], ALU.subtract), "lam2")
            link(d_dve, dve.tensor_scalar(dsm[:, 4:5], dsm[:, 4:5], -LAM_INIT, None, ALU.add), "lam3")
            link(d_dve, dve.tensor_scalar(dsm[:, 8:9], vcol("dnorm"), 1.0 - LAM_INIT, None, ALU.mult), "gain")
            f_act.wait(dve, "root")
            link(l_dve, dve.reciprocal(msm[:, 256:272], msm[:, 240:256]), "rstd")
            def centre(h):
                for c in range(TT):
                    m = h * TT + c
                    f_dve.done(dve.tensor_scalar(hn[:, h % 2, c, :], hsum[:, h, c, :], msm[:, 200 + 2 * m:201 + 2 * m],
                                                 msm[:, 256 + m:257 + m], ALU.subtract, ALU.mult), f"n{c}_{h}")

            centre(0)
            centre(1)
            for h in range(MH):
                f_pe.wait(dve, f"t{h}")
                if h >= 2:
                    f_dve.wait(dve, f"lo{h - 2}")
                f_dve.done(dve.scalar_tensor_tensor(out=scr[1 + h % 2][:, 0:S], in0=ps[:, 4 + h % 2, :], scalar=vcol("mnorm", h),
                                                    in1=moT[:, h, :], op0=ALU.mult, op1=ALU.mult), f"t{h}")
                if h + 2 < MH:
                    centre(h + 2)
                f_act.wait(dve, f"hi{h}")
                f_dve.done(dve.tensor_tensor(hm_lo[:, h, :], scr[1 + h % 2][:, 0:S], hm_hi[:, h, :].bitcast(F32),
                                             ALU.subtract), f"lo{h}")
            f_dve.wait(dve, "lo3")

            for k in range(TURNS):
                if k < ND:
                    n, (h, q) = k, DW[k]
                    if q == 0:
                        d_act.wait(dve, f"al{n}")
                    d_pe.wait(dve, f"s{n}")
                    bias = alih[:, (TT - 1 - q) * P:(TT - 1 - q) * P + S]
                    for i in range(2):
                        d_dve.done(dve.tensor_tensor_reduce(es[:, n % 2, i, :], ps[:, n % 2 * 2 + i, :], bias, DDH ** -0.5, -BIG,
                                                            ALU.add, ALU.max, small(n, i, 1)), f"m{i}_{n}")
                    d_dve.wait(dve, f"m1_{n}")
                    d_dve.done(dve.tensor_scalar(small(n, 2, 2), small(n, 0, 2), -1.0, None, ALU.mult), f"neg{n}")
                if 0 <= k - 1 < ND:
                    n = k - 1
                    d_act.wait(dve, f"e1_{n}")
                    link(d_dve, dve.reciprocal(small(n, 6, 2), small(n, 4, 2)), f"rec{n}")
                    link(d_dve, mul(small(n, 8, 1), small(n, 7, 1), dsm[:, 4:5]), f"rl{n}")
                    link(d_dve, dve.tensor_scalar(pr[:, :], es[:, n % 2, 0, :], small(n, 6, 1), None, ALU.mult), f"p{n}")
                    if n >= 2:
                        d_pe.wait(dve, f"t{n - 2}")
                    link(d_dve, dve.scalar_tensor_tensor(out=aa[:, n % 2, :], in0=es[:, n % 2, 1, :], scalar=small(n, 8, 1),
                                                         in1=pr[:, :], op0=ALU.mult, op1=ALU.add), f"a{n}")
                if k - 2 == ND - 1:
                    for j in range(4):
                        split(by["merge2"], j, 0)
                if ends(k - 2):
                    n = k - 2
                    d_act.wait(dve, f"root{n}")
                    d_dve.done(dve.reciprocal(dsm[:, 48:52], dsm[:, 44:48]), f"rstd{n}")
                if ends(k - 4):
                    n, h = k - 4, DW[k - 4][0]
                    d_act.wait(dve, f"hi{n}")
                    d_dve.done(dve.scalar_tensor_tensor(out=hd_lo[:, h, :], in0=ps[:, 7, :], scalar=dsm[:, 8:9],
                                                        in1=hd_hi[:, h, :].bitcast(F32), op0=ALU.mult,
                                                        op1=ALU.subtract), f"lo{n}")

            run("merge2", merge(2))
            run("out2", residual(2))

            dve.wait_ge(s_rw, 16)
            fg = vec[:, col["ffn"]:col["ffn"] + KD].unsqueeze(2).to_broadcast([P, KD, NE])
            t_dve.done(mul(rwg[:, :, :], rw[:, :, :], fg), "rwg")
            for t in range(TT):
                t_pe.wait(dve, f"x{t}")
                t_dve.done(dve.tensor_copy(x2[:, t, S:D], ps[:, 2 * t + 1, :]), f"x{t}")
            for t in (2, 3):
                t_act.wait(dve, f"x{t}")
                t_dve.wait(dve, f"x{t}")
                t_dve.done(dve.tensor_tensor_reduce(h2[:, t, :], x2[:, t, :], x2[:, t, :], 1.0, 0.0, ALU.mult, ALU.add,
                                                    esm[:, t:t + 1]), f"ss{t}")
            t_act.wait(dve, "root")
            link(t_dve, dve.reciprocal(esm[:, 8:12], esm[:, 4:8]), "rstd")
            t_pe.wait(dve, "logits")

            def per_token(c):
                return esm[:, c:c + 4].unsqueeze(2).to_broadcast([P, TT, NE])

            link(t_dve, mul(lg[:, :, :], ps[:, 0, 0:TT * NE].rearrange("p (t e) -> p t e", e=NE), per_token(8)), "lg")
            link(t_dve, dve.tensor_reduce(esm[:, 12:16], lg[:, :, :], AX, ALU.max), "mx")
            link(t_dve, dve.tensor_tensor(lg[:, :, :], lg[:, :, :], per_token(12), ALU.subtract), "sub")
            t_act.wait(dve, "exp")
            link(t_dve, dve.tensor_reduce(esm[:, 24:28], lg[:, :, :], AX, ALU.add), "sum")
            link(t_dve, dve.reciprocal(esm[:, 28:32], esm[:, 24:28]), "rec")
            link(t_dve, mul(aff[:, :, :], lg[:, :, :], per_token(28)), "aff")
            t_pe.wait(dve, "affT")
            link(t_dve, dve.tensor_copy(aw[:, :], ps[0:NE, 1, :]), "aw")
            for n in range(CAP // 8):
                link(t_dve, dve.max(top8[:, :], aw[:, :]), f"top{n}")
                link(t_dve, dve.match_replace(aw[:, :], top8[:, :], aw[:, :], -1.0), f"rep{n}")
            link(t_dve, dve.memset(awo[:, :], 1.0), "one")
            link(t_dve, dve.tensor_scalar(awm[:, :], aw[:, :], 0.0, None, ALU.is_lt), "mask")
            link(t_dve, dve.tensor_tensor_scan(awc[:, :], awo[:, :], awm[:, :], 0.0, ALU.mult, ALU.add), "scan")
            link(t_dve, mul(awc[:, :], awc[:, :], awm[:, :]), "sel")
            t_pe.wait(dve, "posT")
            link(t_dve, dve.tensor_copy(pos[:, :, :], ps[:, 2, 0:TT * NE].rearrange("p (t e) -> p t e", e=NE)), "pos")
            t_pool.wait(dve, "iota")

            def choose(e):
                slot = pos[:, :, bass.ds(e, 1)].to_broadcast([P, TT, CAP])
                number = iot[:, :].unsqueeze(1).to_broadcast([P, TT, CAP])
                x_dve.done(dve.tensor_tensor(pick[:, :, :], slot, number, ALU.is_equal), "pick")
                x_dve.wait(dve, "pick", e)

            def expert(e, more=True):
                weight = aff[:, :, bass.ds(e, 1)].to_broadcast([P, TT, CAP])
                for r in range(2):
                    e_dve.done(mul(pickg[:, :, r, :], pick[:, :, :], weight), f"pg{r}")
                if more:
                    x_pe.wait(dve, "gather", e)
                    e_dve.wait(dve, "pg1", e)
                    choose(e + 1)
                used(dve, e, 15)
                e_act.wait(dve, "s1", e)
                for q in range(2):
                    e_dve.done(mul(hid[:, q, :], sg[:, q, :], ps[:, 2 + q, :]), f"hid{q}")
                e_pe.wait(dve, "hT", e)
                e_dve.done(dve.tensor_copy(hidT[:, 1, :, :], tiles4(ps[:, 6, :])), "hT1")
                for t, b in enumerate((5, 0, 2, 5)):
                    e_pe.wait(dve, f"o{t}", e)
                    row = x2[:, t, :].rearrange("p (d c) -> p d c", d=2)
                    e_dve.done(dve.tensor_tensor(row, row, ps[:, b:b + 2, :], ALU.add), f"o{t}")

            choose(0)
            with dve.Fori(0, NE - 1) as e:
                expert(e)
            expert(NE - 1, more=False)
            z_act.wait(dve, "root")
            link(z_dve, dve.reciprocal(esm[:, 32:36], esm[:, 20:24]), "rstd")
            dve.wait_ge(s_g, 32)
            for t in range(TT):
                if t >= 2:
                    dve.wait_ge(s_store[t % 2], 16)
                z_dve.done(dve.scalar_tensor_tensor(out=fin[:, t % 2, :], in0=x2[:, t, :], scalar=esm[:, 32 + t:33 + t],
                                                    in1=gbc[:, :], op0=ALU.mult, op1=ALU.mult), f"y{t}")

        @block.tensor
        def _(pe):
            def group(st, j, i, rhs_hi, rhs_lo, ready=None):
                pe.wait_ge(s_lo[j], st.use[j] + i + 1)
                if not (isinstance(i, int) and st.use[j] + i == 0):
                    pe.wait_ge(s_ev[j], st.use[j] + i)
                nk, w = span(st, j, i), width(st)
                dst = ps[0:w, j, :]
                for k in range(nk):
                    if ready is not None:
                        ready(k)
                    for n, (lt, rt) in enumerate(((w_hi, rhs_hi), (w_hi, rhs_lo), (w_lo, rhs_hi))):
                        mm = pe.matmul(dst, lt[:, j, k, 0:w], rt[:, k, :], start=k == 0 and n == 0,
                                       stop=k == nk - 1 and n == 2)
                mm.then_inc(s_mm[j], 1)

            def group_tok(st, i):
                for j in range(4):
                    pe.wait_ge(s_lo[j], st.use[j] + i + 1)
                for t in range(TT):
                    pe.wait_ge(s_ev[t], st.use[t] + i)
                    for k in range(KD):
                        for n, (lt, rt) in enumerate(((h_hi, w_hi), (h_hi, w_lo), (h_lo, w_hi))):
                            mm = pe.matmul(ps[:, t, :], lt[:, k, t * P:(t + 1) * P], rt[:, :, k, :],
                                           start=k == 0 and n == 0, stop=k == KD - 1 and n == 2)
                    mm.then_inc(s_mm[t], 1)

            def run(name, rhs=None, ready=None, between=None):
                st = by[name]
                rhs = rhs or [(h_hi, h_lo)] * 4

                def body(i):
                    if st.kind == "tok":
                        group_tok(st, i)
                    else:
                        for j in range(len(st.tiles)):
                            if between is not None and j == 2 and isinstance(i, int) and i == 0:
                                between()
                            group(st, j, i, *rhs[j], ready=ready if j == 0 and isinstance(i, int) and i == 0 else None)
                if st.n <= 2:
                    for i in range(st.n):
                        body(i)
                elif ready is not None or between is not None:
                    body(0)
                    with pe.Fori(1, st.n) as i:
                        body(i)
                else:
                    with pe.Fori(0, st.n) as i:
                        body(i)

            def norm(n):
                for k in range(KD):
                    n_act[n].wait(pe, f"sq{k}")
                    mm = pe.matmul(ps[:, 4, :], ones[:, :], sq[:, k, :], start=k == 0, stop=k == KD - 1)
                n_pe[n].done(mm, "sum")

            set_pool.wait(pe, "ones")
            pe.wait_ge(s_small, 16 * (len(vec_loads) + 4))
            for g in range(2):
                set_pe.done(pe.transpose(ps[:, g, 0:P], vrow[:, g, :], ident[:, :]), f"vec{g}")
            pe.wait_ge(s_x, 16 * TT)
            set_dve.wait(pe, "vec1")
            for k in range(KD):
                for t in range(TT):
                    mm = pe.transpose(ps[:, k, t * P:(t + 1) * P], x_tok[:, t, k * P:(k + 1) * P], ident[:, :])
                set_pe.done(mm, f"x{k}")
            set_dve.wait(pe, "x7")
            set_act.wait(pe, "x6")
            norm("mix")
            run("q", ready=lambda k: n_dve["mix"].wait(pe, f"lo{k}"))
            run("k")
            run("gk")
            pe.wait_ge(s_gw, 16)
            pe.wait_ge(s_ev[0], by["gk"].use[0] + 1)
            for h in range(GH):
                gp_pe.done(pe.matmul(ps[:, 4 + h, :], wgk[:, h * GDK:(h + 1) * GDK], gk_sb[:, :],
                                     start=True, stop=True), f"gk{h}")
            run("v")
            run("za")
            gp_dve.wait(pe, "kd")
            for t in range(TT):
                for h in range(GH):
                    mm = pe.transpose(ps[:, 4 + t, h * P:(h + 1) * P], kdT[:, h, t * P:(t + 1) * P], ident[:, :])
                gp_pe.done(mm, f"kd{t}")
            gp_act.wait(pe, "kd3")
            gp_dve.wait(pe, "mask")
            for i in range(TT):
                tok = slice(i * P, (i + 1) * P)
                if i:
                    g_dve.wait(pe, "st13", i - 1)
                for h in range(GH):
                    mm = pe.matmul(ps[:, 4, h * P:(h + 1) * P], kT[:, h, tok], qT[:, h, tok], start=h == 0,
                                   stop=True, skip_group_check=True)
                g_pe.done(mm, "a")
                g_dve.wait(pe, "at", i)
                if i:
                    g_dve.wait(pe, "t1", i - 1)
                for h in range(GH):
                    pe.matmul(ps[:, 5 + h // 2, h % 2 * GDV:(h % 2 + 1) * GDV], scoresT[:, h, :],
                              v_tok[:, i, h * GDV:(h + 1) * GDV], start=h % 2 == 0, stop=False, skip_group_check=True)
                for c in range(2):
                    half = slice(c * GCH, (c + 1) * GCH)
                    tokc = slice(i * P + c * GCH, i * P + (c + 1) * GCH)
                    if c:
                        g_dve.wait(pe, "st03", i)
                    for h in range(GH):
                        pe.matmul(ps[half, 5 + h // 2, h % 2 * GDV:(h % 2 + 1) * GDV], qT[:, h, tokc],
                                  state[:, h, :], start=False, stop=c == 1, skip_group_check=True)
                    for h in range(GH):
                        mm = pe.matmul(ps[:, 7 if h < 2 else 4, h % 2 * GDV:(h % 2 + 1) * GDV],
                                       kd_tok[half, i, h * GDK:(h + 1) * GDK], v_tok[half, i, h * GDV:(h + 1) * GDV],
                                       start=h % 2 == 0, stop=True, skip_group_check=True)
                        if h % 2:
                            g_pe.done(mm, f"kv{'AB'[h // 2]}{c}")
                g_act.wait(pe, "on3", i)
                for n in range(KD):
                    mm = pe.transpose(ps[:, 5 + n // 4, n % 4 * P:(n % 4 + 1) * P], o_norm[:, n * P:(n + 1) * P], ident[:, :])
                g_pe.done(mm, "oT")
            run("conv")
            g_dve.wait(pe, "lo1", 3)
            cv_dve.wait(pe, "lo", 7)
            run("merge", [(h_hi, h_lo), (h_hi, h_lo), (oa_hi, oa_lo), (yc_hi, yc_lo)])
            mg_dve[1].wait(pe, "lo", 7)
            run("out", [(m_hi, m_lo)] * 4)
            pe.wait_ge(s_p, 16)
            for k in range(2):
                for t in range(TT):
                    mm = pe.transpose(ps[:, 5 + k, t * P:(t + 1) * P], p_tok[:, t, k * P:(k + 1) * P], ident[:, :])
                p_pe.done(mm, f"p{k}")
            norm("ple")
            p_dve.wait(pe, "lo1")
            run("ple", [(h_hi, h_lo), (pT_hi, pT_lo), (h_hi, h_lo), (pT_hi, pT_lo)],
                ready=lambda k: n_dve["ple"].wait(pe, f"lo{k}"))
            norm("final")
            norm("mix2")
            run("mqk", ready=lambda k: n_dve["mix2"].wait(pe, f"lo{k}"))
            for name in ("mv", "mo", "mg", "dq", "dk", "dv"):
                run(name)
            kt_act.wait(pe, "scaled")
            for c in range(TT):
                pe.wait_ge(s_ev[c], by["dv"].use[c] + 1)
                for h in range(MH):
                    mm = pe.transpose(ps[:, c, h * P:(h + 1) * P], mqkT[:, MH + h, c * P:(c + 1) * P], ident[:, :])
                kt_pe.done(mm, f"kt{c}")
            r_act.wait(pe, "e3")
            for c in range(TT):
                for q in range(4):
                    k = c % 2 * 256 + q * 64
                    mm = pe.transpose(ps[:, 4 + c // 2, k:k + 64], rows[:, q, c * P:(c + 1) * P], ident[0:64, 0:64])
            r_pe.done(mm, "cols")
            r_dve.wait(pe, "spd")
            r_pe.done(pe.matmul(ps[:, 6, 0:256], ones[0:64, :], spd[:, :, :], start=True, stop=True), "spb")
            kt_act.wait(pe, "kt3")
            r_act.wait(pe, "spb")
            def keys(n):
                h, d = WAYS[n]
                if d == 0:
                    if n >= 4:
                        l_dve.wait(pe, f"w{n - 3}")
                    for c in range(TT):
                        tok = slice(c * P, (c + 1) * P)
                        mm = pe.matmul(ps[:, kq_bank(n), tok], mqkT[:, MH + h, tok], mqkT[:, h, tok], start=True, stop=True)
                    l_pe.done(mm, f"kq{n}")
                if n:
                    l_dve.wait(pe, f"arg{n - 1}")
                l_pe.done(pe.matmul(ps[:, 4, :], selr[:, 4 * d + h, :], rowt[:, :], start=True, stop=True), f"nm{n}")
                l_dve.wait(pe, f"wv{n}")
                for m, c in enumerate(state_chunks(d)[:3]):
                    mm = pe.matmul(ps[:, 3, m * (MD + 1):(m + 1) * (MD + 1)], ktok[:, c, h * MD:(h + 1) * MD],
                                   wv[:, c, :], start=True, stop=True)
                l_pe.done(mm, f"kv{n}")

            keys(0)
            for k in range(LTURNS):
                if k + 1 < NW:
                    keys(k + 1)
                if 0 <= k - 1 < NW:
                    n, (h, d) = k - 1, WAYS[k - 1]
                    l_dve.wait(pe, f"w{n}")
                    if n:
                        l_act.wait(pe, f"ni{n - 1}")
                    for c in range(TT):
                        mm = pe.matmul(ps[:, 6 + c // 2, c % 2 * (MD + 1):(c % 2 + 1) * (MD + 1)], wt[:, c, :],
                                       m_tok[:, c, h, :], start=True, stop=True)
                    l_pe.done(mm, f"intra{n}")
                    if n:
                        l_dve.wait(pe, f"tmp{n - 1}")
                    for c in range(TT):
                        mm = pe.matmul(ps[:, c // 2, c % 2 * (MD + 1):(c % 2 + 1) * (MD + 1)], mqkT[:, h, c * P:(c + 1) * P],
                                       cst[:, n % 2, c, :], start=True, stop=True)
                    l_pe.done(mm, f"inter{n}")
            def scores(n):
                h, q = DW[n]
                if n >= 2:
                    d_dve.wait(pe, f"m1_{n - 2}")
                for i in range(2):
                    half = slice(i * DDH, (i + 1) * DDH)
                    mm = pe.matmul(ps[:, n % 2 * 2 + i, :], dqT[half, h, q * P:(q + 1) * P], dkT[half, h, :],
                                   start=True, stop=True)
                d_pe.done(mm, f"s{n}")

            def turned(n):
                d_act.wait(pe, f"o3_{n}")
                if n >= TT:
                    d_dve.wait(pe, f"lo{n - TT}")
                for c in range(TT):
                    mm = pe.transpose(ps[:, 7, c * P:(c + 1) * P], od[:, c, :], ident[:, :])
                d_pe.done(mm, f"oT{n}")

            l_dve.wait(pe, "tmp7")
            scores(0)
            scores(1)
            l_dve.wait(pe, "arg7")
            for h in range(MH):
                f_dve.wait(pe, f"n3_{h}")
                if h >= 2:
                    f_dve.wait(pe, f"t{h - 2}")
                for c in range(TT):
                    mm = pe.transpose(ps[:, 4 + h % 2, c * P:(c + 1) * P], hn[:, h % 2, c, :], ident[:, :])
                f_pe.done(mm, f"t{h}")
            f_dve.wait(pe, "t3")

            for k in range(TURNS):
                if 0 <= k - 1 < ND:
                    n = k - 1
                    d_dve.wait(pe, f"a{n}")
                    if n:
                        d_act.wait(pe, f"t{n - 1}")
                    for c in range(TT):
                        mm = pe.transpose(ps[:, 4, c * P:(c + 1) * P], aa[:, n % 2, c * P:(c + 1) * P], ident[:, :])
                    d_pe.done(mm, f"t{n}")
                if k + 2 < ND:
                    scores(k + 2)
                if 0 <= k - 1 < ND:
                    n, (h, q) = k - 1, DW[k - 1]
                    d_act.wait(pe, f"t{n}")
                    if q == 0 and h >= 2:
                        d_act.wait(pe, f"o3_{n - TT - 1}")
                    for c in range(TT):
                        mm = pe.matmul(ps[:, 5 + h % 2, q * P:(q + 1) * P], aaT[:, n % 2, c, :],
                                       d_tok[:, c, h * DDV:(h + 1) * DDV], start=c == 0, stop=c == TT - 1)
                    d_pe.done(mm, f"o{n}")
                if ends(k - 3) and k - 3 < ND - 1:
                    turned(k - 3)

            def last_head():
                turned(ND - 1)
                d_dve.wait(pe, f"lo{ND - 1}")

            run("merge2", [(h_hi, h_lo), (h_hi, h_lo), (hm_hi, hm_lo), (hd_hi, hd_lo)], between=last_head)
            mg_dve[2].wait(pe, "lo", 7)
            run("out2", [(m_hi, m_lo)] * 4)

            for b in range(4):
                pe.wait_ge(s_ev[b], by["out2"].use[b] + 2)
            for t in range(TT):
                for k in range(KD):
                    mm = pe.transpose(ps[:, 2 * t + k // 4, k % 4 * P:(k % 4 + 1) * P], xT[:, k, t * P:(t + 1) * P], ident[:, :])
                t_pe.done(mm, f"x{t}")
            t_dve.wait(pe, "x0")
            t_act.wait(pe, "x0")
            for t in range(TT):
                for k in range(KD):
                    mm = pe.matmul(ps[:, 0, t * NE:(t + 1) * NE], xT[:, k, t * P:(t + 1) * P], rwg[:, k, :],
                                   start=k == 0, stop=k == KD - 1)
            t_pe.done(mm, "logits")
            t_dve.wait(pe, "aff")
            for t in range(TT):
                mm = pe.transpose(ps[0:NE, 1, t * P:(t + 1) * P], aff[:, t, :], ident[:, :])
            t_pe.done(mm, "affT")
            t_dve.wait(pe, "sel")
            for t in range(TT):
                mm = pe.transpose(ps[:, 2, t * NE:(t + 1) * NE], awc[:, t * P:(t + 1) * P], ident[0:NE, 0:NE])
            t_pe.done(mm, "posT")
            t_dve.wait(pe, "pos")
            t_pool.wait(pe, "h3")

            def gather(e):
                x_dve.wait(pe, "pick", e)
                for k in range(KD):
                    for t in range(TT):
                        mm = pe.matmul(ps[:, 7, k * CAP:(k + 1) * CAP], h2[:, t, k * P:(k + 1) * P], pick[:, t, :],
                                       start=t == 0, stop=t == TT - 1)
                x_pe.done(mm, "gather")

            def chunk(e, n):
                pe.wait_ge(s_ring[n % RING], (e * 2 + (n // RING + 1)) * 16)

            def expert(e, more=True):
                x_act.wait(pe, "xe", e)
                for m in range(2):
                    for k in range(KD):
                        n = m * KD + k
                        chunk(e, n)
                        for q in range(2):
                            for half in range(2):
                                mm = pe.matmul(ps[half * CAP:(half + 1) * CAP, 2 * m + q, :], xe[:, k, :],
                                               ring[:, n % RING, (2 * q + half) * S:(2 * q + half + 1) * S],
                                               start=k == 0, stop=k == KD - 1, skip_group_check=True)
                        mm.then_inc(s_free[n % RING], 1)
                if more:
                    gather(e + 1)
                e_dve.wait(pe, "hid1", e)
                for q in range(2):
                    for c in range(4):
                        mm = pe.transpose(ps[:, 5 + q, c * P:(c + 1) * P], hid[:, q, c * P:(c + 1) * P], ident[:, :])
                e_pe.done(mm, "hT")
                e_act.wait(pe, "hT0", e)
                e_dve.wait(pe, "hT1", e)
                for i in range(8):
                    n = 16 + i
                    chunk(e, n)
                    for j in range(2):
                        q, half, c = i // 4, i // 2 % 2, 2 * i % 4 + j
                        for d in range(2):
                            mm = pe.matmul(ps[d * CAP:(d + 1) * CAP, 4, :], hidT[:, q, c, half * CAP:(half + 1) * CAP],
                                           ring[:, n % RING, j * D + d * S:j * D + (d + 1) * S],
                                           start=i == 0 and j == 0, stop=i == 7 and j == 1, skip_group_check=True)
                    mm.then_inc(s_free[n % RING], 1)
                if more:
                    x_act.wait(pe, "xe", e + 1)
                e_dve.wait(pe, "pg1", e)
                for t in range(TT):
                    mm = pe.transpose(ps[:, 7, t * P:(t + 1) * P], pickg[:, t, :, :], ident[:, :])
                e_pe.done(mm, "place")
                e_act.wait(pe, "place", e)
                for t, b in enumerate((5, 0, 2, 5)):
                    if t == 3:
                        e_dve.wait(pe, "o0", e)
                    for d in range(2):
                        half = slice(d * CAP, (d + 1) * CAP)
                        mm = pe.matmul(ps[:, b + d, :], place[half, t * P:(t + 1) * P], ye[half, :], start=True, stop=True)
                    e_pe.done(mm, f"o{t}")
                e_dve.wait(pe, "o2", e)

            gather(0)
            with pe.Fori(0, NE - 1) as e:
                expert(e)
            expert(NE - 1, more=False)


_INS = ["x", "p", "norm_mix_g", "w_in", "b_merge", "w_gk2", "b_gk", "gla_norm_g", "conv_w",
        "w_branch_a", "w_branch_c", "w_out", "norm_ple_g", "w_ple_gate", "w_ple_proj", "norm_final_g",
        "norm_mix_g_2", "w_in_2", "b_mgate_2", "conv_w_2", "conv_b_2", "mlstm_norm_g_2", "diff_lam_2",
        "diff_norm_g_2", "w_up_a_2", "w_up_b_2", "w_out_2", "norm_ffn_g_2", "w_router_2", "w_gate_e_2",
        "w_up_e_2", "w_down_e_2", "norm_f_g_2"]


def kernel(**inputs):
    import numpy as np
    import concourse.bacc as bacc
    from concourse.bass_utils import run_bass_kernel_spmd

    nc = bacc.Bacc("TRN2", target_bir_lowering=False, num_devices=1)
    arrays, args = {}, {}
    for name in _INS:
        array = np.ascontiguousarray(inputs[name])
        arrays[f"in_{name}"] = array
        args[name] = nc.dram_tensor(f"in_{name}", array.shape, mybir.dt.from_np(array.dtype), kind="ExternalInput").ap()
    args["out"] = nc.dram_tensor("out_y", (1, S, D), F32, kind="ExternalOutput").ap()
    kernel_program(nc, **args)
    result = run_bass_kernel_spmd(nc, [arrays], core_ids=[0])
    return result.results[0]["out_y"]
```
